# Optimizing a Trainium2 kernel written in Bass

```python
import math
import jax
import jax.numpy as jnp
from jax import lax
import numpy as np

D_MODEL = 1024
BATCH = 1
SEQ = 512
DEPTH = 1

NORM_EPS = 1e-6
DA_HEADS = 8
DA_HEAD_DIM = 64
DA_QK_DIM = DA_HEADS * 2 * DA_HEAD_DIM
DA_V_DIM = DA_HEADS * 2 * DA_HEAD_DIM
ROPE_THETA = 10000.0
Q_BLOCK = 128
GD_HEADS = 8
GD_HEAD_K = 128
GD_HEAD_V = 128
GD_QK_DIM = GD_HEADS * GD_HEAD_K
GD_V_DIM = GD_HEADS * GD_HEAD_V
CONV_WIDTH = 4
CHUNK = 64
IN_SPLITS = (DA_QK_DIM, DA_QK_DIM, DA_V_DIM, GD_QK_DIM, GD_QK_DIM, GD_V_DIM, GD_V_DIM, GD_HEADS, GD_HEADS, D_MODEL, D_MODEL)
IN_DIM = 2 * DA_QK_DIM + DA_V_DIM + 2 * GD_QK_DIM + 2 * GD_V_DIM + 2 * GD_HEADS + 2 * D_MODEL
N_EXPERTS = 32
TOP_K = 4
D_EXPERT = 1024
SWIGLU_ALPHA = 1.702
SWIGLU_LIMIT = 7.0
EXPERT_BLOCK = 128

kernel_name = 'hybrid_diffattn_gdn_moe_block'

def rms_norm(x, g):
    xf = x.astype(jnp.float32)
    y = xf * lax.rsqrt(jnp.mean(xf * xf, axis=-1, keepdims=True) + NORM_EPS)
    return y * g.astype(jnp.float32)

def l2_normalize(t):
    tf = t.astype(jnp.float32)
    return tf * lax.rsqrt(jnp.sum(tf * tf, axis=-1, keepdims=True) + NORM_EPS)

def rope_cos_sin(seq_len, dim):
    inv_freq = 1.0 / (ROPE_THETA ** (jnp.arange(0, dim, 2, dtype=jnp.float32) / dim))
    ang = jnp.arange(seq_len, dtype=jnp.float32)[:, None] * inv_freq[None, :]
    ang = jnp.concatenate([ang, ang], axis=-1)
    return jnp.cos(ang), jnp.sin(ang)

def apply_rope(t, cos, sin):
    tf = t.astype(jnp.float32)
    half = tf.shape[-1] // 2
    rot = jnp.concatenate([-tf[..., half:], tf[..., :half]], axis=-1)
    c = cos[None, :, None, None, :]
    s = sin[None, :, None, None, :]
    return (tf * c + rot * s).astype(t.dtype)

def differential_attention(q, k, v, lam):
    b, s, h, _, d = q.shape
    n_blocks = s // Q_BLOCK
    scale = 1.0 / math.sqrt(d)
    q_blocks = jnp.moveaxis(q.reshape(b, n_blocks, Q_BLOCK, h, 2, d), 1, 0)
    vf = v.astype(jnp.float32)
    key_pos = jnp.arange(s)

    def one_block(args):
        q_blk, blk = args
        scores = jnp.einsum('bqhcd,bkhcd->bhcqk', q_blk, k).astype(jnp.float32) * scale
        q_pos = blk * Q_BLOCK + jnp.arange(Q_BLOCK)
        causal = key_pos[None, :] <= q_pos[:, None]
        probs = jax.nn.softmax(jnp.where(causal, scores, -jnp.inf), axis=-1)
        weights = probs[:, :, 0] - lam * probs[:, :, 1]
        return jnp.einsum('bhqk,bkhe->bqhe', weights, vf)

    out = lax.map(one_block, (q_blocks, jnp.arange(n_blocks)))
    return jnp.moveaxis(out, 0, 1).reshape(b, s, h, 2 * d)

def causal_depthwise_conv(x, w):
    c = x.shape[-1]
    return lax.conv_general_dilated(x, w[:, None, :].astype(x.dtype), window_strides=(1,), padding=[(CONV_WIDTH - 1, 0)], dimension_numbers=('NWC', 'WIO', 'NWC'), feature_group_count=c)

def gated_delta_rule_chunked(q, k, v, g, beta):
    b, s, h, dk = q.shape
    dv = v.shape[-1]
    n = s // CHUNK

    def chunks(t):
        return jnp.moveaxis(t.reshape(b, n, CHUNK, h, -1), 3, 1)

    q, k, v = chunks(q), chunks(k), chunks(v)
    g = jnp.moveaxis(g.reshape(b, n, CHUNK, h), 3, 1)
    beta = jnp.moveaxis(beta.reshape(b, n, CHUNK, h), 3, 1)
    cum_g = jnp.cumsum(g, axis=-1)
    incl = jnp.tril(jnp.ones((CHUNK, CHUNK), dtype=bool))
    strict = jnp.tril(jnp.ones((CHUNK, CHUNK), dtype=bool), -1)
    decay = jnp.exp(jnp.where(incl, cum_g[..., :, None] - cum_g[..., None, :], -jnp.inf))
    k_beta = k * beta[..., None]
    a_kk = jnp.where(strict, jnp.einsum('bhnid,bhnjd->bhnij', k_beta, k) * decay, 0.0)
    eye = jnp.eye(CHUNK, dtype=jnp.float32)
    t_inv = lax.linalg.triangular_solve(eye + a_kk, jnp.broadcast_to(eye, a_kk.shape), left_side=True, lower=True, unit_diagonal=True)
    u = jnp.einsum('bhnij,bhnjv->bhniv', t_inv, v * beta[..., None])
    w = jnp.einsum('bhnij,bhnjd->bhnid', t_inv, k_beta * jnp.exp(cum_g)[..., None])
    a_qk = jnp.einsum('bhnid,bhnjd->bhnij', q, k) * decay
    q_dec = q * jnp.exp(cum_g)[..., None]
    k_dec = k * jnp.exp(cum_g[..., -1:] - cum_g)[..., None]
    g_last = jnp.exp(cum_g[..., -1])

    def step(state, xs):
        u_c, w_c, qd_c, kd_c, aqk_c, gl_c = xs
        v_new = u_c - jnp.einsum('bhck,bhkv->bhcv', w_c, state)
        o_c = jnp.einsum('bhck,bhkv->bhcv', qd_c, state) + jnp.einsum('bhcj,bhjv->bhcv', aqk_c, v_new)
        state = state * gl_c[..., None, None] + jnp.einsum('bhck,bhcv->bhkv', kd_c, v_new)
        return state, o_c

    xs = (jnp.moveaxis(u, 2, 0), jnp.moveaxis(w, 2, 0), jnp.moveaxis(q_dec, 2, 0), jnp.moveaxis(k_dec, 2, 0), jnp.moveaxis(a_qk, 2, 0), jnp.moveaxis(g_last, 2, 0))
    state0 = jnp.zeros((b, h, dk, dv), jnp.float32)
    _, o = lax.scan(step, state0, xs)
    return o.transpose(1, 0, 3, 2, 4).reshape(b, s, h, dv)

def moe_ffn(h, router_w, router_b, w_gate, b_gate, w_up, b_up, w_down, b_down):
    b, s, d = h.shape
    n_tok = b * s
    xt = h.reshape(n_tok, d)
    logits = (xt @ router_w + router_b).astype(jnp.float32)
    top_val, top_idx = lax.top_k(logits, TOP_K)
    gates = jax.nn.softmax(top_val, axis=-1)
    n_assign = n_tok * TOP_K
    flat_e = top_idx.reshape(n_assign).astype(jnp.int32)
    flat_tok = jnp.arange(n_assign, dtype=jnp.int32) // TOP_K
    flat_w = gates.reshape(n_assign)
    e_sorted, order = lax.sort((flat_e, jnp.arange(n_assign, dtype=jnp.int32)), num_keys=1, is_stable=True)
    counts = jnp.zeros((N_EXPERTS,), jnp.int32).at[flat_e].add(1)
    padded = (counts + EXPERT_BLOCK - 1) // EXPERT_BLOCK * EXPERT_BLOCK
    pad_end = jnp.cumsum(padded)
    pad_start = pad_end - padded
    start = jnp.cumsum(counts) - counts
    dest = pad_start[e_sorted] + jnp.arange(n_assign, dtype=jnp.int32) - start[e_sorted]
    n_rows = (n_assign + EXPERT_BLOCK - 1) // EXPERT_BLOCK * EXPERT_BLOCK + N_EXPERTS * EXPERT_BLOCK
    row_tok = jnp.zeros((n_rows,), jnp.int32).at[dest].set(flat_tok[order])
    row_w = jnp.zeros((n_rows,), jnp.float32).at[dest].set(flat_w[order])
    n_blocks = n_rows // EXPERT_BLOCK
    block_e = jnp.minimum(jnp.searchsorted(pad_end, jnp.arange(n_blocks, dtype=jnp.int32) * EXPERT_BLOCK, side='right'), N_EXPERTS - 1)
    x_rows = xt[row_tok].reshape(n_blocks, EXPERT_BLOCK, d)

    def expert_block(args):
        xb, e = args
        gate = jnp.minimum(xb @ w_gate[e] + b_gate[e], SWIGLU_LIMIT)
        up = jnp.clip(xb @ w_up[e] + b_up[e], -SWIGLU_LIMIT, SWIGLU_LIMIT)
        act = (up + 1.0) * gate * jax.nn.sigmoid(SWIGLU_ALPHA * gate)
        return act @ w_down[e] + b_down[e]

    y_rows = lax.map(expert_block, (x_rows, block_e)).reshape(n_rows, d)
    out = jnp.zeros((n_tok, d), jnp.float32).at[row_tok].add(y_rows.astype(jnp.float32) * row_w[:, None])
    return out.reshape(b, s, d).astype(h.dtype)

def hybrid_layer(x, layer_idx, mix_norm_g, w_in, lambda_q1, lambda_k1, lambda_q2, lambda_k2, subln_g, conv_w, a_log, dt_bias, gd_norm_g, w_out, ffn_norm_g, router_w, router_b, w_gate, b_gate, w_up, b_up, w_down, b_down):
    f32 = jnp.float32
    b, s, _ = x.shape
    h = rms_norm(x, mix_norm_g).astype(x.dtype)
    proj = h @ w_in
    split_at = np.cumsum(IN_SPLITS)[:-1].tolist()
    da_q, da_k, da_v, gd_q, gd_k, gd_v, gd_z, gd_b, gd_a, gate_a, gate_b = jnp.split(proj, split_at, axis=-1)

    cos, sin = rope_cos_sin(s, DA_HEAD_DIM)
    q_a = apply_rope(da_q.reshape(b, s, DA_HEADS, 2, DA_HEAD_DIM), cos, sin)
    k_a = apply_rope(da_k.reshape(b, s, DA_HEADS, 2, DA_HEAD_DIM), cos, sin)
    v_a = da_v.reshape(b, s, DA_HEADS, 2 * DA_HEAD_DIM)
    lam_init = 0.8 - 0.6 * math.exp(-0.3 * layer_idx)
    lam = jnp.exp(jnp.sum(lambda_q1.astype(f32) * lambda_k1.astype(f32))) - jnp.exp(jnp.sum(lambda_q2.astype(f32) * lambda_k2.astype(f32))) + lam_init
    o_a = differential_attention(q_a, k_a, v_a, lam)
    y_a = (rms_norm(o_a, subln_g) * (1.0 - lam_init)).reshape(b, s, DA_V_DIM)

    qkv = jax.nn.silu(causal_depthwise_conv(jnp.concatenate([gd_q, gd_k, gd_v], axis=-1), conv_w))
    cq, ck, cv = jnp.split(qkv, [GD_QK_DIM, 2 * GD_QK_DIM], axis=-1)
    q_b = l2_normalize(cq.reshape(b, s, GD_HEADS, GD_HEAD_K)) * (GD_HEAD_K ** -0.5)
    k_b = l2_normalize(ck.reshape(b, s, GD_HEADS, GD_HEAD_K))
    v_b = cv.reshape(b, s, GD_HEADS, GD_HEAD_V).astype(f32)
    beta = jax.nn.sigmoid(gd_b.astype(f32))
    g = -jnp.exp(a_log.astype(f32)) * jax.nn.softplus(gd_a.astype(f32) + dt_bias.astype(f32))
    o_b = gated_delta_rule_chunked(q_b, k_b, v_b, g, beta)
    z = gd_z.reshape(b, s, GD_HEADS, GD_HEAD_V).astype(f32)
    y_b = (rms_norm(o_b, gd_norm_g) * jax.nn.silu(z)).reshape(b, s, GD_V_DIM)

    merged = jax.nn.sigmoid(gate_a.astype(f32)) * y_a + jax.nn.sigmoid(gate_b.astype(f32)) * y_b
    x = x + merged.astype(x.dtype) @ w_out

    h2 = rms_norm(x, ffn_norm_g).astype(x.dtype)
    return x + moe_ffn(h2, router_w, router_b, w_gate, b_gate, w_up, b_up, w_down, b_down)

def setup_inputs(seed: int = 0) -> dict:
    key = jax.random.key(seed)
    ks = jax.random.split(key, 24)
    f32 = jnp.float32
    L = DEPTH

    def normal(k, shape, scale):
        return jax.random.normal(k, shape, f32) * scale

    def gain(k, shape):
        return 1.0 + 0.02 * jax.random.normal(k, shape, f32)

    dt = jnp.exp(jax.random.uniform(ks[10], (L, GD_HEADS), f32, math.log(1e-3), math.log(1e-1)))
    return {
        'x': normal(ks[0], (BATCH, SEQ, D_MODEL), 1.0),
        'mix_norm_g': gain(ks[1], (L, D_MODEL)),
        'w_in': normal(ks[2], (L, D_MODEL, IN_DIM), D_MODEL ** -0.5),
        'da_lambda_q1': normal(ks[3], (L, DA_HEAD_DIM), 0.1),
        'da_lambda_k1': normal(ks[4], (L, DA_HEAD_DIM), 0.1),
        'da_lambda_q2': normal(ks[5], (L, DA_HEAD_DIM), 0.1),
        'da_lambda_k2': normal(ks[6], (L, DA_HEAD_DIM), 0.1),
        'da_subln_g': gain(ks[7], (L, 2 * DA_HEAD_DIM)),
        'gd_conv_w': normal(ks[8], (L, CONV_WIDTH, 2 * GD_QK_DIM + GD_V_DIM), CONV_WIDTH ** -0.5),
        'gd_a_log': jnp.log(jax.random.uniform(ks[9], (L, GD_HEADS), f32, 1.0, 16.0)),
        'gd_dt_bias': dt + jnp.log(-jnp.expm1(-dt)),
        'gd_norm_g': gain(ks[11], (L, GD_HEAD_V)),
        'w_out': normal(ks[12], (L, D_MODEL, D_MODEL), D_MODEL ** -0.5),
        'ffn_norm_g': gain(ks[13], (L, D_MODEL)),
        'router_w': normal(ks[14], (L, D_MODEL, N_EXPERTS), D_MODEL ** -0.5),
        'router_b': normal(ks[15], (L, N_EXPERTS), 0.01),
        'exp_w_gate': normal(ks[16], (L, N_EXPERTS, D_MODEL, D_EXPERT), D_MODEL ** -0.5),
        'exp_b_gate': normal(ks[17], (L, N_EXPERTS, D_EXPERT), 0.01),
        'exp_w_up': normal(ks[18], (L, N_EXPERTS, D_MODEL, D_EXPERT), D_MODEL ** -0.5),
        'exp_b_up': normal(ks[19], (L, N_EXPERTS, D_EXPERT), 0.01),
        'exp_w_down': normal(ks[20], (L, N_EXPERTS, D_EXPERT, D_MODEL), D_EXPERT ** -0.5),
        'exp_b_down': normal(ks[21], (L, N_EXPERTS, D_MODEL), 0.01),
        'final_norm_g': gain(ks[22], (D_MODEL,)),
    }

def reference(x, mix_norm_g, w_in, da_lambda_q1, da_lambda_k1, da_lambda_q2, da_lambda_k2, da_subln_g, gd_conv_w, gd_a_log, gd_dt_bias, gd_norm_g, w_out, ffn_norm_g, router_w, router_b, exp_w_gate, exp_b_gate, exp_w_up, exp_b_up, exp_w_down, exp_b_down, final_norm_g):
    for i in range(DEPTH):
        x = hybrid_layer(x, i, mix_norm_g[i], w_in[i], da_lambda_q1[i], da_lambda_k1[i], da_lambda_q2[i], da_lambda_k2[i], da_subln_g[i], gd_conv_w[i], gd_a_log[i], gd_dt_bias[i], gd_norm_g[i], w_out[i], ffn_norm_g[i], router_w[i], router_b[i], exp_w_gate[i], exp_b_gate[i], exp_w_up[i], exp_b_up[i], exp_w_down[i], exp_b_down[i])
    return rms_norm(x, final_norm_g).astype(x.dtype)


_drawn_inputs = setup_inputs


def setup_inputs(seed=0):
    import zlib

    import numpy as np

    out = dict(_drawn_inputs(seed))
    spreads = {}
    factors = {'da_lambda_q2': 20.804,
     'router_b': 3.057,
     'exp_b_gate': 8.0,
     'exp_b_up': 8.0,
     'exp_b_down': 8.0,
     'final_norm_g': 7.965}
    for name, (base, spread) in spreads.items():
        noise = np.random.default_rng([zlib.crc32(name.encode()), seed]).standard_normal(out[name].shape)
        drawn = base * np.exp(spread * noise) if base else spread * noise
        out[name] = jnp.asarray(drawn.astype(out[name].dtype))
    for name, factor in factors.items():
        out[name] = (out[name] * factor).astype(out[name].dtype)
    return out
```

```python
import math
from contextlib import ExitStack

import numpy as np

import concourse.bass as bass
from concourse import mybir

F32 = mybir.dt.float32
F32R = mybir.dt.float32r
BF16 = mybir.dt.bfloat16
I32 = mybir.dt.int32
U32 = mybir.dt.uint32
ALU = mybir.AluOpType
ACT = mybir.ActivationFunctionType
AX = mybir.AxisListType

P = 128
D = 1024
SEQ = 512
NT = SEQ // P
KC = D // P
HALF = 512
H = 8
DH = 64
NE, TOPK = 32, 4
LEVELS = 7
EXTRA = SEQ * TOPK // (P + 1)
NBLK = NE + EXTRA
RT_W = NBLK + 1
EPS = 1e-6
LAM_INIT = 0.8 - 0.6 * math.exp(0.0)
NEG = -1e30
LIMIT, ALPHA = 7.0, 1.702

C_DAQ, C_DAK, C_DAV, C_GDQ = 0, D, 2 * D, 3 * D
C_Z, C_BA, C_GA, C_GB = 6 * D, 7 * D, 7 * D + 2 * H, 8 * D + 2 * H
IN_DIM = 9 * D + 2 * H

_widths = dict(ident=P, upper=P, later=P, before=P, ones=P, neg_m0=P, masks=(LEVELS - 1) * P, causal=P,
               cos=NT * 32, sin=NT * DH, iota=NE, base=NE, onehot=NE)
CST, _at = {}, 0
for _k, _w in _widths.items():
    CST[_k] = (_at, _at + _w)
    _at += _w
NCST = _at
_widths = dict(mix_g=KC, conv=24 * 4, a_log=H, dt=H, router_b=NE, lam=4 * DH, subln=P, gd_g=P)
PAR, _at = {}, 0
for _k, _w in _widths.items():
    PAR[_k] = (_at, _at + _w)
    _at += _w
NPAR = _at


class Signal:

    def __init__(self, sem, known):
        self.sem, self.known, self.count, self.marks = sem, known, 0, {}

    def next(self, key=None, by=1):
        self.count += by
        self.marks[key] = self.count
        return self.sem, by

    def at(self, key):
        return self.sem, self.known.get(key, 1)

    def last(self):
        return self.sem, self.count


def layer_kernel(nc, io, known):
    signals = {}
    with ExitStack() as ctx:
        def sb(name, shape, dt=F32):
            return ctx.enter_context(nc.sbuf_tensor(name, shape, dt))

        def signal(name):
            s = Signal(ctx.enter_context(nc.semaphore(name)), known.get(name, {}))
            signals[name] = s
            return s

        h2_dram = nc.dram_tensor("h2_rows", [SEQ, D], F32, kind="Internal").ap()
        rowtok_dram = nc.dram_tensor("row_token", [P * RT_W, 1], I32, kind="Internal").ap()
        y_dram = nc.dram_tensor("expert_rows", [NBLK * P, D], F32, kind="Internal").ap()

        cst = sb("cst", [P, NCST])
        par = sb("par", [P, NPAR])
        tokid = sb("tokid", [P, NT * TOPK], I32)
        arena_at = -(-nc.sbuf_base // 32) * 32
        arena = sb("arena", [P, 46 * 1024])

        def place(name, word, shape, dt=F32):
            return nc.alloc_sbuf_tensor_at(name, shape, dt, offset=arena_at + 4 * word)

        ring = place("ring", 0, [P, 6, 8 * HALF])
        xs = place("xs", 24 * 1024, [P, NT, D])
        hT = place("hT", 28 * 1024, [P, KC, SEQ])
        ob = place("ob", 32 * 1024, [P, NT, D])
        work = place("work", 36 * 1024, [P, 10 * 1024])
        RAW = (2, 4, 5)
        CHUNK = 2048
        w_hi = [place(f"w_hi{s}", w, [P, CHUNK], F32R) for s, w in enumerate((0, 4096, 3 * 4096, 28 * 1024))]
        w_lo = [place(f"w_lo{s}", w + CHUNK, [P, CHUNK], F32R) for s, w in enumerate((0, 4096, 3 * 4096, 28 * 1024))]
        xT_hi, xT_lo, avT_hi, avT_lo = (place(n, w, [P, D], F32R) for n, w in (
            ("xT_hi", 37 * 1024), ("xT_lo", 32 * 1024), ("avT_hi", 42 * 1024), ("avT_lo", 33 * 1024)))
        btab = sb("btab", [96, 3 * D], BF16)
        sel = sb("sel", [96, NE], BF16)
        wba = sb("wba", [P, KC, 2 * H])
        small = sb("small", [P, 1024])

        def C(name):
            a, b = CST[name]
            return cst[:, a:b]

        def G(name):
            a, b = PAR[name]
            return par[:, a:b]

        small_at = [0]

        def sm(width):
            a = small_at[0]
            small_at[0] += width
            assert small_at[0] <= 1024
            return small[:, a:a + width]

        ident = C("ident")
        causal = C("causal")

        def over_heads(ap, n):
            return ap.unsqueeze(1).to_broadcast([P, n, ap.shape[1]])

        def over_cols(ap, n):
            return ap.unsqueeze(2).to_broadcast([P, ap.shape[1], n])

        slot3 = ring[:, 3:6, :].rearrange("p s n -> p (s n)")
        qkvT = slot3.rearrange("p (c t) -> p c t", c=24)
        xn = ring[:, 3, :].rearrange("p (t c) -> p t c", t=NT)
        qaT = ring[:, 3, :].rearrange("p (h t) -> p h t", h=H)
        kaT = ring[:, 4, :].rearrange("p (h t) -> p h t", h=H)
        va = ring[:, 5, :].rearrange("p (t c) -> p t c", t=NT)
        oa = ring[:, 2, :].rearrange("p (t c) -> p t c", t=NT)
        mT = ring[:, 3, :].rearrange("p (c t) -> p c t", c=KC)
        h2 = ob[:, :, :]
        h2T = hT[:, :, :]

        def heads(ap):
            return ap.rearrange("p (h n) -> p h n", h=H)

        gdn = [ring[:, 2, k * 1024:(k + 1) * 1024] for k in range(4)]
        gdn += [xs[:, k, :] for k in range(4)]
        gdn += [work[:, k * 1024:(k + 1) * 1024] for k in range(10)]
        k_tok, v_w, aT, tri, triT, xlev, gl, dT = (heads(gdn[k]) for k in range(8))
        btm = [heads(gdn[8]), heads(gdn[9])]
        state, w_rhs, p_out, p_dec = (heads(gdn[k]) for k in range(10, 14))
        qs_s, a_row = heads(gdn[14]), heads(gdn[15])
        qkd = work[:, 8 * 1024:10 * 1024].rearrange("p (h c n) -> p h c n", h=H, c=2)
        raw = [work[:, k * 520:k * 520 + SEQ + 3] for k in range(2)]
        cacc = [work[:, 1040 + k * SEQ:1040 + (k + 1) * SEQ] for k in range(2)]
        sqb = [work[:, 2064 + k * SEQ:2064 + (k + 1) * SEQ] for k in range(2)]
        bias_st = work[0:96, 3200:3200 + D]
        bias_re = work[0:96, 3200 + D:3200 + 2 * D]
        bias_hi = work[0:96, 3200 + 2 * D:3200 + 2 * D + D // 2].bitcast(BF16)
        bias_mid = work[0:96, 3200 + 2 * D + D // 2:3200 + 3 * D].bitcast(BF16)
        bias_lo = work[0:96, 3200 + 3 * D:3200 + 3 * D + D // 2].bitcast(BF16)
        rope1 = [work[:, k * 512:(k + 1) * 512] for k in range(2)]
        rope2 = [work[:, 1024 + k * 512:1536 + k * 512] for k in range(2)]
        roped = [work[:, 2048 + k * 2048:4096 + k * 2048].rearrange("p (t c) -> p t c", t=NT) for k in range(2)]
        probs = [[work[:, (2 * k + c) * 512:(2 * k + c + 1) * 512] for c in range(2)] for k in range(2)]
        wdiff = [work[:, 2048 + k * 512:2560 + k * 512] for k in range(2)]
        wT = [work[:, 3072 + k * 512:3584 + k * 512] for k in range(2)]
        gate_s = [work[:, 7168 + k * 512:7680 + k * 512] for k in range(2)]
        sqm = [work[:, 8192 + k * 1024:9216 + k * 1024] for k in range(2)]
        g2 = work[:, 0:1024]
        gf = work[:, 9216:10240]
        rw = work[:, 1024:1024 + KC * NE].rearrange("p (c e) -> p c e", c=KC)
        rt = work[:, 2048:9216]
        rt_cols, n = {}, 4096
        for name, w in dict(scat=16, lg=128, top=32, tix=32, tixf=16, hot=512, mask=128, gsum=4, cnt=32, xb=32, inc=32, shift=32,
                            big=512, bef=16, rank=128, dest=128, dk=16, blk=16, blkf=16).items():
            rt_cols[name] = (n, n + w)
            n += w
        assert n <= 7168

        def rt_at(name):
            lo, hi = rt_cols[name]
            return rt[:, lo:hi]

        xg = work[:, 0:1024]
        gm = [work[:, 2048 + k * 512:2560 + k * 512] for k in range(2)]
        sg = [work[:, 3072 + k * 512:3584 + k * 512] for k in range(2)]
        um = [work[:, 4096 + k * 512:4608 + k * 512] for k in range(2)]
        av = [work[:, 5120 + k * 512:5632 + k * 512] for k in range(2)]
        ys = work[:, 7168:8192]

        ps = [ctx.enter_context(nc.psum_tensor(f"bank{b}", [P, HALF], F32)) for b in range(8)]

        ss, rstd = sm(NT), sm(NT)
        ba = sm(NT * 2 * H).rearrange("p (t c) -> p t c", t=NT)
        beta, gdec, spt, spe = (sm(NT * H).rearrange("p (t h) -> p t h", t=NT) for _ in range(4))
        ealog = sm(H)
        dec = sm(3 * NT * H)
        eg, ed, glast = (dec[:, k * NT * H:(k + 1) * NT * H].rearrange("p (t h) -> p t h", t=NT) for k in range(3))
        nrm = sm(NT * 2 * H).rearrange("p (t c) -> p t c", t=NT)
        k_s, v_s, k_w, o_q, o_s = (sm(NT * H).rearrange("p (t h) -> p t h", t=NT) for _ in range(5))
        lam2, nlam = sm(2), sm(1)
        mx, nmx, esum, recs, ratio = sm(4), sm(4), sm(4), sm(4), sm(2)
        osq = sm(2 * NT * H)
        e_idx = sm(RT_W).bitcast(I32)
        e_idx1 = sm(1).bitcast(I32)
        e_held = sm(1).bitcast(I32)
        y_idx = sm(NT * TOPK).bitcast(I32)
        gw = sm(NT * TOPK)
        be = sm(16).bitcast(I32)
        lamtmp = sm(DH)

        ld_cst, ld_x, ld_ba, ld_bias, ld_rt, ld_x2, ld_g = (signal(n) for n in (
            "ld_cst", "ld_x", "ld_ba", "ld_bias", "ld_rt", "ld_x2", "ld_g"))
        ld_w = [signal(f"ld_w{s}") for s in range(2)]
        pe_hT, pe_proj, pe_gd, pe_att, pe_mrg, pe_rt = (signal(n) for n in (
            "pe_hT", "pe_proj", "pe_gd", "pe_att", "pe_mrg", "pe_rt"))
        act_pre, act_conv, act_gd, act_att, act_mrg, act_rt = (signal(n) for n in (
            "act_pre", "act_conv", "act_gd", "act_att", "act_mrg", "act_rt"))
        dve_pre, dve_conv, dve_gd, dve_att, dve_mrg, dve_rt, dve_fin = (signal(n) for n in (
            "dve_pre", "dve_conv", "dve_gd", "dve_att", "dve_mrg", "dve_rt", "dve_fin"))
        pool_pre, pool_gd, pool_att, pool_mrg = (signal(n) for n in ("pool_pre", "pool_gd", "pool_att", "pool_mrg"))
        st_h2, st_rt, st_y, st_out, act_fin = (signal(n) for n in ("st_h2", "st_rt", "st_y", "st_out", "act_fin"))
        ld_row = [signal(f"ld_row{s}") for s in range(6)]
        x_rows, x_idx = signal("x_rows"), signal("x_idx")
        e_tr = signal("e_tr")
        ld_e = [signal(f"ld_e{r}") for r in range(6)]
        e_used, a_hi, v_lo, p_lo = signal("e_used"), signal("a_hi"), signal("v_lo"), signal("p_lo")
        v_act, v_y, v_tr = signal("v_act"), signal("v_y"), signal("v_tr")
        a_sig, a_tr, a_y = signal("a_sig"), signal("a_tr"), signal("a_y")

        chunks = [("in", C_GDQ + HALF * j) for j in range(6)]
        chunks += [("in", C_DAQ + HALF * j) for j in range(6)]
        chunks += [("in", C_Z), ("in", C_Z + HALF), ("in", C_GA), ("in", C_GA + HALF), ("in", C_GB), ("in", C_GB + HALF)]
        chunks += [("out", 0), ("out", HALF)]

        def wtile(n):
            return ring[:, n % 2, :].rearrange("p (c n) -> p c n", c=KC)

        def last_of(n):
            if n < 6:
                return "gd", 4 * n + 3
            if n < 12:
                return "da", n - 6, NT - 1
            return ("z", "ga", "gb", "out")[(n - 12) // 2], n % 2, NT - 1

        def w_landed(e, n):
            e.wait_ge(ld_w[n % 2].sem, 16 * (n // 2 + 1))

        block = ctx.enter_context(nc.Block())

        def chunk_source(e, c):
            if c < 8:
                w, hf, rows = io["w_up" if c // 2 % 2 else "w_gate"], c // 4, D // 2
                return w[bass.ds(e, 1), c % 2 * rows:(c % 2 + 1) * rows, hf * HALF:(hf + 1) * HALF].rearrange("e (c p) n -> p (e c) n", p=P)
            rows = D // 4
            return io["w_down"][bass.ds(e, 1), (c - 8) * rows:(c - 7) * rows, :].rearrange("e (c p) n -> p (e c) n", p=P)

        def raw_chunk(c):
            return ring[:, RAW[c // 2 % 3], c % 2 * CHUNK:(c % 2 + 1) * CHUNK]

        ON_POOL = (1, 5, 9)

        def small_part(i, c):
            mine = [k for k in range(12) if (k in ON_POOL) == (c in ON_POOL)]
            return (p_lo if c in ON_POOL else v_lo).sem, len(mine) * i + mine.index(c) + 1

        @block.sync
        def _(sp):
            sp.dma_start(xs[:, :, :], io["x"].rearrange("(t p) c -> p t c", p=P)).then_inc(ld_x.sem, 16)
            sp.dma_start(cst[:, :], io["cst"]).then_inc(ld_cst.sem, 16)
            sp.dma_start(par[:, :], io["par"]).then_inc(ld_cst.sem, 16)
            sp.dma_start(tokid[:, :], io["tokid"]).then_inc(ld_cst.sem, 16)
            for n, (which, c0) in enumerate(chunks):
                if n >= 2:
                    sp.wait_ge(*pe_proj.at(last_of(n - 2)))
                src = io["w_in"] if which == "in" else io["w_out"]
                sp.dma_start(wtile(n), src[:, c0:c0 + HALF].rearrange("(c p) n -> p c n", p=P)).then_inc(ld_w[n % 2].sem, 16)
                if n == 1:
                    sp.dma_start(wba[:, :, :], io["w_in"][:, C_BA:C_BA + 2 * H].rearrange("(c p) n -> p c n", p=P)).then_inc(ld_ba.sem, 16)
                if n == 12:
                    sp.wait_ge(*dve_gd.at("end"))
                    sp.wait_ge(*pool_gd.at("end"))
                    sp.dma_start(xs[:, :, :], io["x"].rearrange("(t p) c -> p t c", p=P)).then_inc(ld_x2.sem, 16)
            sp.wait_ge(*act_att.at("end"))
            sp.wait_ge(*dve_att.at("end"))
            sp.wait_ge(*pool_att.at("end"))
            sp.wait_ge(*pe_att.at("end"))
            sp.dma_start(g2, io["ffn_g"].to_broadcast([P, D])).then_inc(ld_g.sem, 16)
            sp.dma_start(rw, io["router_w"].rearrange("(c p) e -> p c e", p=P)).then_inc(ld_g.sem, 16)

            def load_block(e, i):
                for c in range(12):
                    if c >= 6 or not isinstance(i, int):
                        sp.wait_ge(*(small_part(i, c - 6) if c >= 6 else small_part(i - 1, c + 6)))
                    sp.dma_start(raw_chunk(c).rearrange("p (c n) -> p c n", n=HALF if c < 8 else D), chunk_source(e, c)).then_inc(ld_e[c % 6].sem, 16)

            sp.wait_ge(*act_mrg.at("mT_last"))
            sp.wait_ge(*pe_mrg.at(("mT", KC - 1)))
            sp.wait_ge(*pool_mrg.at("merged"))
            sp.dma_start(gf, io["final_g"].to_broadcast([P, D])).then_inc(ld_g.sem, 16)
            load_block(0, 0)
            with sp.Fori(1, NE) as i:
                load_block(i, i)
            sp.wait_ge(*dve_rt.at("be"))
            n_extra = sp.value_load(be[0:1, 15:16], min_val=0, max_val=EXTRA)
            with sp.If(n_extra > 0):
                with sp.Fori(NE, NBLK) as i:
                    e = sp.value_load(be[0:1, bass.ds(i - NE, 1)], min_val=0, max_val=NE - 1)
                    load_block(e, i)
            for t in range(NT):
                sp.wait_ge(*dve_fin.at(("out", t)))
                sp.dma_start(io["out"].rearrange("(t p) c -> p t c", p=P)[:, t, :], xs[:, t, :]).then_inc(st_out.sem, 16)
            sp.wait_ge(st_out.sem, 16 * NT)

        @block.gpsimd
        def _(g):
            def nxt(key=None):
                return pool_pre.next(key)

            g.memset(e_idx[:, :], 0).then_inc(*nxt())
            g.wait_ge(*pool_pre.last())
            g.dma_start(rowtok_dram.rearrange("(p b) o -> p (b o)", p=P), e_idx[:, :]).then_inc(st_rt.sem, 16)
            for r in range(2):
                g.memset(raw[r][:, 0:3], 0.0).then_inc(*nxt("pad"))
            n = 0
            for j, name in enumerate(("b_gate", "b_up", "b_down")):
                for part in range(3):
                    g.dma_start(bias_st[32 * part:32 * part + NE, :], io[name]).then_inc(ld_bias.sem, 16)
                    n += 16
                g.wait_ge(ld_bias.sem, n)
                col = slice(j * D, (j + 1) * D)
                g.tensor_copy(bias_hi, bias_st).then_inc(*nxt())
                g.wait_ge(*pool_pre.last())
                g.tensor_tensor(bias_re, bias_st, bias_hi, ALU.subtract).then_inc(*nxt())
                g.wait_ge(*pool_pre.last())
                g.tensor_copy(bias_mid, bias_re).then_inc(*nxt())
                g.wait_ge(*pool_pre.last())
                g.tensor_tensor(bias_re, bias_re, bias_mid, ALU.subtract).then_inc(*nxt())
                g.wait_ge(*pool_pre.last())
                g.tensor_copy(bias_lo, bias_re).then_inc(*nxt())
                g.wait_ge(*pool_pre.last())
                g.tensor_copy(btab[0:32, col], bias_hi[0:32, :]).then_inc(*nxt())
                g.tensor_copy(btab[32:64, col], bias_mid[32:64, :]).then_inc(*nxt())
                g.tensor_copy(btab[64:96, col], bias_lo[64:96, :]).then_inc(*nxt())
                g.wait_ge(*pool_pre.last())
            g.wait_ge(ld_cst.sem, 48)
            g.tensor_copy(sel[:, :], C("onehot")[0:96, :]).then_inc(*nxt("bias"))

            for ct in range(2 * H):
                g.wait_ge(*act_conv.at(("silu", ct)))
                if ct >= 2:
                    g.wait_ge(*pe_gd.at(("ssq", ct - 2)))
                g.tensor_tensor(sqb[ct % 2], qkvT[:, ct, :], qkvT[:, ct, :], ALU.mult).then_inc(*pool_gd.next(("sq", ct)))

            def gdn_pool(t):
                for gr in range(2):
                    hs = slice(4 * gr, 4 * gr + 4)
                    g.wait_ge(*act_gd.at(("dT", t, gr)))
                    g.tensor_tensor(dT[:, hs, :], dT[:, hs, :], over_heads(C("upper"), 4), ALU.mult).then_inc(*pool_gd.next(("dT", t, gr)))
                for l in range(1, LEVELS):
                    if l == 1:
                        g.wait_ge(*act_gd.at(("aT", t, 1)))
                    if l >= 3:
                        g.wait_ge(*pe_gd.at(("X", t, l - 2, 1)))
                    a = C("masks")[:, (l - 1) * P:l * P]
                    g.tensor_tensor(btm[l % 2], aT, over_heads(a, H), ALU.mult).then_inc(*pool_gd.next(("B", t, l)))
                if t > 0:
                    for gr in range(2):
                        hs = slice(4 * gr, 4 * gr + 4)
                        cs = slice(gr * HALF, (gr + 1) * HALF)
                        g.wait_ge(*dve_gd.at(("o", t, gr)))
                        g.tensor_tensor(ob[:, t, cs], ob[:, t, cs], qs_s[:, hs, :].rearrange("p h n -> p (h n)"), ALU.add).then_inc(*pool_gd.next(("o", t, gr)))

            for t in range(NT):
                gdn_pool(t)
            g.wait_ge(*pool_gd.last())
            g.memset(e_idx1, 0).then_inc(*pool_gd.next("end"))

            for c in range(4):
                for t in range(NT):
                    k = c * NT + t
                    g.wait_ge(*dve_att.at(("rope", c, t)))
                    if c >= 2 and t == 0:
                        g.wait_ge(*pe_att.at(("qkT", c - 2, 3)))
                    g.tensor_tensor(roped[c % 2][:, t, :], rope1[k % 2], rope2[k % 2], ALU.add).then_inc(*pool_att.next(("rope", c, t)))
            g.wait_ge(*pool_att.last())
            g.memset(e_idx1, 0).then_inc(*pool_att.next("end"))

            for k in range(2 * NT):
                src = (oa if k < NT else ob)[:, k % NT, :]
                if k == 0:
                    g.wait_ge(*act_att.at("end"))
                if k >= 2:
                    g.wait_ge(*dve_mrg.at(("osq", k - 2)))
                g.tensor_tensor(sqm[k % 2], src, src, ALU.mult).then_inc(*pool_mrg.next(("sq", k)))
            for c in range(2):
                for t in range(NT):
                    cs = slice(c * HALF, (c + 1) * HALF)
                    g.wait_ge(*dve_mrg.at(("gb", c, t)))
                    g.tensor_tensor(ob[:, t, cs], ob[:, t, cs], oa[:, t, cs], ALU.add).then_inc(*pool_mrg.next(("m", c, t)))
            g.wait_ge(*pool_mrg.last())
            g.memset(e_idx1, 0).then_inc(*pool_mrg.next("merged"))

            g.wait_ge(st_rt.sem, 16)
            g.wait_ge(*dve_rt.at("dest"))
            scat = rt_at("scat").bitcast(I32)
            for k in range(NT * TOPK):
                g.indirect_dma_start(out=rowtok_dram[:, :], out_offset=bass.IndirectOffsetOnAxis(ap=scat[:, k:k + 1], axis=0),
                                     in_=tokid[:, k:k + 1], in_offset=None).then_inc(st_rt.sem, 16)
            g.wait_ge(st_rt.sem, 16 * (NT * TOPK + 1))
            g.dma_start(e_idx[:, :], rowtok_dram.rearrange("(p b) o -> p (b o)", p=P)).then_inc(ld_rt.sem, 16)
            g.wait_ge(ld_rt.sem, 16)
            g.wait_ge(st_h2.sem, 16 * NT)
            g.wait_ge(*dve_rt.at("end"))

            def gather(i, first=False):
                g.tensor_copy(e_idx1, e_idx[:, bass.ds(i, 1)] if not first else e_idx[:, 0:1]).then_inc(x_idx.sem, 1)
                g.wait_ge(x_idx.sem, 2 * i + 1)
                g.tensor_tensor(e_held, e_idx1, e_idx1, ALU.add).then_inc(x_idx.sem, 1)
                g.indirect_dma_start(out=xg, out_offset=None, in_=h2_dram[:, :],
                                     in_offset=bass.IndirectOffsetOnAxis(ap=e_idx1, axis=0)).then_inc(x_rows.sem, 16)

            gather(0, True)

            def body(i):
                g.wait_ge(e_tr.sem, 4 * i + 2)
                g.wait_ge(x_rows.sem, 16 * i + 16)
                g.wait_ge(x_idx.sem, 2 * i + 2)
                gather(i + 1)
                for c in ON_POOL:
                    g.wait_ge(a_hi.sem, 12 * i + c + 1)
                    g.tensor_tensor(w_lo[c % 4][:, :], raw_chunk(c), w_hi[c % 4][:, :], ALU.subtract).then_inc(p_lo.sem, 1)

            body(0)
            with g.Fori(1, NE) as i:
                body(i)
            n_extra = g.value_load(be[0:1, 15:16], min_val=0, max_val=EXTRA)
            with g.If(n_extra > 0):
                with g.Fori(NE, NBLK) as i:
                    body(i)
                g.wait_ge(x_rows.sem, 16 * (NBLK + 1))
                g.wait_ge(st_y.sem, 16 * (NBLK + 1))
            g.wait_ge(x_rows.sem, 16 * (NE + 1))
            g.wait_ge(st_y.sem, 16 * (NE + 1))

            def collect(rows):
                for k in range(NT * TOPK):
                    r = k % 6
                    if k >= 6:
                        g.wait_ge(*dve_fin.at(("row", k - 6)))
                    g.indirect_dma_start(out=ring[:, r, 0:D], out_offset=None, in_=rows,
                                         in_offset=bass.IndirectOffsetOnAxis(ap=y_idx[:, k:k + 1], axis=0)).then_inc(ld_row[r].sem, 16)

            with g.If(n_extra > 0):
                collect(y_dram[:, :])
            with g.Else():
                collect(y_dram[0:NE * P, :])

        @block.scalar
        def _(a):
            a.wait_ge(ld_x.sem, 16)
            for t in range(NT):
                a.activation(xn[:, t, :], xs[:, t, :], ACT.Square, accum_out=ss[:, t:t + 1]).then_inc(*act_pre.next(("ss", t)))
            a.wait_ge(*dve_pre.at("var"))
            a.activation(rstd, ss, ACT.Sqrt).then_inc(*act_pre.next("std"))
            a.wait_ge(ld_cst.sem, 48)
            for kc in range(0, KC, 2):
                a.wait_ge(*pe_hT.at(kc))
                a.activation(hT[:, kc, :], ps[kc][:, :], ACT.Copy, scale=G("mix_g")[:, kc:kc + 1]).then_inc(*act_pre.next(("hT", kc)))

            def silu(ct):
                a.wait_ge(*dve_conv.at(ct))
                a.activation(qkvT[:, ct, :], cacc[ct % 2], ACT.Silu).then_inc(*act_conv.next(("silu", ct)))

            for ct in range(3 * H):
                a.wait_ge(*pe_proj.at(("gd", ct)))
                if ct == 0:
                    a.wait_ge(*pool_pre.at("pad"))
                if ct >= 2:
                    a.wait_ge(*dve_conv.at(ct - 2))
                a.activation(raw[ct % 2][:, 3:], ps[ct % 4][:, :], ACT.Copy).then_inc(*act_conv.next(("raw", ct)))
                if ct >= 1:
                    silu(ct - 1)
            silu(3 * H - 1)

            a.wait_ge(*dve_gd.at("ba"))
            a.activation(beta, ba[:, :, 0:H], ACT.Sigmoid).then_inc(*act_gd.next("beta"))
            a.activation(ealog, G("a_log"), ACT.Exp).then_inc(*act_gd.next())
            for k in range(2):
                a.wait_ge(*dve_gd.at(("lam", k)))
                a.activation(lam2[:, k:k + 1], nlam if k else lam2[:, 0:1], ACT.Exp).then_inc(*act_gd.next(("lam", k)))
            a.wait_ge(*dve_gd.at("nabs"))
            a.activation(spe, spe, ACT.Exp).then_inc(*act_gd.next("spe"))
            a.wait_ge(*dve_gd.at("spe1"))
            a.activation(spe, spe, ACT.Ln).then_inc(*act_gd.next("ln"))
            a.wait_ge(*dve_gd.at("nrm"))
            a.activation(nrm, nrm, ACT.Sqrt).then_inc(*act_gd.next("nrm"))
            a.wait_ge(*pe_gd.at("dec"))
            a.activation(dec, ps[5][:, 0:3 * NT * H], ACT.Exp).then_inc(*act_gd.next("dec"))

            def flat(ap, gr):
                return ap[:, 4 * gr:4 * gr + 4, :].rearrange("p h n -> p (h n)")

            for t in range(NT):
                for gr in range(2):
                    a.wait_ge(*pe_gd.at(("D", t, gr)))
                    if t > 0:
                        a.wait_ge(*dve_gd.at(("qkd", t - 1, 3)))
                    a.activation(flat(dT, gr), ps[gr][:, :], ACT.Exp).then_inc(*act_gd.next(("dT", t, gr)))
                for gr in range(2):
                    a.wait_ge(*pe_gd.at(("K", t, gr)))
                    if t > 0:
                        a.wait_ge(*pe_gd.at(("dS", t - 1, 1)))
                    a.activation(flat(k_tok, gr), ps[6 + gr][:, :], ACT.Copy).then_inc(*act_gd.next(("K", t, gr)))
                for gr in range(2):
                    a.wait_ge(*pe_gd.at(("aT", t, gr)))
                    if t > 0:
                        a.wait_ge(*pool_gd.at(("B", t - 1, LEVELS - 1)))
                    a.activation(flat(aT, gr), ps[4 + gr][:, :], ACT.Copy).then_inc(*act_gd.next(("aT", t, gr)))
                for gr in range(2):
                    a.wait_ge(*pe_gd.at(("triT", t, gr)))
                    a.activation(flat(triT, gr), ps[6 + gr][:, :], ACT.Copy).then_inc(*act_gd.next(("triT", t, gr)))
                for l in range(1, LEVELS):
                    for gr in range(2):
                        a.wait_ge(*pe_gd.at(("X", t, l, gr)))
                        a.wait_ge(*pe_gd.at(("YT", t, l - 1, gr) if l > 1 else ("triT", t, gr)))
                        a.activation(flat(xlev, gr), ps[gr][:, :], ACT.Copy).then_inc(*act_gd.next(("X", t, l, gr)))
                for gr in range(2):
                    a.wait_ge(*pe_gd.at(("P", t, gr)))
                    a.activation(flat(p_out, gr), ps[2 + gr][:, :], ACT.Copy).then_inc(*act_gd.next(("P", t, gr)))

            for c in range(4):
                for h4 in range(4):
                    a.wait_ge(*pe_att.at(("qkT", c, h4)))
                    dst = (qaT if c < 2 else kaT)[:, 4 * (c % 2) + h4, :]
                    a.activation(dst, ps[4 + h4][:, :], ACT.Copy).then_inc(*act_att.next(("qkT", c, h4)))
            for c in range(2):
                for t in range(NT):
                    a.wait_ge(*pe_proj.at(("da", 4 + c, t)))
                    a.activation(va[:, t, c * HALF:(c + 1) * HALF], ps[t][:, :], ACT.Copy).then_inc(*act_att.next(("v", c, t)))

            def att_wT(n):
                h, i = divmod(n, NT)
                a.wait_ge(*pe_att.at(("wT", n)))
                a.activation(wT[n % 2][:, 0:(i + 1) * P], ps[4 + n % 2][:, 0:(i + 1) * P], ACT.Copy).then_inc(*act_att.next(("wT", n)))

            def att_out(n):
                h, i = divmod(n, NT)
                a.wait_ge(*pe_att.at(("pv", n)))
                a.activation(oa[:, i, h * P:(h + 1) * P], ps[6 + n % 2][:, 0:P], ACT.Copy,
                             scale=recs[:, 2 * (n % 2):2 * (n % 2) + 1]).then_inc(*act_att.next(("out", n)))

            NS = H * NT
            for n in range(NS + 2):
                if n < NS:
                    i = n % NT
                    for c in range(2):
                        k = 2 * (n % 2) + c
                        a.wait_ge(*dve_att.at(("max", n, c)))
                        if n >= 2:
                            a.wait_ge(*dve_att.at(("diff", n - 2)))
                        a.activation(probs[n % 2][c][:, 0:(i + 1) * P], ps[k][:, 0:(i + 1) * P], ACT.Exp, bias=nmx[:, k:k + 1],
                                     scale=DH ** -0.5, accum_out=esum[:, k:k + 1]).then_inc(*act_att.next(("exp", n, c)))
                if n >= 1 and n - 1 < NS:
                    att_wT(n - 1)
                if n >= 2:
                    att_out(n - 2)
            a.wait_ge(*act_att.last())
            a.activation(lamtmp[:, 0:1], lamtmp[:, 0:1], ACT.Copy).then_inc(*act_att.next("end"))

            a.wait_ge(*dve_mrg.at("ovar"))
            a.activation(osq, osq, ACT.Sqrt).then_inc(*act_mrg.next("ostd"))
            k = 0
            for j, name in enumerate(("z", "ga", "gb")):
                for c in range(2):
                    for t in range(NT):
                        a.wait_ge(*pe_proj.at((name, c, t)))
                        if k >= 2:
                            a.wait_ge(*dve_mrg.at(("gate", k - 2)))
                        a.activation(gate_s[k % 2], ps[k % 4][:, :], ACT.Sigmoid if j else ACT.Silu).then_inc(*act_mrg.next(("gate", k)))
                        k += 1
            for kc in range(KC):
                a.wait_ge(*pe_mrg.at(("mT", kc)))
                a.activation(mT[:, kc, :], ps[4 + kc % 4][:, :], ACT.Copy).then_inc(*act_mrg.next("mT_last" if kc == KC - 1 else ("mT", kc)))

            for t in range(NT):
                a.wait_ge(*dve_mrg.at(("x1", 1, t)))
                a.activation(rt[:, t * D:(t + 1) * D], xs[:, t, :], ACT.Square, accum_out=ss[:, t:t + 1]).then_inc(*act_rt.next(("ss", t)))
            a.wait_ge(*dve_rt.at("var"))
            a.activation(rstd, ss, ACT.Sqrt).then_inc(*act_rt.next("std"))
            for t in range(NT):
                a.wait_ge(*dve_rt.at(("h2", t)))
                a.dma_start(h2_dram[t * P:(t + 1) * P, :], h2[:, t, :]).then_inc(st_h2.sem, 16)
            for kc in range(KC):
                a.wait_ge(*pe_rt.at(("h2T", kc)))
                a.activation(h2T[:, kc, :], ps[4 + kc % 4][:, :], ACT.Copy).then_inc(*act_rt.next(("h2T", kc)))
            a.wait_ge(*dve_rt.at("gsub"))
            a.activation(gw, gw, ACT.Exp).then_inc(*act_rt.next("gexp"))
            a.wait_ge(*dve_rt.at("end"))

            def to_hi(dst, k, bank, value):
                a.wait_ge(e_tr.sem, value)
                a.activation(dst[:, k * HALF:(k + 1) * HALF], ps[bank][:, :], ACT.Copy).then_inc(a_tr.sem, 1)

            for half in range(2):
                to_hi(xT_hi, half, 7 - half, half + 1)

            def w_parts(i, chunks):
                for c in chunks:
                    a.wait_ge(ld_e[c % 6].sem, 32 * i + 16 * (c // 6) + 16)
                    a.wait_ge(e_used.sem, 12 * i + c + 1)
                    a.activation(w_hi[c % 4][:, :], raw_chunk(c), ACT.Copy).then_inc(a_hi.sem, 1)

            def result(i):
                a.wait_ge(e_used.sem, 12 * i + 16)
                a.wait_ge(st_y.sem, 16 * i + 16)
                a.activation(ys[:, HALF:D], ps[5][:, :], ACT.Copy).then_inc(a_y.sem, 1)
                a.wait_ge(v_y.sem, i + 2)
                a.wait_ge(a_y.sem, i + 2)
                a.dma_start(y_dram[bass.ds(i * P, P), :], ys[:, :]).then_inc(st_y.sem, 16)

            def body(i, before=False):
                w_parts(i, range(0, 3))
                if before:
                    result(i - 1)
                w_parts(i, range(3, 8))
                a.wait_ge(v_act.sem, 8 * i + 9)
                a.activation(sg[0], gm[0], ACT.Sigmoid, scale=ALPHA).then_inc(a_sig.sem, 1)
                w_parts(i, range(8, 10))
                to_hi(avT_hi, 0, 6, 4 * i + 3)
                w_parts(i, range(10, 11))
                a.wait_ge(v_act.sem, 8 * i + 13)
                a.activation(sg[1], gm[1], ACT.Sigmoid, scale=ALPHA).then_inc(a_sig.sem, 1)
                to_hi(xT_hi, 0, 7, 4 * i + 4)
                w_parts(i, range(11, 12))
                to_hi(xT_hi, 1, 6, 4 * i + 5)
                to_hi(avT_hi, 1, 7, 4 * i + 6)

            a.sem_inc(st_y.sem, 16)
            a.sem_inc(a_y.sem, 1)
            body(0)
            with a.Fori(1, NE) as i:
                body(i, True)
            result(NE - 1)
            n_extra = a.value_load(be[0:1, 15:16], min_val=0, max_val=EXTRA)
            with a.If(n_extra > 0):
                with a.Fori(NE, NBLK) as i:
                    body(i)
                    result(i)

            for t in range(NT):
                a.wait_ge(*dve_fin.at(("sum", t)))
                a.activation(hT[:, 0:2, :].rearrange("p c n -> p (c n)"), xs[:, t, :], ACT.Square,
                             accum_out=ss[:, t:t + 1]).then_inc(*act_fin.next(("ss", t)))
                a.wait_ge(*dve_fin.at(("var", t)))
                a.activation(rstd[:, t:t + 1], ss[:, t:t + 1], ACT.Sqrt).then_inc(*act_fin.next(("std", t)))

        @block.tensor
        def _(pe):
            pe.sem_inc(e_used.sem, 4)
            pe.wait_ge(ld_cst.sem, 48)
            pe.wait_ge(*dve_pre.at(("xn", NT - 1)))
            for kc in range(KC):
                for t in range(NT):
                    mm = pe.transpose(ps[kc][:, t * P:(t + 1) * P], xn[:, t, kc * P:(kc + 1) * P], ident)
                mm.then_inc(*pe_hT.next(kc))

            pe.wait_ge(*act_pre.at(("hT", KC - 2)))
            pe.wait_ge(*dve_pre.at(("hT", KC - 1)))
            for ct in range(3 * H):
                if ct % 4 == 0:
                    w_landed(pe, ct // 4)
                if ct >= 4:
                    pe.wait_ge(*act_conv.at(("raw", ct - 4)))
                for kc in range(KC):
                    mm = pe.matmul(ps[ct % 4][:, :], wtile(ct // 4)[:, kc, (ct % 4) * P:(ct % 4 + 1) * P], hT[:, kc, :],
                                   start=kc == 0, stop=kc == KC - 1)
                mm.then_inc(*pe_proj.next(("gd", ct)))
            pe.wait_ge(ld_ba.sem, 16)
            for t in range(NT):
                for kc in range(KC):
                    mm = pe.matmul(ps[4][:, t * 2 * H:(t + 1) * 2 * H], hT[:, kc, t * P:(t + 1) * P], wba[:, kc, :],
                                   start=kc == 0, stop=kc == KC - 1)
            mm.then_inc(*pe_proj.next("ba"))
            for ct in range(2 * H):
                pe.wait_ge(*pool_gd.at(("sq", ct)))
                for t in range(NT):
                    c = t * 2 * H + ct
                    mm = pe.matmul(ps[6][:, c:c + 1], sqb[ct % 2][:, t * P:(t + 1) * P], C("ones")[:, 0:1], start=True, stop=True)
                mm.then_inc(*pe_gd.next(("ssq", ct)))
            pe.wait_ge(*dve_gd.at("g"))
            gall = gdec.rearrange("p t h -> p (t h)")
            n = NT * H
            for j, name in enumerate(("upper", "later", "ones")):
                mm = pe.matmul(ps[5][:, j * n:(j + 1) * n], C(name), gall, start=True, stop=True)
            mm.then_inc(*pe_gd.next("dec"))

            def qT(h, t):
                return qkvT[:, h, t * P:(t + 1) * P]

            def kT(h, t):
                return qkvT[:, H + h, t * P:(t + 1) * P]

            def four(bank, gr, name, key, lhsT, rhs=None):
                for j in range(4):
                    h = 4 * gr + j
                    out = ps[bank][:, j * P:(j + 1) * P]
                    if rhs is None:
                        mm = pe.transpose(out, lhsT(h), ident)
                    else:
                        mm = pe.matmul(out, lhsT(h), rhs(h), start=True, stop=True)
                mm.then_inc(*pe_gd.next((name,) + key))

            pe.wait_ge(*act_gd.at("dec"))
            pe.wait_ge(*act_conv.at(("silu", 3 * H - 1)))
            pe.wait_ge(*dve_gd.at("coef"))
            for t in range(NT):
                for gr in range(2):
                    pe.wait_ge(*dve_gd.at(("gl", t)))
                    if t > 1:
                        pe.wait_ge(*dve_gd.at(("qs", t - 1, gr)))
                    four(gr, gr, "D", (t, gr), lambda h: gl[:, h, :], lambda h: C("upper"))
                for pr in range(4):
                    if t > 0:
                        if pr < 2:
                            pe.wait_ge(*act_gd.at(("P", t - 1, pr)))
                        else:
                            pe.wait_ge(*dve_gd.at(("S", t - 1, pr - 2)))
                    for j in range(2):
                        h = 2 * pr + j
                        qk = qkvT[:, h:h + H + 1:H, t * P:(t + 1) * P]
                        mm = pe.matmul(ps[2 + pr][:, j * 2 * P:(j + 1) * 2 * P], kT(h, t), qk, start=True, stop=True)
                    mm.then_inc(*pe_gd.next(("qk", t, pr)))
                for gr in range(2):
                    if t > 0:
                        pe.wait_ge(*dve_gd.at(("o", t - 1, gr)))
                    four(6 + gr, gr, "V", (t, gr), lambda h: qkvT[:, 2 * H + h, t * P:(t + 1) * P])
                for gr in range(2):
                    pe.wait_ge(*dve_gd.at(("v", t, gr)))
                    four(6 + gr, gr, "K", (t, gr), lambda h: kT(h, t))
                for gr in range(2):
                    pe.wait_ge(*dve_gd.at(("qkd", t, 2 * gr + 1)))
                    pe.wait_ge(*act_gd.at(("dT", t, gr)))
                    four(gr, gr, "Yt", (t, gr), lambda h: qkd[:, h, 1, :])
                for gr in range(2):
                    pe.wait_ge(*dve_gd.at(("a", t, gr)))
                    pe.wait_ge(*dve_gd.at(("qkd", t, 3)))
                    four(4 + gr, gr, "aT", (t, gr), lambda h: a_row[:, h, :])
                for gr in range(2):
                    pe.wait_ge(*dve_gd.at(("tri", t, 0, gr)))
                    pe.wait_ge(*act_gd.at(("K", t, gr)))
                    four(6 + gr, gr, "triT", (t, gr), lambda h: tri[:, h, :])
                for l in range(1, LEVELS):
                    for gr in range(2):
                        pe.wait_ge(*pool_gd.at(("B", t, l)))
                        pe.wait_ge(*dve_gd.at(("tri", t, l - 1, gr)))
                        if l > 1:
                            pe.wait_ge(*act_gd.at(("X", t, l - 1, gr)))
                        four(gr, gr, "X", (t, l, gr), lambda h: btm[l % 2][:, h, :], lambda h: tri[:, h, :])
                    for gr in range(2):
                        pe.wait_ge(*act_gd.at(("X", t, l, gr)))
                        if l > 1:
                            pe.wait_ge(*dve_gd.at(("triT", t, l - 1, gr)))
                        else:
                            pe.wait_ge(*act_gd.at(("triT", t, gr)))
                        if l < LEVELS - 1:
                            four(2 + gr, gr, "Y", (t, l, gr), lambda h: triT[:, h, :], lambda h: xlev[:, h, :])
                        four(4 + gr, gr, "YT", (t, l, gr), lambda h: xlev[:, h, :], lambda h: triT[:, h, :])
                if t > 0:
                    for gr in range(2):
                        pe.wait_ge(*dve_gd.at(("S", t - 1, gr)))
                        four(6 + gr, gr, "KS", (t, gr), lambda h: kT(h, t), lambda h: state[:, h, :])
                        pe.wait_ge(*act_gd.at(("X", t, LEVELS - 1, gr)))
                        four(gr, gr, "QS", (t, gr), lambda h: qT(h, t), lambda h: state[:, h, :])
                for gr in range(2):
                    pe.wait_ge(*dve_gd.at(("w", t, gr) if t else ("v", t, gr)))
                    pe.wait_ge(*dve_gd.at(("triT", t, LEVELS - 1, gr)))
                    four(2 + gr, gr, "P", (t, gr), lambda h: triT[:, h, :], lambda h: (w_rhs if t else v_w)[:, h, :])
                for gr in range(2):
                    pe.wait_ge(*act_gd.at(("P", t, gr)))
                    four(6 + gr, gr, "O", (t, gr), lambda h: qkd[:, h, 0, :], lambda h: p_out[:, h, :])
                if t < NT - 1:
                    for gr in range(2):
                        pe.wait_ge(*dve_gd.at(("pd", t, gr)))
                        four(4 + gr, gr, "dS", (t, gr), lambda h: k_tok[:, h, :], lambda h: p_dec[:, h, :])

            def qkT(c):
                for h4 in range(4):
                    for t in range(NT):
                        pe.wait_ge(*pool_att.at(("rope", c, t)))
                    if c >= 1:
                        pe.wait_ge(*act_att.at(("qkT", c - 1, h4)))
                    for t in range(NT):
                        mm = pe.transpose(ps[4 + h4][:, t * P:(t + 1) * P], roped[c % 2][:, t, h4 * P:(h4 + 1) * P], ident)
                    mm.then_inc(*pe_att.next(("qkT", c, h4)))

            pe.wait_ge(*dve_gd.at("end"))
            for c in range(6):
                w_landed(pe, 6 + c)
                for t in range(NT):
                    if 1 <= c < 5:
                        pe.wait_ge(*dve_att.at(("rope", c - 1, t)))
                    elif c:
                        pe.wait_ge(*act_att.at(("v", c - 5, t)))
                    for kc in range(KC):
                        mm = pe.matmul(ps[t][:, :], hT[:, kc, t * P:(t + 1) * P], wtile(6 + c)[:, kc, :],
                                       start=kc == 0, stop=kc == KC - 1)
                    mm.then_inc(*pe_proj.next(("da", c, t)))
                if 1 <= c < 5:
                    qkT(c - 1)

            def scores(n):
                h, i = divmod(n, NT)
                for c in range(2):
                    if n >= 2:
                        pe.wait_ge(*act_att.at(("exp", n - 2, c)))
                    else:
                        pe.wait_ge(*act_att.at(("v", 1, 2 * n + c)))
                    r = slice(c * DH, (c + 1) * DH)
                    pe.matmul(ps[2 * (n % 2) + c][:, 0:(i + 1) * P], qaT[r, h, i * P:(i + 1) * P], kaT[r, h, 0:(i + 1) * P],
                              start=True, stop=True).then_inc(*pe_att.next(("sc", n, c)))

            def diff_T(n):
                h, i = divmod(n, NT)
                pe.wait_ge(*dve_att.at(("diff", n)))
                pe.wait_ge(*act_att.at(("wT", n - 2) if n >= 2 else ("qkT", 3, n)))
                for kb in range(i + 1):
                    mm = pe.transpose(ps[4 + n % 2][:, kb * P:(kb + 1) * P], wdiff[n % 2][:, kb * P:(kb + 1) * P], ident)
                mm.then_inc(*pe_att.next(("wT", n)))

            def pv(n):
                h, i = divmod(n, NT)
                pe.wait_ge(*act_att.at(("wT", n)))
                pe.wait_ge(*act_att.at(("out", n - 2) if n >= 2 else ("qkT", 3, 2 + n)))
                for kb in range(i + 1):
                    mm = pe.matmul(ps[6 + n % 2][:, 0:P], wT[n % 2][:, kb * P:(kb + 1) * P], va[:, kb, h * P:(h + 1) * P],
                                   start=kb == 0, stop=kb == i)
                mm.then_inc(*pe_att.next(("pv", n)))

            NS = H * NT
            pe.wait_ge(*act_att.at(("qkT", 3, 3)))
            pe.wait_ge(*act_att.at(("v", 1, NT - 1)))
            for n in range(NS + 2):
                if n < NS:
                    scores(n)
                if 1 <= n <= NS:
                    diff_T(n - 1)
                if n >= 2:
                    pv(n - 2)
            pe_att.marks["end"] = pe_att.count

            pe.wait_ge(*act_att.at("end"))
            k = 0
            for j, name in enumerate(("z", "ga", "gb")):
                for c in range(2):
                    w_landed(pe, 12 + 2 * j + c)
                    for t in range(NT):
                        if k >= 4:
                            pe.wait_ge(*act_mrg.at(("gate", k - 4)))
                        for kc in range(KC):
                            mm = pe.matmul(ps[k % 4][:, :], hT[:, kc, t * P:(t + 1) * P], wtile(12 + 2 * j + c)[:, kc, :],
                                           start=kc == 0, stop=kc == KC - 1)
                        mm.then_inc(*pe_proj.next((name, c, t)))
                        k += 1
            for kc in range(KC):
                if kc >= 4:
                    pe.wait_ge(*act_mrg.at(("mT", kc - 4)))
                for t in range(NT):
                    pe.wait_ge(*pool_mrg.at(("m", kc // 4, t)))
                    mm = pe.transpose(ps[4 + kc % 4][:, t * P:(t + 1) * P], ob[:, t, kc * P:(kc + 1) * P], ident)
                mm.then_inc(*pe_mrg.next(("mT", kc)))
            pe.wait_ge(*act_mrg.at("mT_last"))
            pe.wait_ge(*act_mrg.at(("gate", 6 * NT - 1)))
            for c in range(2):
                w_landed(pe, 18 + c)
                for t in range(NT):
                    if c:
                        pe.wait_ge(*dve_mrg.at(("x1", 0, t)))
                    for kc in range(KC):
                        mm = pe.matmul(ps[t][:, :], mT[:, kc, t * P:(t + 1) * P], wtile(18 + c)[:, kc, :],
                                       start=kc == 0, stop=kc == KC - 1)
                    mm.then_inc(*pe_proj.next(("out", c, t)))

            for kc in range(KC):
                if kc >= 4:
                    pe.wait_ge(*act_rt.at(("h2T", kc - 4)))
                for t in range(NT):
                    pe.wait_ge(*dve_rt.at(("h2", t)))
                    mm = pe.transpose(ps[4 + kc % 4][:, t * P:(t + 1) * P], h2[:, t, kc * P:(kc + 1) * P], ident)
                mm.then_inc(*pe_rt.next(("h2T", kc)))
            pe.wait_ge(*act_rt.at(("h2T", KC - 1)))
            pe.wait_ge(ld_g.sem, 48)
            for t in range(NT):
                for kc in range(KC):
                    mm = pe.matmul(ps[0][:, t * NE:(t + 1) * NE], h2T[:, kc, t * P:(t + 1) * P], rw[:, kc, :],
                                   start=kc == 0, stop=kc == KC - 1)
            mm.then_inc(*pe_rt.next("logits"))
            pe.wait_ge(*dve_rt.at("mask"))
            mask = rt_at("mask").rearrange("p (t e) -> p t e", t=NT)
            for t in range(NT):
                for u in range(t + 1):
                    pe.matmul(ps[1][:, t * NE:(t + 1) * NE], C("before") if u == t else C("ones"), mask[:, u, :],
                              start=u == 0, stop=u == t)
            for u in range(NT):
                mm = pe.matmul(ps[2][:, 0:NE], C("ones"), mask[:, u, :], start=u == 0, stop=u == NT - 1)
            mm.then_inc(*pe_rt.next("rank"))

            def rows_T(b, half):
                for j in range(4):
                    c = 4 * half + j
                    mm = pe.transpose(ps[b][:, j * P:(j + 1) * P], xg[:, c * P:(c + 1) * P], ident)
                mm.then_inc(e_tr.sem, 1)

            pe.wait_ge(*act_rt.at(("h2T", KC - 1)))
            pe.wait_ge(*dve_rt.at("end"))
            pe.wait_ge(x_rows.sem, 16)
            rows_T(7, 0)
            rows_T(6, 1)
            pe.wait_ge(*pool_pre.at("bias"))

            def bias(b, e, col):
                pe.matmul(ps[b][:, :], sel[:, bass.ds(e, 1)].to_broadcast([96, P]), btab[:, col:col + HALF], start=True, stop=False)

            def in_parts(bank, x_hi, x_lo, kc, c, col, stop):
                k, n = slice(kc * P, (kc + 1) * P), slice(col, col + HALF)
                pe.matmul(ps[bank][:, :], x_hi[:, k], w_hi[c % 4][:, n], start=False, stop=False)
                pe.matmul(ps[bank][:, :], x_lo[:, k], w_hi[c % 4][:, n], start=False, stop=False)
                return pe.matmul(ps[bank][:, :], x_hi[:, k], w_lo[c % 4][:, n], start=False, stop=stop)

            def body(i, e):
                def act_T(hf):
                    pe.wait_ge(v_act.sem, 8 * i + 4 * hf + 12)
                    if hf:
                        pe.wait_ge(v_tr.sem, 4 * i + 4)
                    for j in range(4):
                        mm = pe.transpose(ps[6 + hf][:, j * P:(j + 1) * P], av[hf][:, j * P:(j + 1) * P], ident)
                    mm.then_inc(e_tr.sem, 1)

                pe.wait_ge(v_tr.sem, 4 * i + 2)
                for s in range(4):
                    pe.wait_ge(v_act.sem, 8 * i + 4 * (s // 2) + s % 2 + 1)
                    bias(s, e, s % 2 * D + s // 2 * HALF)
                    for c in (2 * s, 2 * s + 1):
                        pe.wait_ge(*small_part(i, c))
                        for j in range(4):
                            mm = in_parts(s, xT_hi, xT_lo, 4 * (c % 2) + j, c, j * HALF, c % 2 == 1 and j == 3)
                        mm.then_inc(e_used.sem, 1)
                        if c == 6:
                            act_T(0)
                pe.wait_ge(x_rows.sem, 16 * i + 32)
                rows_T(7, 0)
                pe.wait_ge(v_y.sem, i + 1)
                pe.wait_ge(a_y.sem, i + 1)
                for nh in range(2):
                    bias(4 + nh, e, 2 * D + nh * HALF)
                pe.wait_ge(v_tr.sem, 4 * i + 3)
                for c in range(8, 12):
                    pe.wait_ge(*small_part(i, c))
                    if c == 9:
                        rows_T(6, 1)
                    if c == 10:
                        pe.wait_ge(v_tr.sem, 4 * i + 6)
                    for j in range(2):
                        for nh in range(2):
                            mm = in_parts(4 + nh, avT_hi, avT_lo, 2 * (c - 8) + j, c, j * D + nh * HALF, c == 11 and j == 1)
                        if c == 9 and j == 0:
                            act_T(1)
                    mm.then_inc(e_used.sem, 1)

            with pe.Fori(0, NE) as i:
                body(i, i)
            n_extra = pe.value_load(be[0:1, 15:16], min_val=0, max_val=EXTRA)
            with pe.If(n_extra > 0):
                with pe.Fori(NE, NBLK) as i:
                    e = pe.value_load(be[0:1, bass.ds(i - NE, 1)], min_val=0, max_val=NE - 1)
                    body(i, e)

        @block.vector
        def _(v):
            v.sem_inc(v_act.sem, 8)
            v.sem_inc(v_y.sem, 1)

            def then(sig, ins, key=None):
                ins.then_inc(*sig.next(key))
                v.wait_ge(*sig.last())

            v.wait_ge(*act_pre.at(("ss", NT - 1)))
            then(dve_pre, v.tensor_scalar(ss, ss, 1.0 / D, EPS, ALU.mult, ALU.add), "var")
            v.wait_ge(*act_pre.at("std"))
            then(dve_pre, v.reciprocal(rstd, rstd))
            for t in range(NT):
                v.tensor_scalar(xn[:, t, :], xs[:, t, :], rstd[:, t:t + 1], None, ALU.mult).then_inc(*dve_pre.next(("xn", t)))
            v.wait_ge(ld_cst.sem, 48)
            for kc in range(1, KC, 2):
                v.wait_ge(*pe_hT.at(kc))
                v.tensor_scalar(hT[:, kc, :], ps[kc][:, :], G("mix_g")[:, kc:kc + 1], None, ALU.mult).then_inc(*dve_pre.next(("hT", kc)))

            for ct in range(3 * H):
                v.wait_ge(*act_conv.at(("raw", ct)))
                if ct >= 2:
                    v.wait_ge(*act_conv.at(("silu", ct - 2)))
                wt = G("conv")[:, 4 * ct:4 * ct + 4]
                src, dst = raw[ct % 2], cacc[ct % 2]
                then(dve_conv, v.tensor_scalar(dst, src[:, 3:3 + SEQ], wt[:, 3:4], None, ALU.mult))
                for j in range(3):
                    then(dve_conv, v.scalar_tensor_tensor(out=dst, in0=src[:, j:j + SEQ], scalar=wt[:, j:j + 1], in1=dst,
                                                          op0=ALU.mult, op1=ALU.add), ct if j == 2 else None)

            def per_head(ap):
                return ap.unsqueeze(1).to_broadcast([P, NT, H])

            for k in range(2):
                q, kk = G("lam")[:, 2 * k * DH:(2 * k + 1) * DH], G("lam")[:, (2 * k + 1) * DH:(2 * k + 2) * DH]
                then(dve_gd, v.tensor_tensor(lamtmp, q, kk, ALU.mult))
                then(dve_gd, v.tensor_reduce((nlam if k else lam2[:, 0:1]), lamtmp, AX.X, ALU.add), ("lam", k))
            v.wait_ge(*pe_proj.at("ba"))
            then(dve_gd, v.tensor_copy(ba, ps[4][:, 0:NT * 2 * H].rearrange("p (t c) -> p t c", t=NT)), "ba")
            then(dve_gd, v.tensor_tensor(spt, ba[:, :, H:2 * H], per_head(G("dt")), ALU.add))
            then(dve_gd, v.scalar_tensor_tensor(out=spe, in0=spt, scalar=-1.0, in1=spt, op0=ALU.mult, op1=ALU.min), "nabs")
            v.wait_ge(*act_gd.at("spe"))
            then(dve_gd, v.tensor_scalar(spe, spe, 1.0, None, ALU.add), "spe1")
            v.wait_ge(*act_gd.at("ln"))
            then(dve_gd, v.scalar_tensor_tensor(out=spt, in0=spt, scalar=0.0, in1=spe, op0=ALU.max, op1=ALU.add))
            then(dve_gd, v.scalar_tensor_tensor(out=gdec, in0=spt, scalar=-1.0, in1=per_head(ealog), op0=ALU.mult, op1=ALU.mult), "g")
            then(dve_gd, v.scalar_tensor_tensor(out=nlam, in0=lam2[:, 1:2], scalar=LAM_INIT, in1=lam2[:, 0:1],
                                                op0=ALU.subtract, op1=ALU.subtract))
            v.wait_ge(*pe_gd.at(("ssq", 2 * H - 1)))
            then(dve_gd, v.tensor_scalar(nrm, ps[6][:, 0:NT * 2 * H].rearrange("p (t c) -> p t c", t=NT), EPS, None, ALU.add))
            then(dve_gd, v.reciprocal(k_s, nrm[:, :, H:2 * H]), "nrm")
            v.wait_ge(*act_gd.at("nrm"))
            then(dve_gd, v.reciprocal(nrm, nrm))
            then(dve_gd, v.tensor_tensor(k_s, k_s, beta, ALU.mult))
            then(dve_gd, v.tensor_tensor(v_s, nrm[:, :, H:2 * H], beta, ALU.mult))
            then(dve_gd, v.tensor_scalar(o_s, nrm[:, :, 0:H], P ** -0.5, None, ALU.mult))
            v.wait_ge(*act_gd.at("dec"))
            then(dve_gd, v.scalar_tensor_tensor(out=k_w, in0=k_s, scalar=-1.0, in1=eg, op0=ALU.mult, op1=ALU.mult))
            then(dve_gd, v.tensor_tensor(o_q, o_s, eg, ALU.mult), "coef")

            def bank4(b):
                return ps[b][:, :].rearrange("p (h n) -> p h n", h=4)

            for t in range(NT):
                if t > 0:
                    v.wait_ge(*pe_gd.at(("D", t - 1, 1)))
                then(dve_gd, v.tensor_tensor(gl, over_heads(C("later"), H), over_cols(gdec[:, t, :], P), ALU.mult), ("gl", t))
                for gr in range(2):
                    hs = slice(4 * gr, 4 * gr + 4)
                    v.wait_ge(*pe_gd.at(("V", t, gr)))
                    then(dve_gd, v.tensor_tensor(v_w[:, hs, :], bank4(6 + gr), over_cols(v_s[:, t, hs], P), ALU.mult), ("v", t, gr))
                for pr in range(4):
                    v.wait_ge(*pe_gd.at(("qk", t, pr)))
                    v.wait_ge(*pool_gd.at(("dT", t, pr // 2)))
                    if t > 0:
                        v.wait_ge(*pe_gd.at(("O", t - 1, 1)))
                    hs = slice(2 * pr, 2 * pr + 2)
                    then(dve_gd, v.tensor_tensor(qkd[:, hs, :, :], ps[2 + pr][:, :].rearrange("p (h c n) -> p h c n", h=2, c=2),
                                                 dT[:, hs, :].unsqueeze(2).to_broadcast([P, 2, 2, P]), ALU.mult), ("qkd", t, pr))
                for gr in range(2):
                    hs = slice(4 * gr, 4 * gr + 4)
                    v.wait_ge(*pe_gd.at(("Yt", t, gr)))
                    if t > 0:
                        v.wait_ge(*pool_gd.at(("o", t - 1, gr)) if t > 1 else dve_gd.last())
                    then(dve_gd, v.tensor_tensor(a_row[:, hs, :], bank4(gr), over_cols(k_s[:, t, hs], P), ALU.mult), ("a", t, gr))
                    then(dve_gd, v.tensor_tensor(tri[:, hs, :], a_row[:, hs, :], over_heads(C("neg_m0"), 4), ALU.mult))
                    then(dve_gd, v.tensor_tensor(tri[:, hs, :], tri[:, hs, :], over_heads(ident, 4), ALU.add), ("tri", t, 0, gr))
                for l in range(1, LEVELS):
                    for gr in range(2):
                        hs = slice(4 * gr, 4 * gr + 4)
                        if l < LEVELS - 1:
                            v.wait_ge(*pe_gd.at(("Y", t, l, gr)))
                            then(dve_gd, v.tensor_tensor(tri[:, hs, :], tri[:, hs, :], bank4(2 + gr), ALU.subtract), ("tri", t, l, gr))
                        v.wait_ge(*pe_gd.at(("YT", t, l, gr)))
                        then(dve_gd, v.tensor_tensor(triT[:, hs, :], triT[:, hs, :], bank4(4 + gr), ALU.subtract), ("triT", t, l, gr))
                if t > 0:
                    for gr in range(2):
                        hs = slice(4 * gr, 4 * gr + 4)
                        v.wait_ge(*pe_gd.at(("KS", t, gr)))
                        for h in range(4 * gr, 4 * gr + 4):
                            ins = v.scalar_tensor_tensor(out=w_rhs[:, h, :], in0=ps[6 + gr][:, (h % 4) * P:(h % 4 + 1) * P],
                                                         scalar=k_w[:, t, h:h + 1], in1=v_w[:, h, :], op0=ALU.mult, op1=ALU.add)
                        then(dve_gd, ins, ("w", t, gr))
                        v.wait_ge(*pe_gd.at(("QS", t, gr)))
                        if t > 1:
                            v.wait_ge(*pool_gd.at(("o", t - 1, gr)))
                        then(dve_gd, v.tensor_tensor(qs_s[:, hs, :], bank4(gr), over_cols(o_q[:, t, hs], P), ALU.mult), ("qs", t, gr))
                for gr in range(2):
                    hs = slice(4 * gr, 4 * gr + 4)
                    v.wait_ge(*act_gd.at(("P", t, gr)))
                    if t > 0:
                        v.wait_ge(*pe_gd.at(("dS", t - 1, 1)))
                    then(dve_gd, v.tensor_tensor(p_dec[:, hs, :], p_out[:, hs, :], over_cols(ed[:, t, hs], P), ALU.mult), ("pd", t, gr))
                for gr in range(2):
                    hs = slice(4 * gr, 4 * gr + 4)
                    v.wait_ge(*pe_gd.at(("O", t, gr)))
                    out = ob[:, t, gr * HALF:(gr + 1) * HALF].rearrange("p (h n) -> p h n", h=4)
                    then(dve_gd, v.tensor_tensor(out, bank4(6 + gr), over_cols(o_s[:, t, hs], P), ALU.mult), ("o", t, gr))
                if t < NT - 1:
                    for gr in range(2):
                        hs = slice(4 * gr, 4 * gr + 4)
                        v.wait_ge(*pe_gd.at(("dS", t, gr)))
                        if t == 0:
                            then(dve_gd, v.tensor_copy(state[:, hs, :], bank4(4 + gr)), ("S", t, gr))
                        else:
                            for h in range(4 * gr, 4 * gr + 4):
                                ins = v.scalar_tensor_tensor(out=state[:, h, :], in0=state[:, h, :], scalar=glast[:, t, h:h + 1],
                                                             in1=ps[4 + gr][:, (h % 4) * P:(h % 4 + 1) * P], op0=ALU.mult, op1=ALU.add)
                            then(dve_gd, ins, ("S", t, gr))
            dve_gd.marks["end"] = dve_gd.count

            v.wait_ge(*pool_gd.at("end"))
            cos = C("cos").rearrange("p (t j) -> p t j", t=NT)
            sin = C("sin").rearrange("p (t b j) -> p t b j", t=NT, b=2)
            for c in range(4):
                for t in range(NT):
                    k = c * NT + t
                    v.wait_ge(*pe_proj.at(("da", c, t)))
                    if k >= 2:
                        v.wait_ge(*pool_att.at(("rope", (k - 2) // NT, (k - 2) % NT)))
                    x4 = ps[t][:, :].rearrange("p (g b j) -> p g b j", b=2, j=32)
                    r1, r2 = (r[k % 2].rearrange("p (g b j) -> p g b j", b=2, j=32) for r in (rope1, rope2))
                    v.tensor_tensor(r1, x4, cos[:, t, :].unsqueeze(1).unsqueeze(1).to_broadcast([P, 8, 2, 32]), ALU.mult).then_inc(*dve_att.next())
                    for b in range(2):
                        ins = v.tensor_tensor(r2[:, :, b, :], x4[:, :, 1 - b, :], sin[:, t, b, :].unsqueeze(1).to_broadcast([P, 8, 32]), ALU.mult)
                        ins.then_inc(*dve_att.next(("rope", c, t) if b else None))

            def diff(n):
                i, k = n % NT, 2 * (n % 2)
                v.wait_ge(*act_att.at(("exp", n, 1)))
                if n >= 2:
                    v.wait_ge(*act_att.at(("out", n - 2)))
                    v.wait_ge(*pe_att.at(("wT", n - 2)))
                then(dve_att, v.reciprocal(recs[:, k:k + 2], esum[:, k:k + 2]))
                rr = ratio[:, n % 2:n % 2 + 1]
                then(dve_att, v.scalar_tensor_tensor(out=rr, in0=esum[:, k:k + 1], scalar=recs[:, k + 1:k + 2], in1=nlam,
                                                     op0=ALU.mult, op1=ALU.mult))
                cols = slice(0, (i + 1) * P)
                then(dve_att, v.scalar_tensor_tensor(out=wdiff[n % 2][:, cols], in0=probs[n % 2][1][:, cols], scalar=rr,
                                                     in1=probs[n % 2][0][:, cols], op0=ALU.mult, op1=ALU.add), ("diff", n))

            NS = H * NT
            v.wait_ge(*pe_att.at(("qkT", 3, 3)))
            v.wait_ge(*pool_att.at("end"))
            for n in range(NS):
                i = n % NT
                for c in range(2):
                    k = 2 * (n % 2) + c
                    v.wait_ge(*pe_att.at(("sc", n, c)))
                    diag = ps[k][:, i * P:(i + 1) * P]
                    then(dve_att, v.tensor_tensor(diag, diag, causal, ALU.add))
                    then(dve_att, v.tensor_reduce(mx[:, k:k + 1], ps[k][:, 0:(i + 1) * P], AX.X, ALU.max))
                    then(dve_att, v.tensor_scalar(nmx[:, k:k + 1], mx[:, k:k + 1], -DH ** -0.5, None, ALU.mult), ("max", n, c))
                if n >= 1:
                    diff(n - 1)
            diff(NS - 1)
            dve_att.marks["end"] = dve_att.count

            for k in range(2 * NT):
                v.wait_ge(*pool_mrg.at(("sq", k)))
                then(dve_mrg, v.tensor_reduce(osq[:, k * H:(k + 1) * H], sqm[k % 2].rearrange("p (h n) -> p h n", h=H), AX.X, ALU.add), ("osq", k))
            then(dve_mrg, v.tensor_scalar(osq, osq, 1.0 / P, EPS, ALU.mult, ALU.add), "ovar")
            v.wait_ge(*act_mrg.at("ostd"))
            then(dve_mrg, v.reciprocal(osq, osq))
            for k in range(2 * NT):
                o = heads((oa if k < NT else ob)[:, k % NT, :])
                then(dve_mrg, v.tensor_tensor(o, o, over_cols(osq[:, k * H:(k + 1) * H], P), ALU.mult))
                gain, scale = (G("subln"), 1.0 - LAM_INIT) if k < NT else (G("gd_g"), 1.0)
                then(dve_mrg, v.scalar_tensor_tensor(out=o, in0=o, scalar=scale, in1=over_heads(gain, H), op0=ALU.mult, op1=ALU.mult))
            k = 0
            for j in range(3):
                for c in range(2):
                    for t in range(NT):
                        v.wait_ge(*act_mrg.at(("gate", k)))
                        o = (oa if j == 1 else ob)[:, t, c * HALF:(c + 1) * HALF]
                        then(dve_mrg, v.tensor_tensor(o, o, gate_s[k % 2], ALU.mult), ("gate", k))
                        if j == 2:
                            dve_mrg.marks[("gb", c, t)] = dve_mrg.count
                        k += 1
            v.wait_ge(ld_x2.sem, 16)
            for c in range(2):
                for t in range(NT):
                    v.wait_ge(*pe_proj.at(("out", c, t)))
                    xc = xs[:, t, c * HALF:(c + 1) * HALF]
                    v.tensor_tensor(xc, xc, ps[t][:, :], ALU.add).then_inc(*dve_mrg.next(("x1", c, t)))

            v.wait_ge(*act_rt.at(("ss", NT - 1)))
            then(dve_rt, v.tensor_scalar(ss, ss, 1.0 / D, EPS, ALU.mult, ALU.add), "var")
            v.wait_ge(*act_rt.at("std"))
            then(dve_rt, v.reciprocal(rstd, rstd))
            v.wait_ge(ld_g.sem, 48)
            for t in range(NT):
                v.scalar_tensor_tensor(out=h2[:, t, :], in0=xs[:, t, :], scalar=rstd[:, t:t + 1], in1=g2,
                                       op0=ALU.mult, op1=ALU.mult).then_inc(*dve_rt.next(("h2", t)))
            lg = rt_at("lg").rearrange("p (t e) -> p t e", t=NT)
            top = rt_at("top").rearrange("p (t k) -> p t k", t=NT)
            tix = rt_at("tix").bitcast(U32).rearrange("p (t k) -> p t k", t=NT)
            gw3 = gw.rearrange("p (t k) -> p t k", t=NT)
            v.wait_ge(*pe_rt.at("logits"))
            then(dve_rt, v.tensor_tensor(lg, ps[0][:, 0:NT * NE].rearrange("p (t e) -> p t e", t=NT),
                                         G("router_b").unsqueeze(1).to_broadcast([P, NT, NE]), ALU.add))
            for t in range(NT):
                then(dve_rt, v.max(top[:, t, :], lg[:, t, :]))
                then(dve_rt, v.max_index(tix[:, t, :], top[:, t, :], lg[:, t, :]))
            then(dve_rt, v.tensor_tensor(gw3, top[:, :, 0:TOPK], top[:, :, 0:1].to_broadcast([P, NT, TOPK]), ALU.subtract), "gsub")
            tixf, hot = rt_at("tixf"), rt_at("hot").rearrange("p (a e) -> p a e", e=NE)
            then(dve_rt, v.tensor_copy(tixf.rearrange("p (t k) -> p t k", t=NT), tix[:, :, 0:TOPK]))
            then(dve_rt, v.tensor_tensor(hot, C("iota").unsqueeze(1).to_broadcast([P, NT * TOPK, NE]), over_cols(tixf, NE), ALU.is_equal))
            mask = rt_at("mask").rearrange("p (t e) -> p t e", t=NT)
            then(dve_rt, v.tensor_reduce(mask, rt_at("hot").rearrange("p (t k e) -> p t e k", t=NT, k=TOPK), AX.X, ALU.add), "mask")
            gsum = rt_at("gsum")
            v.wait_ge(*act_rt.at("gexp"))
            then(dve_rt, v.tensor_reduce(gsum, gw3, AX.X, ALU.add))
            then(dve_rt, v.reciprocal(gsum, gsum))
            then(dve_rt, v.tensor_tensor(gw3, gw3, over_cols(gsum, TOPK), ALU.mult))
            cnt, xb, inc, shift = rt_at("cnt"), rt_at("xb"), rt_at("inc"), rt_at("shift")
            v.wait_ge(*pe_rt.at("rank"))
            then(dve_rt, v.tensor_copy(cnt, ps[2][:, 0:NE]))
            then(dve_rt, v.tensor_scalar(xb, cnt, float(P), None, ALU.is_gt))
            for m in range(2, NT):
                then(dve_rt, v.scalar_tensor_tensor(out=xb, in0=cnt, scalar=float(m * P), in1=xb, op0=ALU.is_gt, op1=ALU.add))
            then(dve_rt, v.tensor_tensor_scan(inc, C("ones")[:, 0:NE], xb, 0.0, ALU.mult, ALU.add))
            then(dve_rt, v.tensor_tensor(shift, inc, xb, ALU.subtract))
            then(dve_rt, v.scalar_tensor_tensor(out=shift, in0=shift, scalar=float(P), in1=C("base"), op0=ALU.mult, op1=ALU.subtract))
            then(dve_rt, v.tensor_scalar(shift, shift, float(P * (NE - 1)), None, ALU.add))
            big = rt_at("big").rearrange("p (b e) -> p b e", e=NE)
            then(dve_rt, v.tensor_tensor(big, over_cols(C("iota")[:, 0:16], NE), inc.unsqueeze(1).to_broadcast([P, 16, NE]), ALU.is_ge))
            bef = rt_at("bef")
            then(dve_rt, v.tensor_reduce(bef, big, AX.X, ALU.add))
            then(dve_rt, v.tensor_scalar(bef, bef, float(NE - 1), None, ALU.min))
            then(dve_rt, v.tensor_copy(bef[:, 15:16], inc[:, NE - 1:NE]))
            then(dve_rt, v.tensor_copy(be, bef), "be")
            rank, dest = rt_at("rank").rearrange("p (t e) -> p t e", t=NT), rt_at("dest").rearrange("p (t e) -> p t e", t=NT)
            then(dve_rt, v.tensor_copy(rank, ps[1][:, 0:NT * NE].rearrange("p (t e) -> p t e", t=NT)))
            then(dve_rt, v.scalar_tensor_tensor(out=dest, in0=rank, scalar=float(P), in1=shift.unsqueeze(1).to_broadcast([P, NT, NE]),
                                                op0=ALU.is_ge, op1=ALU.mult))
            then(dve_rt, v.tensor_tensor(dest, dest, rank, ALU.add))
            then(dve_rt, v.tensor_tensor(dest, dest, C("base").unsqueeze(1).to_broadcast([P, NT, NE]), ALU.add))
            hot4, dk = rt_at("hot").rearrange("p (t k e) -> p t k e", t=NT, k=TOPK), rt_at("dk")
            then(dve_rt, v.tensor_tensor(hot4, hot4, dest.unsqueeze(2).to_broadcast([P, NT, TOPK, NE]), ALU.mult))
            then(dve_rt, v.tensor_reduce(dk, hot, AX.X, ALU.add))
            then(dve_rt, v.tensor_copy(y_idx, dk))
            blk, blkf = rt_at("blk").bitcast(I32), rt_at("blkf")
            then(dve_rt, v.tensor_scalar(blk, y_idx, 7, None, ALU.logical_shift_right))
            then(dve_rt, v.tensor_copy(blkf, blk))
            then(dve_rt, v.tensor_scalar(blkf, blkf, float(-(P * RT_W - 1)), None, ALU.mult))
            then(dve_rt, v.scalar_tensor_tensor(out=blkf, in0=dk, scalar=float(RT_W), in1=blkf, op0=ALU.mult, op1=ALU.add))
            then(dve_rt, v.tensor_copy(rt_at("scat").bitcast(I32), blkf), "dest")
            dve_rt.marks["end"] = dve_rt.count

            def to_lo(dst, hi, k, bank, value):
                v.wait_ge(a_tr.sem, value)
                cols = slice(k * HALF, (k + 1) * HALF)
                v.tensor_tensor(dst[:, cols], ps[bank][:, :], hi[:, cols], ALU.subtract).then_inc(v_tr.sem, 1)

            for half in range(2):
                to_lo(xT_lo, xT_hi, half, 7 - half, half + 1)

            def w_parts(i, chunks):
                for c in chunks:
                    if c in ON_POOL:
                        continue
                    v.wait_ge(a_hi.sem, 12 * i + c + 1)
                    v.tensor_tensor(w_lo[c % 4][:, :], raw_chunk(c), w_hi[c % 4][:, :], ALU.subtract).then_inc(v_lo.sem, 1)

            def swiglu(i, hf):
                n = 8 * i + 4 * hf + 8
                v.wait_ge(e_used.sem, 12 * i + 4 * hf + 6)
                v.wait_ge(v_act.sem, n)
                v.tensor_scalar(gm[hf], ps[2 * hf][:, :], LIMIT, None, ALU.min).then_inc(v_act.sem, 1)
                v.wait_ge(e_used.sem, 12 * i + 4 * hf + 8)
                v.tensor_scalar(um[hf], ps[2 * hf + 1][:, :], LIMIT, -LIMIT, ALU.min, ALU.max).then_inc(v_act.sem, 1)
                v.wait_ge(v_act.sem, n + 2)
                v.scalar_tensor_tensor(out=um[hf], in0=um[hf], scalar=1.0, in1=gm[hf], op0=ALU.add, op1=ALU.mult).then_inc(v_act.sem, 1)
                v.wait_ge(v_act.sem, n + 3)
                v.wait_ge(a_sig.sem, 2 * i + hf + 1)
                v.wait_ge(e_tr.sem, 4 * i + 2)
                v.tensor_tensor(av[hf], um[hf], sg[hf], ALU.mult).then_inc(v_act.sem, 1)

            def result(i):
                v.wait_ge(e_used.sem, 12 * i + 16)
                v.wait_ge(st_y.sem, 16 * i + 16)
                v.tensor_copy(ys[:, 0:HALF], ps[4][:, :]).then_inc(v_y.sem, 1)

            def body(i, before=False):
                w_parts(i, range(0, 3))
                if before:
                    result(i - 1)
                w_parts(i, range(3, 8))
                swiglu(i, 0)
                w_parts(i, range(8, 10))
                to_lo(avT_lo, avT_hi, 0, 6, 4 * i + 3)
                w_parts(i, range(10, 11))
                swiglu(i, 1)
                to_lo(xT_lo, xT_hi, 0, 7, 4 * i + 4)
                to_lo(xT_lo, xT_hi, 1, 6, 4 * i + 5)
                w_parts(i, range(11, 12))
                to_lo(avT_lo, avT_hi, 1, 7, 4 * i + 6)

            body(0)
            with v.Fori(1, NE) as i:
                body(i, True)
            result(NE - 1)
            n_extra = v.value_load(be[0:1, 15:16], min_val=0, max_val=EXTRA)
            with v.If(n_extra > 0):
                with v.Fori(NE, NBLK) as i:
                    body(i)
                    result(i)

            for t in range(NT):
                for k in range(TOPK):
                    n = t * TOPK + k
                    v.wait_ge(ld_row[n % 6].sem, 16 * (n // 6 + 1))
                    then(dve_fin, v.scalar_tensor_tensor(out=xs[:, t, :], in0=ring[:, n % 6, 0:D], scalar=gw[:, n:n + 1], in1=xs[:, t, :],
                                                         op0=ALU.mult, op1=ALU.add), ("row", n))
                dve_fin.marks[("sum", t)] = dve_fin.count
                v.wait_ge(*act_fin.at(("ss", t)))
                then(dve_fin, v.tensor_scalar(ss[:, t:t + 1], ss[:, t:t + 1], 1.0 / D, EPS, ALU.mult, ALU.add), ("var", t))
                v.wait_ge(*act_fin.at(("std", t)))
                then(dve_fin, v.reciprocal(rstd[:, t:t + 1], rstd[:, t:t + 1]))
                v.scalar_tensor_tensor(out=xs[:, t, :], in0=xs[:, t, :], scalar=rstd[:, t:t + 1], in1=gf,
                                       op0=ALU.mult, op1=ALU.mult).then_inc(*dve_fin.next(("out", t)))

    return {name: s.marks for name, s in signals.items()}


def constants():
    i = np.arange(P)
    c = np.zeros((P, NCST), np.float32)

    def put(name, a):
        lo, hi = CST[name]
        c[:, lo:hi] = np.asarray(a, np.float32).reshape(P, hi - lo)

    put("ident", np.eye(P))
    put("upper", i[:, None] <= i[None, :])
    put("later", i[:, None] > i[None, :])
    put("before", i[:, None] < i[None, :])
    put("ones", np.ones((P, P)))

    def between(l, row, col):
        return (row >> (l + 1) == col >> (l + 1)) & ((row >> l) & 1 == 1) & ((col >> l) & 1 == 0)

    put("neg_m0", np.where(between(0, i[:, None], i[None, :]), -1.0, 0.0))
    put("masks", np.concatenate([between(l, i[None, :], i[:, None]) for l in range(1, LEVELS)], axis=1))
    put("causal", np.where(i[None, :] <= i[:, None], 0.0, NEG))
    inv = (1.0 / (np.float32(10000.0) ** (np.arange(0, DH, 2, dtype=np.float32) / np.float32(DH)))).astype(np.float32)
    ang = np.arange(SEQ, dtype=np.float32)[:, None] * inv[None, :]
    cos, sin = np.cos(ang), np.sin(ang)
    put("cos", cos.reshape(NT, P, 32).transpose(1, 0, 2))
    put("sin", np.stack([-sin, sin], axis=1).reshape(NT, P, 2, 32).transpose(1, 0, 2, 3))
    put("iota", np.broadcast_to(np.arange(NE), (P, NE)))
    put("base", np.broadcast_to(P * np.arange(NE), (P, NE)))
    put("onehot", i[:, None] % NE == np.arange(NE)[None, :])
    tok = np.repeat(np.arange(NT)[None, :] * P + i[:, None], TOPK, axis=1).astype(np.int32)
    return c, tok


_IO = dict(w_in="w_in", w_out="w_out", router_w="router_w", b_gate="exp_b_gate", b_up="exp_b_up", b_down="exp_b_down",
           w_gate="exp_w_gate", w_up="exp_w_up", w_down="exp_w_down")


def kernel(**inputs):
    import concourse.bacc as bacc
    from concourse.bass_utils import run_bass_kernel_spmd

    x = {k: np.asarray(v) for k, v in inputs.items()}

    def rows(a):
        return np.broadcast_to(a.reshape(1, -1), (P, a.size))

    cst, tok = constants()
    conv = x["gd_conv_w"][0].reshape(4, 24, P).transpose(2, 1, 0).reshape(P, 96)
    par = np.concatenate([x["mix_norm_g"].reshape(KC, P).T, conv, rows(x["gd_a_log"]), rows(x["gd_dt_bias"]), rows(x["router_b"]),
                          rows(x["da_lambda_q1"]), rows(x["da_lambda_k1"]), rows(x["da_lambda_q2"]), rows(x["da_lambda_k2"]),
                          rows(x["da_subln_g"]), rows(x["gd_norm_g"])], axis=1)
    arrays = {"x": x["x"].reshape(SEQ, D), "cst": cst, "par": np.ascontiguousarray(par), "tokid": tok,
              "ffn_g": x["ffn_norm_g"].reshape(1, D), "final_g": x["final_norm_g"].reshape(1, D)}
    for name, source in _IO.items():
        arrays[name] = x[source][0]

    def build(known):
        nc = bacc.Bacc("TRN2", target_bir_lowering=False, num_devices=1)
        io = {name: nc.dram_tensor(f"in_{name}", a.shape, mybir.dt.from_np(a.dtype), kind="ExternalInput").ap()
              for name, a in arrays.items()}
        io["out"] = nc.dram_tensor("out_rows", (SEQ, D), F32, kind="ExternalOutput").ap()
        return nc, layer_kernel(nc, io, known)

    _, counts = build({})
    nc, _ = build(counts)
    got = run_bass_kernel_spmd(nc, [{f"in_{n}": a for n, a in arrays.items()}], core_ids=[0])
    return got.results[0]["out_rows"].reshape(x["x"].shape)
```

```python
import math
from contextlib import ExitStack

import numpy as np

import concourse.bass as bass
from concourse import mybir

F32 = mybir.dt.float32
F32R = mybir.dt.float32r
BF16 = mybir.dt.bfloat16
I32 = mybir.dt.int32
U32 = mybir.dt.uint32
ALU = mybir.AluOpType
ACT = mybir.ActivationFunctionType
AX = mybir.AxisListType

P = 128
D = 1024
SEQ = 512
NT = SEQ // P
KC = D // P
HALF = 512
QUART = HALF // 2
CT_BA = 3
CT_NORM = 19
H = 8
DH = 64
NE, TOPK = 32, 4
LEVELS = 7
EXTRA = SEQ * TOPK // (P + 1)
NBLK = NE + EXTRA
RT_W = NBLK + 1
EPS = 1e-6
LAM_INIT = 0.8 - 0.6 * math.exp(0.0)
NEG = -1e30
LIMIT, ALPHA = 7.0, 1.702

C_DAQ, C_DAK, C_DAV, C_GDQ = 0, D, 2 * D, 3 * D
C_Z, C_BA, C_GA, C_GB = 6 * D, 7 * D, 7 * D + 2 * H, 8 * D + 2 * H
IN_DIM = 9 * D + 2 * H

_widths = dict(ident=P, upper=P, later=P, before=P, ones=P, neg_m0=P, masks=(LEVELS - 1) * P, causal=P,
               cos=NT * 32, sin=NT * DH, iota=NE, base=NE, onehot=NE)
CST, _at = {}, 0
for _k, _w in _widths.items():
    CST[_k] = (_at, _at + _w)
    _at += _w
NCST = _at
_widths = dict(mix_g=KC, conv=24 * 4, a_log=H, dt=H, router_b=NE, lam=4 * DH, subln=P, gd_g=P)
PAR, _at = {}, 0
for _k, _w in _widths.items():
    PAR[_k] = (_at, _at + _w)
    _at += _w
NPAR = _at


class Signal:

    def __init__(self, sem, known):
        self.sem, self.known, self.count, self.marks = sem, known, 0, {}

    def next(self, key=None, by=1):
        self.count += by
        self.marks[key] = self.count
        return self.sem, by

    def at(self, key):
        return self.sem, self.known.get(key, 1)

    def last(self):
        return self.sem, self.count


def layer_kernel(nc, io, known):
    signals = {}
    with ExitStack() as ctx:
        def sb(name, shape, dt=F32):
            return ctx.enter_context(nc.sbuf_tensor(name, shape, dt))

        def signal(name):
            s = Signal(ctx.enter_context(nc.semaphore(name)), known.get(name, {}))
            signals[name] = s
            return s

        h2_dram = nc.dram_tensor("h2_rows", [SEQ, D], F32, kind="Internal").ap()
        rowtok_dram = nc.dram_tensor("row_token", [P * RT_W, 1], I32, kind="Internal").ap()
        y_dram = nc.dram_tensor("expert_rows", [NBLK * P, D], F32, kind="Internal").ap()

        cst = sb("cst", [P, NCST])
        par = sb("par", [P, NPAR])
        tokid = sb("tokid", [P, NT * TOPK], I32)
        arena_at = -(-nc.sbuf_base // 32) * 32
        arena = sb("arena", [P, 46 * 1024])

        def place(name, word, shape, dt=F32):
            return nc.alloc_sbuf_tensor_at(name, shape, dt, offset=arena_at + 4 * word)

        K = 1024
        ring = place("ring", 0, [P, 6, 2 * K])
        ob = place("ob", 20 * K, [P, NT, D])
        x0 = place("x0", 20 * K, [P, NT, D])
        xs = place("xs", 40 * K, [P, NT, D])
        hT_hi = place("hT_hi", 12 * K, [P, KC, SEQ], F32R)
        hT_lo = place("hT_lo", 16 * K, [P, KC, SEQ], F32R)
        mT_hi, mT_lo = hT_hi, hT_lo
        h2T = place("h2T", 24 * K, [P, KC, SEQ])
        scratch = place("scratch", 28 * K, [P, 18 * K])
        raw_w = [place(f"raw_w{r}", w * K, [P, 2 * K]) for r, w in enumerate((24, 26, 44))]
        wba_hi = place("wba_hi", 44 * K - 256, [P, KC, 2 * H], F32R)
        wba_lo = place("wba_lo", 44 * K - 128, [P, KC, 2 * H], F32R)
        CHUNK = 2048
        w_hi = [place(f"w_hi{i}", w * K, [P, CHUNK], F32R) for i, w in enumerate((28, 32, 12, 16))]
        w_lo = [place(f"w_lo{i}", w * K, [P, CHUNK], F32R) for i, w in enumerate((30, 34, 14, 18))]
        xT_hi, xT_lo, avT_hi, avT_lo = (place(n, w * K, [P, D], F32R) for n, w in (
            ("xT_hi", 45), ("xT_lo", 20), ("avT_hi", 21), ("avT_lo", 22)))
        btab = sb("btab", [96, 3 * D], BF16)
        sel = sb("sel", [96, NE], BF16)
        wba = sb("wba", [P, KC, 2 * H])
        gate_s = [sb(f"gate{k}", [P, QUART]) for k in range(2)]
        small = sb("small", [P, 1024])

        def C(name):
            a, b = CST[name]
            return cst[:, a:b]

        def G(name):
            a, b = PAR[name]
            return par[:, a:b]

        small_at = [0]

        def sm(width):
            a = small_at[0]
            small_at[0] += width
            assert small_at[0] <= 1024
            return small[:, a:a + width]

        ident = C("ident")
        causal = C("causal")

        def over_heads(ap, n):
            return ap.unsqueeze(1).to_broadcast([P, n, ap.shape[1]])

        def over_cols(ap, n):
            return ap.unsqueeze(2).to_broadcast([P, ap.shape[1], n])

        q_place = ring[:, :, :].rearrange("p s n -> p (s n)")
        qkvT = q_place.rearrange("p (c t) -> p c t", c=24)
        xn = q_place[:, 0:4 * K].rearrange("p (t c) -> p t c", t=NT)
        qaT = q_place[:, 0:4 * K].rearrange("p (h t) -> p h t", h=H)
        kaT = q_place[:, 4 * K:8 * K].rearrange("p (h t) -> p h t", h=H)
        va = q_place[:, 8 * K:12 * K].rearrange("p (t c) -> p t c", t=NT)
        h2 = ob[:, :, :]

        def at_k(k, n=K):
            a = round((k - 28) * K)
            return scratch[:, a:a + n]

        def heads(ap):
            return ap.rearrange("p (h n) -> p h n", h=H)

        gdn = [scratch[:, k * K:(k + 1) * K] for k in range(18)]
        k_tok, v_w, aT, tri, triT, xlev, gl, dT = (heads(gdn[k]) for k in range(8))
        btm = [heads(gdn[8]), heads(gdn[9])]
        state, w_rhs, p_out, p_dec = (heads(gdn[k]) for k in range(10, 14))
        qs_s, a_row = heads(gdn[14]), heads(gdn[15])
        qkd = scratch[:, 16 * K:18 * K].rearrange("p (h c n) -> p h c n", h=H, c=2)
        raw = [scratch[:, 8 * K + k * 520:8 * K + k * 520 + SEQ + 3] for k in range(2)]
        cacc = [scratch[:, 8 * K + 1040 + k * SEQ:8 * K + 1040 + (k + 1) * SEQ] for k in range(2)]
        sqb = [scratch[:, 8 * K + 2064 + k * SEQ:8 * K + 2064 + (k + 1) * SEQ] for k in range(2)]
        bias_st = [at_k(39.25 + j)[0:96, :] for j in range(3)]
        bias_hi, bias_mid, bias_lo = (at_k(42.25 + j / 2, K // 2)[0:96, :].bitcast(BF16) for j in range(3))
        baT = at_k(42.25, HALF)[0:2 * H, :]
        rope1 = [at_k(38 + k / 2, HALF) for k in range(2)]
        rope2 = [at_k(39 + k / 2, HALF) for k in range(2)]
        roped = [at_k(40 + 2 * k, 2 * K).rearrange("p (t c) -> p t c", t=NT) for k in range(2)]
        probs = [[at_k(36 + k + c / 2, HALF) for c in range(2)] for k in range(2)]
        wdiff = [at_k(38 + k / 2, HALF) for k in range(2)]
        wT = [at_k(39 + k / 2, HALF) for k in range(2)]
        sqm = [at_k(36 + k) for k in range(2)]
        ga = at_k(40, 4 * K).rearrange("p (t c) -> p t c", t=NT)
        gf, g2, junk = at_k(36), at_k(37), at_k(39)
        rw = at_k(38, KC * NE).rearrange("p (c e) -> p c e", c=KC)
        rt = place("rt", 12 * K, [P, 4 * K])
        rt_cols, n = {}, 0
        for name, w in dict(scat=16, lg=128, top=32, tix=32, tixf=16, hot=512, mask=128, gsum=4, cnt=32, xb=32, inc=32, shift=32,
                            big=512, bef=16, rank=128, dest=128, dk=16, blk=16, blkf=16).items():
            rt_cols[name] = (n, n + w)
            n += w
        assert n <= 4 * K

        def rt_at(name):
            lo, hi = rt_cols[name]
            return rt[:, lo:hi]

        xg = at_k(44)
        gm, sg, um, av = ([raw_ap[:, k * HALF:(k + 1) * HALF] for k in range(2)] for raw_ap in
                          (place(n, w * K, [P, D]) for n, w in (("gm", 24), ("sg", 25), ("um", 26), ("av", 27))))
        ys = place("ys", 23 * K, [P, D])

        banks = ctx.enter_context(nc.psum_tensor("banks", [P, 8, HALF], F32))
        ps = [banks[:, b, :] for b in range(8)]

        ss, rstd = sm(NT), sm(NT)
        ba = sm(NT * 2 * H).rearrange("p (t c) -> p t c", t=NT)
        beta, gdec, spt, spe = (sm(NT * H).rearrange("p (t h) -> p t h", t=NT) for _ in range(4))
        ealog = sm(H)
        dec = sm(3 * NT * H)
        eg, ed, glast = (dec[:, k * NT * H:(k + 1) * NT * H].rearrange("p (t h) -> p t h", t=NT) for k in range(3))
        nrm = sm(NT * 2 * H).rearrange("p (t c) -> p t c", t=NT)
        k_s, v_s, k_w, o_q, o_s = (sm(NT * H).rearrange("p (t h) -> p t h", t=NT) for _ in range(5))
        lam2, nlam = sm(2), sm(1)
        mx, nmx, esum, recs, ratio = sm(4), sm(4), sm(4), sm(4), sm(2)
        osq, oasq = sm(NT * H), sm(NT * H)
        e_idx = sm(RT_W).bitcast(I32)
        e_idx1 = sm(1).bitcast(I32)
        e_held = sm(1).bitcast(I32)
        y_idx = sm(NT * TOPK).bitcast(I32)
        gw = sm(NT * TOPK)
        be = sm(16).bitcast(I32)
        lamtmp = sm(DH)

        ld_cst, ld_x, ld_ba, ld_bias, ld_rt, ld_x2, ld_g = (signal(n) for n in (
            "ld_cst", "ld_x", "ld_ba", "ld_bias", "ld_rt", "ld_x2", "ld_g"))
        ld_w = [signal(f"ld_w{s}") for s in range(3)]
        w_hi_done, w_lo_done = signal("w_hi_done"), signal("w_lo_done")
        pe_hT, pe_proj, pe_gd, pe_att, pe_mrg, pe_rt = (signal(n) for n in (
            "pe_hT", "pe_proj", "pe_gd", "pe_att", "pe_mrg", "pe_rt"))
        act_pre, act_conv, act_gd, act_att, act_mrg, act_rt = (signal(n) for n in (
            "act_pre", "act_conv", "act_gd", "act_att", "act_mrg", "act_rt"))
        dve_pre, dve_conv, dve_gd, dve_att, dve_mrg, dve_rt, dve_fin = (signal(n) for n in (
            "dve_pre", "dve_conv", "dve_gd", "dve_att", "dve_mrg", "dve_rt", "dve_fin"))
        pool_pre, pool_gd, pool_att, pool_mrg = (signal(n) for n in ("pool_pre", "pool_gd", "pool_att", "pool_mrg"))
        st_h2, st_rt, st_y, st_out, act_fin = (signal(n) for n in ("st_h2", "st_rt", "st_y", "st_out", "act_fin"))
        ld_row = [signal(f"ld_row{s}") for s in range(6)]
        x_rows, x_idx = signal("x_rows"), signal("x_idx")
        e_tr = signal("e_tr")
        ld_e = [signal(f"ld_e{r}") for r in range(6)]
        e_used, a_hi, v_lo, p_lo = signal("e_used"), signal("a_hi"), signal("v_lo"), signal("p_lo")
        v_act, v_y, v_tr = signal("v_act"), signal("v_y"), signal("v_tr")
        a_sig, a_tr, a_y = signal("a_sig"), signal("a_tr"), signal("a_y")

        columns = [("w_in", c0 + QUART * j) for c0, n in ((C_GDQ, 12), (C_DAQ, 12), (C_Z, 4), (C_GA, 4), (C_GB, 4)) for j in range(n)]
        columns += [("w_out", QUART * j) for j in range(4)]
        DA, GATE, OUT = 12, 24, 36

        def by_rows(ap):
            return ap.rearrange("p (c n) -> p c n", c=KC)

        def w_split(e, s, small):
            if small:
                e.wait_ge(*w_hi_done.at(s))
                e.tensor_tensor(w_lo[s % 2][:, :], raw_w[s % 3][:, :], w_hi[s % 2][:, :], ALU.subtract).then_inc(*w_lo_done.next(s))
            else:
                e.wait_ge(ld_w[s % 3].sem, 16 * (s // 3 + 1))
                if s >= 2:
                    e.wait_ge(*pe_proj.at(("used", s - 2)))
                e.activation(w_hi[s % 2][:, :], raw_w[s % 3][:, :], ACT.Copy).then_inc(*w_hi_done.next(s))

        NS = H * NT
        GATE_ROWS = 12 * NT * KC // (3 * NS)

        def ended(k, rows):
            return range(GATE_ROWS * k // rows, GATE_ROWS * (k + 1) // rows) if 0 <= k < 3 * NS else ()

        block = ctx.enter_context(nc.Block())

        def chunk_source(e, c):
            if c < 8:
                w, hf, rows = io["w_up" if c // 2 % 2 else "w_gate"], c // 4, D // 2
                return w[bass.ds(e, 1), c % 2 * rows:(c % 2 + 1) * rows, hf * HALF:(hf + 1) * HALF].rearrange("e (c p) n -> p (e c) n", p=P)
            rows = D // 4
            return io["w_down"][bass.ds(e, 1), (c - 8) * rows:(c - 7) * rows, :].rearrange("e (c p) n -> p (e c) n", p=P)

        def raw_chunk(c):
            return ring[:, c % 6, :]

        ON_POOL = (1, 5, 9)

        def small_part(i, c):
            mine = [k for k in range(12) if (k in ON_POOL) == (c in ON_POOL)]
            return (p_lo if c in ON_POOL else v_lo).sem, len(mine) * i + mine.index(c) + 1

        @block.sync
        def _(sp):
            sp.dma_start(x0[:, :, :], io["x"].rearrange("(t p) c -> p t c", p=P)).then_inc(ld_x.sem, 16)
            sp.dma_start(cst[:, :], io["cst"]).then_inc(ld_cst.sem, 16)
            sp.dma_start(par[:, :], io["par"]).then_inc(ld_cst.sem, 16)
            sp.dma_start(tokid[:, :], io["tokid"]).then_inc(ld_cst.sem, 16)
            for s, (name, c0) in enumerate(columns):
                if s >= 3:
                    sp.wait_ge(*w_lo_done.at(s - 3))
                if s == DA + 2:
                    sp.wait_ge(*dve_gd.at("end"))
                    sp.wait_ge(*pool_gd.at("end"))
                sp.dma_start(by_rows(raw_w[s % 3][:, :]), io[name][:, c0:c0 + QUART].rearrange("(c p) n -> p c n", p=P)).then_inc(ld_w[s % 3].sem, 16)
                if s == 1:
                    sp.dma_start(wba[:, :, :], io["w_in"][:, C_BA:C_BA + 2 * H].rearrange("(c p) n -> p c n", p=P)).then_inc(ld_ba.sem, 16)
            sp.wait_ge(*dve_mrg.at(("m", H - 1)))
            sp.dma_start(xs[:, :, :], io["x"].rearrange("(t p) c -> p t c", p=P)).then_inc(ld_x2.sem, 16)
            sp.dma_start(g2, io["ffn_g"].to_broadcast([P, D])).then_inc(ld_g.sem, 16)
            sp.dma_start(rw, io["router_w"].rearrange("(c p) e -> p c e", p=P)).then_inc(ld_g.sem, 16)
            sp.dma_start(gf, io["final_g"].to_broadcast([P, D])).then_inc(ld_g.sem, 16)

            def load_block(e, i):
                for c in range(12):
                    if c >= 6 or not isinstance(i, int):
                        sp.wait_ge(*(small_part(i, c - 6) if c >= 6 else small_part(i - 1, c + 6)))
                    sp.dma_start(raw_chunk(c).rearrange("p (c n) -> p c n", n=HALF if c < 8 else D), chunk_source(e, c)).then_inc(ld_e[c % 6].sem, 16)

            load_block(0, 0)
            with sp.Fori(1, NE) as i:
                load_block(i, i)
            sp.wait_ge(*dve_rt.at("be"))
            n_extra = sp.value_load(be[0:1, 15:16], min_val=0, max_val=EXTRA)
            with sp.If(n_extra > 0):
                with sp.Fori(NE, NBLK) as i:
                    e = sp.value_load(be[0:1, bass.ds(i - NE, 1)], min_val=0, max_val=NE - 1)
                    load_block(e, i)
            for t in range(NT):
                sp.wait_ge(*dve_fin.at(("out", t)))
                sp.dma_start(io["out"].rearrange("(t p) c -> p t c", p=P)[:, t, :], xs[:, t, :]).then_inc(st_out.sem, 16)
            sp.wait_ge(st_out.sem, 16 * NT)

        @block.gpsimd
        def _(g):
            def nxt(key=None):
                return pool_pre.next(key)

            g.memset(e_idx[:, :], 0).then_inc(*nxt())
            g.wait_ge(*pool_pre.last())
            g.dma_start(rowtok_dram.rearrange("(p b) o -> p (b o)", p=P), e_idx[:, :]).then_inc(st_rt.sem, 16)
            for r in range(2):
                g.memset(raw[r][:, 0:3], 0.0).then_inc(*nxt("pad"))
            for j, name in enumerate(("b_gate", "b_up", "b_down")):
                for part in range(3):
                    g.dma_start(bias_st[j][32 * part:32 * part + NE, :], io[name]).then_inc(ld_bias.sem, 16)
            g.wait_ge(ld_cst.sem, 48)
            g.tensor_copy(sel[:, :], C("onehot")[0:96, :]).then_inc(*nxt("bias"))

            for ct in range(2 * H):
                g.wait_ge(*act_conv.at(("silu", ct)))
                if ct >= 2:
                    g.wait_ge(*pe_gd.at(("ssq", ct - 2)))
                g.tensor_tensor(sqb[ct % 2], qkvT[:, ct, :], qkvT[:, ct, :], ALU.mult).then_inc(*pool_gd.next(("sq", ct)))

            def gdn_pool(t):
                for gr in range(2):
                    hs = slice(4 * gr, 4 * gr + 4)
                    g.wait_ge(*act_gd.at(("dT", t, gr)))
                    g.tensor_tensor(dT[:, hs, :], dT[:, hs, :], over_heads(C("upper"), 4), ALU.mult).then_inc(*pool_gd.next(("dT", t, gr)))
                for l in range(1, LEVELS):
                    if l == 1:
                        g.wait_ge(*act_gd.at(("aT", t, 1)))
                    if l >= 3:
                        g.wait_ge(*pe_gd.at(("X", t, l - 2, 1)))
                    a = C("masks")[:, (l - 1) * P:l * P]
                    g.tensor_tensor(btm[l % 2], aT, over_heads(a, H), ALU.mult).then_inc(*pool_gd.next(("B", t, l)))
                if t > 0:
                    for gr in range(2):
                        hs = slice(4 * gr, 4 * gr + 4)
                        cs = slice(gr * HALF, (gr + 1) * HALF)
                        g.wait_ge(*dve_gd.at(("o", t, gr)))
                        g.tensor_tensor(ob[:, t, cs], ob[:, t, cs], qs_s[:, hs, :].rearrange("p h n -> p (h n)"), ALU.add).then_inc(*pool_gd.next(("o", t, gr)))

            for t in range(NT):
                gdn_pool(t)
            g.wait_ge(*pool_gd.last())
            g.memset(e_idx1, 0).then_inc(*pool_gd.next("end"))

            for t in range(NT):
                if t >= 2:
                    g.wait_ge(*dve_att.at(("osq", t - 2)))
                g.tensor_tensor(sqm[t % 2], ob[:, t, :], ob[:, t, :], ALU.mult).then_inc(*pool_att.next(("sq", t)))

            for c in range(4):
                for t in range(NT):
                    k = c * NT + t
                    g.wait_ge(*dve_att.at(("rope", c, t)))
                    if c >= 2 and t == 0:
                        g.wait_ge(*pe_att.at(("qkT", c - 2, 3)))
                    g.tensor_tensor(roped[c % 2][:, t, :], rope1[k % 2], rope2[k % 2], ALU.add).then_inc(*pool_att.next(("rope", c, t)))
            g.wait_ge(*pool_att.last())
            g.memset(e_idx1, 0).then_inc(*pool_att.next("end"))

            g.wait_ge(*act_att.at(("gate", 8 * NT - 1)))
            for t in range(NT):
                g.tensor_scalar(ga[:, t, :], ga[:, t, :], 1.0, None, ALU.add).then_inc(*pool_mrg.next())
                g.wait_ge(*pool_mrg.last())
                g.tensor_tensor(heads(ga[:, t, :]), heads(ga[:, t, :]), over_heads(G("subln"), H), ALU.mult).then_inc(*pool_mrg.next(("ga", t)))

            g.wait_ge(st_rt.sem, 16)
            g.wait_ge(*dve_rt.at("dest"))
            scat = rt_at("scat").bitcast(I32)
            for k in range(NT * TOPK):
                g.indirect_dma_start(out=rowtok_dram[:, :], out_offset=bass.IndirectOffsetOnAxis(ap=scat[:, k:k + 1], axis=0),
                                     in_=tokid[:, k:k + 1], in_offset=None).then_inc(st_rt.sem, 16)
            g.wait_ge(st_rt.sem, 16 * (NT * TOPK + 1))
            g.dma_start(e_idx[:, :], rowtok_dram.rearrange("(p b) o -> p (b o)", p=P)).then_inc(ld_rt.sem, 16)
            g.wait_ge(ld_rt.sem, 16)
            g.wait_ge(st_h2.sem, 16 * NT)
            g.wait_ge(*dve_rt.at("end"))

            def gather(i, first=False):
                g.tensor_copy(e_idx1, e_idx[:, bass.ds(i, 1)] if not first else e_idx[:, 0:1]).then_inc(x_idx.sem, 1)
                g.wait_ge(x_idx.sem, 2 * i + 1)
                g.tensor_tensor(e_held, e_idx1, e_idx1, ALU.add).then_inc(x_idx.sem, 1)
                g.indirect_dma_start(out=xg, out_offset=None, in_=h2_dram[:, :],
                                     in_offset=bass.IndirectOffsetOnAxis(ap=e_idx1, axis=0)).then_inc(x_rows.sem, 16)

            gather(0, True)

            def body(i):
                g.wait_ge(e_tr.sem, 4 * i + 2)
                g.wait_ge(x_rows.sem, 16 * i + 16)
                g.wait_ge(x_idx.sem, 2 * i + 2)
                gather(i + 1)
                for c in ON_POOL:
                    g.wait_ge(a_hi.sem, 12 * i + c + 1)
                    g.tensor_tensor(w_lo[c % 4][:, :], raw_chunk(c), w_hi[c % 4][:, :], ALU.subtract).then_inc(p_lo.sem, 1)

            body(0)
            with g.Fori(1, NE) as i:
                body(i)
            n_extra = g.value_load(be[0:1, 15:16], min_val=0, max_val=EXTRA)
            with g.If(n_extra > 0):
                with g.Fori(NE, NBLK) as i:
                    body(i)
                g.wait_ge(x_rows.sem, 16 * (NBLK + 1))
                g.wait_ge(st_y.sem, 16 * (NBLK + 1))
            g.wait_ge(x_rows.sem, 16 * (NE + 1))
            g.wait_ge(st_y.sem, 16 * (NE + 1))

            def collect(rows):
                for k in range(NT * TOPK):
                    r = k % 6
                    if k >= 6:
                        g.wait_ge(*dve_fin.at(("row", k - 6)))
                    g.indirect_dma_start(out=ring[:, r, 0:D], out_offset=None, in_=rows,
                                         in_offset=bass.IndirectOffsetOnAxis(ap=y_idx[:, k:k + 1], axis=0)).then_inc(ld_row[r].sem, 16)

            with g.If(n_extra > 0):
                collect(y_dram[:, :])
            with g.Else():
                collect(y_dram[0:NE * P, :])

        @block.scalar
        def _(a):
            a.wait_ge(ld_x.sem, 16)
            for t in range(NT):
                a.activation(xn[:, t, :], x0[:, t, :], ACT.Square, accum_out=ss[:, t:t + 1]).then_inc(*act_pre.next(("ss", t)))
            a.wait_ge(*dve_pre.at("var"))
            a.activation(rstd, ss, ACT.Sqrt).then_inc(*act_pre.next("std"))
            a.wait_ge(ld_cst.sem, 48)
            for kc in range(KC):
                a.wait_ge(*pe_hT.at(kc))
                a.activation(hT_hi[:, kc, :], ps[kc][:, :], ACT.Copy, scale=G("mix_g")[:, kc:kc + 1]).then_inc(*act_pre.next(("hT", kc)))
                if kc == 3:
                    w_split(a, 0, False)
            w_split(a, 1, False)
            a.wait_ge(ld_ba.sem, 16)
            a.activation(wba_hi[:, :, :], wba[:, :, :], ACT.Copy).then_inc(*act_pre.next("wba"))

            def silu(ct):
                a.wait_ge(*dve_conv.at(ct))
                a.activation(qkvT[:, ct, :], cacc[ct % 2], ACT.Silu).then_inc(*act_conv.next(("silu", ct)))

            def strength_and_decay():
                a.wait_ge(*dve_gd.at("ba"))
                a.activation(beta, ba[:, :, 0:H], ACT.Sigmoid).then_inc(*act_gd.next("beta"))
                a.activation(ealog, G("a_log"), ACT.Exp).then_inc(*act_gd.next())
                for k in range(2):
                    a.wait_ge(*dve_gd.at(("lam", k)))
                    a.activation(lam2[:, k:k + 1], nlam if k else lam2[:, 0:1], ACT.Exp).then_inc(*act_gd.next(("lam", k)))
                a.wait_ge(*dve_gd.at("nabs"))
                a.activation(spe, spe, ACT.Exp).then_inc(*act_gd.next("spe"))
                a.wait_ge(*dve_gd.at("spe1"))
                a.activation(spe, spe, ACT.Ln).then_inc(*act_gd.next("ln"))

            def norms_and_decays():
                a.wait_ge(*dve_gd.at("nrm"))
                a.activation(nrm, nrm, ACT.Sqrt).then_inc(*act_gd.next("nrm"))
                a.wait_ge(*pe_gd.at("dec"))
                a.activation(dec, ps[5][:, 0:3 * NT * H], ACT.Exp).then_inc(*act_gd.next("dec"))

            for ct in range(3 * H):
                a.wait_ge(*pe_proj.at(("gd", ct)))
                if ct == 0:
                    a.wait_ge(*pool_pre.at("pad"))
                if ct >= 2:
                    a.wait_ge(*dve_conv.at(ct - 2))
                a.activation(raw[ct % 2][:, 3:], ps[ct % 4][:, :], ACT.Copy).then_inc(*act_conv.next(("raw", ct)))
                if ct >= 1:
                    silu(ct - 1)
                if ct % 2 == 1 and (ct + 3) // 2 < DA:
                    w_split(a, (ct + 3) // 2, False)
                if ct == CT_BA:
                    a.wait_ge(*pe_proj.at("baT"))
                    a.activation(baT, ps[4][0:2 * H, :], ACT.Copy).then_inc(*act_gd.next("baT"))
                if ct == CT_BA + 2:
                    strength_and_decay()
                if ct == CT_NORM:
                    norms_and_decays()
            silu(3 * H - 1)

            def flat(ap, gr):
                return ap[:, 4 * gr:4 * gr + 4, :].rearrange("p h n -> p (h n)")

            for t in range(NT):
                for gr in range(2):
                    a.wait_ge(*pe_gd.at(("D", t, gr)))
                    if t > 0:
                        a.wait_ge(*dve_gd.at(("qkd", t - 1, 3)))
                    a.activation(flat(dT, gr), ps[gr][:, :], ACT.Exp).then_inc(*act_gd.next(("dT", t, gr)))
                for gr in range(2):
                    a.wait_ge(*pe_gd.at(("K", t, gr)))
                    if t > 0:
                        a.wait_ge(*pe_gd.at(("dS", t - 1, 1)))
                    a.activation(flat(k_tok, gr), ps[6 + gr][:, :], ACT.Copy).then_inc(*act_gd.next(("K", t, gr)))
                for gr in range(2):
                    a.wait_ge(*pe_gd.at(("aT", t, gr)))
                    if t > 0:
                        a.wait_ge(*pool_gd.at(("B", t - 1, LEVELS - 1)))
                    a.activation(flat(aT, gr), ps[4 + gr][:, :], ACT.Copy).then_inc(*act_gd.next(("aT", t, gr)))
                for gr in range(2):
                    a.wait_ge(*pe_gd.at(("triT", t, gr)))
                    a.activation(flat(triT, gr), ps[6 + gr][:, :], ACT.Copy).then_inc(*act_gd.next(("triT", t, gr)))
                for l in range(1, LEVELS):
                    for gr in range(2):
                        a.wait_ge(*pe_gd.at(("X", t, l, gr)))
                        a.wait_ge(*pe_gd.at(("YT", t, l - 1, gr) if l > 1 else ("triT", t, gr)))
                        a.activation(flat(xlev, gr), ps[gr][:, :], ACT.Copy).then_inc(*act_gd.next(("X", t, l, gr)))
                for gr in range(2):
                    a.wait_ge(*pe_gd.at(("P", t, gr)))
                    a.activation(flat(p_out, gr), ps[2 + gr][:, :], ACT.Copy).then_inc(*act_gd.next(("P", t, gr)))

            a.wait_ge(*dve_gd.at("end"))
            a.wait_ge(*pool_gd.at("end"))
            w_split(a, DA, False)
            w_split(a, DA + 1, False)
            a.wait_ge(*dve_att.at("ovar"))
            a.activation(osq, osq, ACT.Sqrt).then_inc(*act_att.next("ostd"))
            for c in range(6):
                for t in range(NT):
                    if c >= 4:
                        a.wait_ge(*pe_proj.at(("da", c, t)))
                        a.activation(va[:, t, (c - 4) * HALF:(c - 3) * HALF], ps[t][:, :], ACT.Copy).then_inc(*act_att.next(("v", c - 4, t)))
                    if t % 2 == 1:
                        w_split(a, DA + 2 * c + 2 + t // 2, False)
                if 1 <= c < 5:
                    for h4 in range(4):
                        a.wait_ge(*pe_att.at(("qkT", c - 1, h4)))
                        dst = (qaT if c < 3 else kaT)[:, 4 * ((c - 1) % 2) + h4, :]
                        a.activation(dst, ps[4 + h4][:, :], ACT.Copy).then_inc(*act_att.next(("qkT", c - 1, h4)))

            def att_wT(n):
                h, i = divmod(n, NT)
                a.wait_ge(*pe_att.at(("wT", n)))
                a.activation(wT[n % 2][:, 0:(i + 1) * P], ps[4][:, 0:(i + 1) * P], ACT.Copy).then_inc(*act_att.next(("wT", n)))

            def att_out(n):
                h, i = divmod(n, NT)
                a.wait_ge(*pe_att.at(("pv", n)))
                k = n % 2
                rec = recs[:, 2 * k:2 * k + 1]
                if n >= 2:
                    a.wait_ge(*act_att.at(("ssq", n - 2)))
                a.activation(ps[5][:, (1 + k) * P:(2 + k) * P], ps[5][:, 0:P], ACT.Square, scale=rec,
                             accum_out=oasq[:, n:n + 1]).then_inc(*act_att.next(("ssq", n)))
                a.activation(qaT[:, h, i * P:(i + 1) * P], ps[5][:, 0:P], ACT.Copy, scale=rec).then_inc(*act_att.next(("out", n)))

            def gates(k):
                for u in ended(k, KC):
                    (j, q), t = divmod(u // NT, 4), u % NT
                    a.wait_ge(*pe_proj.at(("gate", u)))
                    if j != 1 and u >= 2:
                        a.wait_ge(*dve_att.at(("gate", u - 2)))
                    dst = ga[:, t, q * QUART:(q + 1) * QUART] if j == 1 else gate_s[u % 2][:, :]
                    a.activation(dst, ps[6 + u % 2][:, 0:QUART], ACT.Tanh, scale=0.5).then_inc(*act_att.next(("gate", u)))
                for g in ended(k, NT * KC):
                    w_split(a, GATE + 2 + g, False)

            for n in range(NS + 2):
                gates(3 * n - 1)
                if n < NS:
                    i = n % NT
                    for c in range(2):
                        k = 2 * (n % 2) + c
                        a.wait_ge(*dve_att.at(("max", n)))
                        if n >= 2:
                            a.wait_ge(*dve_att.at(("diff", n - 2)))
                        a.activation(probs[n % 2][c][:, 0:(i + 1) * P], ps[k][:, 0:(i + 1) * P], ACT.Exp, bias=nmx[:, k:k + 1],
                                     scale=DH ** -0.5, accum_out=esum[:, k:k + 1]).then_inc(*act_att.next(("exp", n, c)))
                gates(3 * n)
                if n >= 1 and n - 1 < NS:
                    att_wT(n - 1)
                gates(3 * n + 1)
                if n >= 2:
                    att_out(n - 2)
            act_att.marks["end"] = act_att.count

            a.wait_ge(*dve_mrg.at("ovar"))
            a.activation(oasq, oasq, ACT.Sqrt).then_inc(*act_mrg.next("ostd"))
            for kc in range(KC):
                a.wait_ge(*pe_mrg.at(("mT", kc)))
                a.activation(mT_hi[:, kc, :], ps[4 + kc % 4][:, :], ACT.Copy).then_inc(*act_mrg.next(("mT", kc)))
            for s in (OUT + 2, OUT + 3):
                w_split(a, s, False)

            for t in range(NT):
                a.wait_ge(*dve_mrg.at(("x1", 1, t)))
                if t:
                    a.wait_ge(*act_rt.at(("ss", t - 1)))
                a.activation(junk, xs[:, t, :], ACT.Square, accum_out=ss[:, t:t + 1]).then_inc(*act_rt.next(("ss", t)))
                a.wait_ge(*dve_rt.at(("var", t)))
                a.activation(rstd[:, t:t + 1], ss[:, t:t + 1], ACT.Sqrt).then_inc(*act_rt.next(("std", t)))
                a.wait_ge(*dve_rt.at(("h2", t)))
                a.dma_start(h2_dram[t * P:(t + 1) * P, :], h2[:, t, :]).then_inc(st_h2.sem, 16)
            for kc in range(KC):
                a.wait_ge(*pe_rt.at(("h2T", kc)))
                a.activation(h2T[:, kc, :], ps[4 + kc % 4][:, :], ACT.Copy).then_inc(*act_rt.next(("h2T", kc)))
            a.wait_ge(*dve_rt.at("gsub"))
            a.activation(gw, gw, ACT.Exp).then_inc(*act_rt.next("gexp"))
            a.wait_ge(*dve_rt.at("end"))

            def to_hi(dst, k, bank, value):
                a.wait_ge(e_tr.sem, value)
                a.activation(dst[:, k * HALF:(k + 1) * HALF], ps[bank][:, :], ACT.Copy).then_inc(a_tr.sem, 1)

            for half in range(2):
                to_hi(xT_hi, half, 7 - half, half + 1)

            def w_parts(i, chunks):
                for c in chunks:
                    a.wait_ge(ld_e[c % 6].sem, 32 * i + 16 * (c // 6) + 16)
                    a.wait_ge(e_used.sem, 12 * i + c + 1)
                    a.activation(w_hi[c % 4][:, :], raw_chunk(c), ACT.Copy).then_inc(a_hi.sem, 1)

            def result(i):
                a.wait_ge(e_used.sem, 12 * i + 16)
                a.wait_ge(st_y.sem, 16 * i + 16)
                a.activation(ys[:, HALF:D], ps[5][:, :], ACT.Copy).then_inc(a_y.sem, 1)
                a.wait_ge(v_y.sem, i + 2)
                a.wait_ge(a_y.sem, i + 2)
                a.dma_start(y_dram[bass.ds(i * P, P), :], ys[:, :]).then_inc(st_y.sem, 16)

            def body(i, before=False):
                w_parts(i, range(0, 3))
                if before:
                    result(i - 1)
                w_parts(i, range(3, 8))
                a.wait_ge(v_act.sem, 8 * i + 9)
                a.activation(sg[0], gm[0], ACT.Sigmoid, scale=ALPHA).then_inc(a_sig.sem, 1)
                w_parts(i, range(8, 10))
                to_hi(avT_hi, 0, 6, 4 * i + 3)
                w_parts(i, range(10, 11))
                a.wait_ge(v_act.sem, 8 * i + 13)
                a.activation(sg[1], gm[1], ACT.Sigmoid, scale=ALPHA).then_inc(a_sig.sem, 1)
                to_hi(xT_hi, 0, 7, 4 * i + 4)
                w_parts(i, range(11, 12))
                to_hi(xT_hi, 1, 6, 4 * i + 5)
                to_hi(avT_hi, 1, 7, 4 * i + 6)

            a.sem_inc(st_y.sem, 16)
            a.sem_inc(a_y.sem, 1)
            body(0)
            with a.Fori(1, NE) as i:
                body(i, True)
            result(NE - 1)
            n_extra = a.value_load(be[0:1, 15:16], min_val=0, max_val=EXTRA)
            with a.If(n_extra > 0):
                with a.Fori(NE, NBLK) as i:
                    body(i)
                    result(i)

            for t in range(NT):
                a.wait_ge(*dve_fin.at(("sum", t)))
                if t:
                    a.wait_ge(*act_fin.at(("ss", t - 1)))
                a.activation(junk, xs[:, t, :], ACT.Square,
                             accum_out=ss[:, t:t + 1]).then_inc(*act_fin.next(("ss", t)))
                a.wait_ge(*dve_fin.at(("var", t)))
                a.activation(rstd[:, t:t + 1], ss[:, t:t + 1], ACT.Sqrt).then_inc(*act_fin.next(("std", t)))

        @block.tensor
        def _(pe):
            pe.sem_inc(e_used.sem, 4)
            pe.wait_ge(ld_cst.sem, 48)
            pe.wait_ge(*dve_pre.at(("xn", NT - 1)))
            for kc in range(KC):
                for t in range(NT):
                    mm = pe.transpose(ps[kc][:, t * P:(t + 1) * P], xn[:, t, kc * P:(kc + 1) * P], ident)
                mm.then_inc(*pe_hT.next(kc))

            def in_three(out, k_hi, k_lo, n_hi, n_lo, first, last):
                pe.matmul(out, k_hi, n_hi, start=first, stop=False)
                pe.matmul(out, k_hi, n_lo, start=False, stop=False)
                return pe.matmul(out, k_lo, n_hi, start=False, stop=last)

            def by_channel(ct):
                s, cols = ct // 2, slice(ct % 2 * P, (ct % 2 + 1) * P)
                pe.wait_ge(*w_lo_done.at(s))
                for kc in range(KC):
                    mm = in_three(ps[ct % 4][:, :], by_rows(w_hi[s % 2][:, :])[:, kc, cols], by_rows(w_lo[s % 2][:, :])[:, kc, cols],
                                  hT_hi[:, kc, :], hT_lo[:, kc, :], kc == 0, kc == KC - 1)
                mm.then_inc(*pe_proj.next(("gd", ct)))
                if ct % 2:
                    pe_proj.marks[("used", s)] = pe_proj.count

            def by_token(out, src_hi, src_lo, t, s, kc, first=True, last=True):
                tok = slice(t * P, (t + 1) * P)
                return in_three(out, src_hi[:, kc, tok], src_lo[:, kc, tok], by_rows(w_hi[s % 2][:, :])[:, kc, :],
                                by_rows(w_lo[s % 2][:, :])[:, kc, :], first and kc == 0, last and kc == KC - 1)

            def ssq(ct):
                pe.wait_ge(*pool_gd.at(("sq", ct)))
                for t in range(NT):
                    c = t * 2 * H + ct
                    mm = pe.matmul(ps[6][:, c:c + 1], sqb[ct % 2][:, t * P:(t + 1) * P], C("ones")[:, 0:1], start=True, stop=True)
                mm.then_inc(*pe_gd.next(("ssq", ct)))

            pe.wait_ge(*dve_pre.at(("hT", KC - 1)))
            for ct in range(3 * H):
                if ct >= 4:
                    pe.wait_ge(*act_conv.at(("raw", ct - 4)))
                by_channel(ct)
                if ct == CT_BA:
                    pe.wait_ge(*dve_pre.at("wba"))
                    for kc in range(KC):
                        mm = in_three(ps[4][0:2 * H, :], wba_hi[:, kc, :], wba_lo[:, kc, :], hT_hi[:, kc, :], hT_lo[:, kc, :],
                                      kc == 0, kc == KC - 1)
                    mm.then_inc(*pe_proj.next("baT"))
                if ct == CT_BA + 1:
                    pe.wait_ge(*act_gd.at("baT"))
                    for t in range(NT):
                        mm = pe.transpose(ps[7][:, t * 2 * H:(t + 1) * 2 * H], baT[:, t * P:(t + 1) * P], ident[0:2 * H, 0:2 * H])
                    mm.then_inc(*pe_proj.next("ba"))
                if ct == CT_BA + 5:
                    pe.wait_ge(*dve_gd.at("g"))
                    gall = gdec.rearrange("p t h -> p (t h)")
                    n = NT * H
                    for j, name in enumerate(("upper", "later", "ones")):
                        mm = pe.matmul(ps[5][:, j * n:(j + 1) * n], C(name), gall, start=True, stop=True)
                    mm.then_inc(*pe_gd.next("dec"))
                if 2 <= ct < 2 * H + 2:
                    ssq(ct - 2)

            def qT(h, t):
                return qkvT[:, h, t * P:(t + 1) * P]

            def kT(h, t):
                return qkvT[:, H + h, t * P:(t + 1) * P]

            def four(bank, gr, name, key, lhsT, rhs=None):
                for j in range(4):
                    h = 4 * gr + j
                    out = ps[bank][:, j * P:(j + 1) * P]
                    if rhs is None:
                        mm = pe.transpose(out, lhsT(h), ident)
                    else:
                        mm = pe.matmul(out, lhsT(h), rhs(h), start=True, stop=True)
                mm.then_inc(*pe_gd.next((name,) + key))

            pe.wait_ge(*act_gd.at("dec"))
            pe.wait_ge(*act_conv.at(("silu", 3 * H - 1)))
            pe.wait_ge(*dve_gd.at("coef"))
            for t in range(NT):
                for gr in range(2):
                    pe.wait_ge(*dve_gd.at(("gl", t)))
                    if t > 1:
                        pe.wait_ge(*dve_gd.at(("qs", t - 1, gr)))
                    four(gr, gr, "D", (t, gr), lambda h: gl[:, h, :], lambda h: C("upper"))
                for pr in range(4):
                    if t > 0:
                        if pr < 2:
                            pe.wait_ge(*act_gd.at(("P", t - 1, pr)))
                        else:
                            pe.wait_ge(*dve_gd.at(("S", t - 1, pr - 2)))
                    for j in range(2):
                        h = 2 * pr + j
                        qk = qkvT[:, h:h + H + 1:H, t * P:(t + 1) * P]
                        mm = pe.matmul(ps[2 + pr][:, j * 2 * P:(j + 1) * 2 * P], kT(h, t), qk, start=True, stop=True)
                    mm.then_inc(*pe_gd.next(("qk", t, pr)))
                for gr in range(2):
                    if t > 0:
                        pe.wait_ge(*dve_gd.at(("o", t - 1, gr)))
                    four(6 + gr, gr, "V", (t, gr), lambda h: qkvT[:, 2 * H + h, t * P:(t + 1) * P])
                for gr in range(2):
                    pe.wait_ge(*dve_gd.at(("v", t, gr)))
                    four(6 + gr, gr, "K", (t, gr), lambda h: kT(h, t))
                for gr in range(2):
                    pe.wait_ge(*dve_gd.at(("qkd", t, 2 * gr + 1)))
                    pe.wait_ge(*act_gd.at(("dT", t, gr)))
                    four(gr, gr, "Yt", (t, gr), lambda h: qkd[:, h, 1, :])
                for gr in range(2):
                    pe.wait_ge(*dve_gd.at(("a", t, gr)))
                    pe.wait_ge(*dve_gd.at(("qkd", t, 3)))
                    four(4 + gr, gr, "aT", (t, gr), lambda h: a_row[:, h, :])
                for gr in range(2):
                    pe.wait_ge(*dve_gd.at(("tri", t, 0, gr)))
                    pe.wait_ge(*act_gd.at(("K", t, gr)))
                    four(6 + gr, gr, "triT", (t, gr), lambda h: tri[:, h, :])
                for l in range(1, LEVELS):
                    for gr in range(2):
                        pe.wait_ge(*pool_gd.at(("B", t, l)))
                        pe.wait_ge(*dve_gd.at(("tri", t, l - 1, gr)))
                        if l > 1:
                            pe.wait_ge(*act_gd.at(("X", t, l - 1, gr)))
                        four(gr, gr, "X", (t, l, gr), lambda h: btm[l % 2][:, h, :], lambda h: tri[:, h, :])
                    for gr in range(2):
                        pe.wait_ge(*act_gd.at(("X", t, l, gr)))
                        if l > 1:
                            pe.wait_ge(*dve_gd.at(("triT", t, l - 1, gr)))
                        else:
                            pe.wait_ge(*act_gd.at(("triT", t, gr)))
                        if l < LEVELS - 1:
                            four(2 + gr, gr, "Y", (t, l, gr), lambda h: triT[:, h, :], lambda h: xlev[:, h, :])
                        four(4 + gr, gr, "YT", (t, l, gr), lambda h: xlev[:, h, :], lambda h: triT[:, h, :])
                if t > 0:
                    for gr in range(2):
                        pe.wait_ge(*dve_gd.at(("S", t - 1, gr)))
                        four(6 + gr, gr, "KS", (t, gr), lambda h: kT(h, t), lambda h: state[:, h, :])
                        pe.wait_ge(*act_gd.at(("X", t, LEVELS - 1, gr)))
                        four(gr, gr, "QS", (t, gr), lambda h: qT(h, t), lambda h: state[:, h, :])
                for gr in range(2):
                    pe.wait_ge(*dve_gd.at(("w", t, gr) if t else ("v", t, gr)))
                    pe.wait_ge(*dve_gd.at(("triT", t, LEVELS - 1, gr)))
                    four(2 + gr, gr, "P", (t, gr), lambda h: triT[:, h, :], lambda h: (w_rhs if t else v_w)[:, h, :])
                for gr in range(2):
                    pe.wait_ge(*act_gd.at(("P", t, gr)))
                    four(6 + gr, gr, "O", (t, gr), lambda h: qkd[:, h, 0, :], lambda h: p_out[:, h, :])
                if t < NT - 1:
                    for gr in range(2):
                        pe.wait_ge(*dve_gd.at(("pd", t, gr)))
                        four(4 + gr, gr, "dS", (t, gr), lambda h: k_tok[:, h, :], lambda h: p_dec[:, h, :])

            def qkT(c):
                for h4 in range(4):
                    for t in range(NT):
                        pe.wait_ge(*pool_att.at(("rope", c, t)))
                    if c >= 1:
                        pe.wait_ge(*act_att.at(("qkT", c - 1, h4)))
                    for t in range(NT):
                        mm = pe.transpose(ps[4 + h4][:, t * P:(t + 1) * P], roped[c % 2][:, t, h4 * P:(h4 + 1) * P], ident)
                    mm.then_inc(*pe_att.next(("qkT", c, h4)))

            pe.wait_ge(*dve_gd.at("end"))
            for c in range(6):
                for part in range(2):
                    s = DA + 2 * c + part
                    pe.wait_ge(*w_lo_done.at(s))
                    for t in range(NT):
                        if part == 0 and 1 <= c < 5:
                            pe.wait_ge(*dve_att.at(("rope", c - 1, t)))
                        elif part == 0 and c:
                            pe.wait_ge(*act_att.at(("v", c - 5, t)))
                        for kc in range(KC):
                            mm = by_token(ps[t][:, part * QUART:(part + 1) * QUART], hT_hi, hT_lo, t, s, kc)
                        mm.then_inc(*pe_proj.next(("da", c, t) if part else None))
                    pe_proj.marks[("used", s)] = pe_proj.count
                if 1 <= c < 5:
                    qkT(c - 1)

            def scores(n):
                h, i = divmod(n, NT)
                for c in range(2):
                    if n >= 2:
                        pe.wait_ge(*act_att.at(("exp", n - 2, c)))
                    else:
                        pe.wait_ge(*act_att.at(("v", 1, 2 * n + c)))
                    r = slice(c * DH, (c + 1) * DH)
                    pe.matmul(ps[2 * (n % 2) + c][:, 0:(i + 1) * P], qaT[r, h, i * P:(i + 1) * P], kaT[r, h, 0:(i + 1) * P],
                              start=True, stop=True).then_inc(*pe_att.next(("sc", n, c)))

            def diff_T(n):
                h, i = divmod(n, NT)
                pe.wait_ge(*dve_att.at(("diff", n)))
                if n:
                    pe.wait_ge(*act_att.at(("wT", n - 1)))
                for kb in range(i + 1):
                    mm = pe.transpose(ps[4][:, kb * P:(kb + 1) * P], wdiff[n % 2][:, kb * P:(kb + 1) * P], ident)
                mm.then_inc(*pe_att.next(("wT", n)))

            def pv(n):
                h, i = divmod(n, NT)
                pe.wait_ge(*act_att.at(("wT", n)))
                if n:
                    pe.wait_ge(*act_att.at(("out", n - 1)))
                for kb in range(i + 1):
                    mm = pe.matmul(ps[5][:, 0:P], wT[n % 2][:, kb * P:(kb + 1) * P], va[:, kb, h * P:(h + 1) * P],
                                   start=kb == 0, stop=kb == i)
                mm.then_inc(*pe_att.next(("pv", n)))

            def gate_rows(k):
                for q in range(GATE_ROWS * k, GATE_ROWS * (k + 1)):
                    u, kc = divmod(q, KC)
                    g, t = divmod(u, NT)
                    if kc == 0:
                        if t == 0:
                            pe.wait_ge(*w_lo_done.at(GATE + g))
                        if u >= 2:
                            pe.wait_ge(*(dve_att if u - 2 < 4 * NT else act_att).at(("gate", u - 2)))
                    mm = by_token(ps[6 + u % 2][:, 0:QUART], hT_hi, hT_lo, t, GATE + g, kc)
                    if kc == KC - 1:
                        mm.then_inc(*pe_proj.next(("gate", u)))
                        if t == NT - 1:
                            pe_proj.marks[("used", GATE + g)] = pe_proj.count

            pe.wait_ge(*act_att.at(("qkT", 3, 3)))
            pe.wait_ge(*act_att.at(("v", 1, NT - 1)))
            for n in range(NS + 2):
                if n < NS:
                    scores(n)
                    gate_rows(3 * n)
                if 1 <= n <= NS:
                    diff_T(n - 1)
                if n < NS:
                    gate_rows(3 * n + 1)
                if n >= 2:
                    pv(n - 2)
                if n < NS:
                    gate_rows(3 * n + 2)

            pe.wait_ge(*act_att.at("end"))

            def merged_T(kc):
                if kc >= 4:
                    pe.wait_ge(*dve_mrg.at(("mT", kc - 4)))
                pe.wait_ge(*dve_mrg.at(("m", kc)))
                for t in range(NT):
                    mm = pe.transpose(ps[4 + kc % 4][:, t * P:(t + 1) * P], ob[:, t, kc * P:(kc + 1) * P], ident)
                mm.then_inc(*pe_mrg.next(("mT", kc)))

            merged_T(0)
            for s in (OUT, OUT + 1):
                pe.wait_ge(*w_lo_done.at(s))
            for kc in range(KC):
                if kc < KC - 1:
                    merged_T(kc + 1)
                pe.wait_ge(*dve_mrg.at(("mT", kc)))
                for part in range(2):
                    for t in range(NT):
                        mm = by_token(ps[t][:, part * QUART:(part + 1) * QUART], mT_hi, mT_lo, t, OUT + part, kc, part == 0, part == 1)
                        if kc == KC - 1:
                            mm.then_inc(*pe_proj.next(("out", 0, t) if part else None))
                    pe_proj.marks[("used", OUT + part)] = pe_proj.count
            for s in (OUT + 2, OUT + 3):
                pe.wait_ge(*w_lo_done.at(s))
            for t in range(NT):
                pe.wait_ge(*dve_mrg.at(("x1", 0, t)))
                for part in range(2):
                    for kc in range(KC):
                        mm = by_token(ps[t][:, part * QUART:(part + 1) * QUART], mT_hi, mT_lo, t, OUT + 2 + part, kc)
                mm.then_inc(*pe_proj.next(("out", 1, t)))

            for kc in range(KC):
                if kc >= 4:
                    pe.wait_ge(*act_rt.at(("h2T", kc - 4)))
                for t in range(NT):
                    pe.wait_ge(*dve_rt.at(("h2", t)))
                    mm = pe.transpose(ps[4 + kc % 4][:, t * P:(t + 1) * P], h2[:, t, kc * P:(kc + 1) * P], ident)
                mm.then_inc(*pe_rt.next(("h2T", kc)))
            pe.wait_ge(*act_rt.at(("h2T", KC - 1)))
            pe.wait_ge(ld_g.sem, 48)
            for t in range(NT):
                for kc in range(KC):
                    mm = pe.matmul(ps[0][:, t * NE:(t + 1) * NE], h2T[:, kc, t * P:(t + 1) * P], rw[:, kc, :],
                                   start=kc == 0, stop=kc == KC - 1)
            mm.then_inc(*pe_rt.next("logits"))
            pe.wait_ge(*dve_rt.at("mask"))
            mask = rt_at("mask").rearrange("p (t e) -> p t e", t=NT)
            for t in range(NT):
                for u in range(t + 1):
                    pe.matmul(ps[1][:, t * NE:(t + 1) * NE], C("before") if u == t else C("ones"), mask[:, u, :],
                              start=u == 0, stop=u == t)
            for u in range(NT):
                mm = pe.matmul(ps[2][:, 0:NE], C("ones"), mask[:, u, :], start=u == 0, stop=u == NT - 1)
            mm.then_inc(*pe_rt.next("rank"))

            def rows_T(b, half):
                for j in range(4):
                    c = 4 * half + j
                    mm = pe.transpose(ps[b][:, j * P:(j + 1) * P], xg[:, c * P:(c + 1) * P], ident)
                mm.then_inc(e_tr.sem, 1)

            pe.wait_ge(*act_rt.at(("h2T", KC - 1)))
            pe.wait_ge(*dve_rt.at("end"))
            pe.wait_ge(x_rows.sem, 16)
            rows_T(7, 0)
            rows_T(6, 1)
            pe.wait_ge(*pool_pre.at("bias"))

            def bias(b, e, col):
                pe.matmul(ps[b][:, :], sel[:, bass.ds(e, 1)].to_broadcast([96, P]), btab[:, col:col + HALF], start=True, stop=False)

            def in_parts(bank, x_hi, x_lo, kc, c, col, stop):
                k, n = slice(kc * P, (kc + 1) * P), slice(col, col + HALF)
                pe.matmul(ps[bank][:, :], x_hi[:, k], w_hi[c % 4][:, n], start=False, stop=False)
                pe.matmul(ps[bank][:, :], x_lo[:, k], w_hi[c % 4][:, n], start=False, stop=False)
                return pe.matmul(ps[bank][:, :], x_hi[:, k], w_lo[c % 4][:, n], start=False, stop=stop)

            def body(i, e):
                def act_T(hf):
                    pe.wait_ge(v_act.sem, 8 * i + 4 * hf + 12)
                    if hf:
                        pe.wait_ge(v_tr.sem, 4 * i + 4)
                    for j in range(4):
                        mm = pe.transpose(ps[6 + hf][:, j * P:(j + 1) * P], av[hf][:, j * P:(j + 1) * P], ident)
                    mm.then_inc(e_tr.sem, 1)

                pe.wait_ge(v_tr.sem, 4 * i + 2)
                for s in range(4):
                    pe.wait_ge(v_act.sem, 8 * i + 4 * (s // 2) + s % 2 + 1)
                    bias(s, e, s % 2 * D + s // 2 * HALF)
                    for c in (2 * s, 2 * s + 1):
                        pe.wait_ge(*small_part(i, c))
                        for j in range(4):
                            mm = in_parts(s, xT_hi, xT_lo, 4 * (c % 2) + j, c, j * HALF, c % 2 == 1 and j == 3)
                        mm.then_inc(e_used.sem, 1)
                        if c == 6:
                            act_T(0)
                pe.wait_ge(x_rows.sem, 16 * i + 32)
                rows_T(7, 0)
                pe.wait_ge(v_y.sem, i + 1)
                pe.wait_ge(a_y.sem, i + 1)
                for nh in range(2):
                    bias(4 + nh, e, 2 * D + nh * HALF)
                pe.wait_ge(v_tr.sem, 4 * i + 3)
                for c in range(8, 12):
                    pe.wait_ge(*small_part(i, c))
                    if c == 9:
                        rows_T(6, 1)
                    if c == 10:
                        pe.wait_ge(v_tr.sem, 4 * i + 6)
                    for j in range(2):
                        for nh in range(2):
                            mm = in_parts(4 + nh, avT_hi, avT_lo, 2 * (c - 8) + j, c, j * D + nh * HALF, c == 11 and j == 1)
                        if c == 9 and j == 0:
                            act_T(1)
                    mm.then_inc(e_used.sem, 1)

            with pe.Fori(0, NE) as i:
                body(i, i)
            n_extra = pe.value_load(be[0:1, 15:16], min_val=0, max_val=EXTRA)
            with pe.If(n_extra > 0):
                with pe.Fori(NE, NBLK) as i:
                    e = pe.value_load(be[0:1, bass.ds(i - NE, 1)], min_val=0, max_val=NE - 1)
                    body(i, e)

        @block.vector
        def _(v):
            v.sem_inc(v_act.sem, 8)
            v.sem_inc(v_y.sem, 1)

            def then(sig, ins, key=None):
                ins.then_inc(*sig.next(key))
                v.wait_ge(*sig.last())

            v.wait_ge(*act_pre.at(("ss", NT - 1)))
            then(dve_pre, v.tensor_scalar(ss, ss, 1.0 / D, EPS, ALU.mult, ALU.add), "var")
            v.wait_ge(*act_pre.at("std"))
            then(dve_pre, v.reciprocal(rstd, rstd))
            for t in range(NT):
                v.tensor_scalar(xn[:, t, :], x0[:, t, :], rstd[:, t:t + 1], None, ALU.mult).then_inc(*dve_pre.next(("xn", t)))
            v.wait_ge(ld_cst.sem, 48)
            for kc in range(KC):
                v.wait_ge(*act_pre.at(("hT", kc)))
                v.scalar_tensor_tensor(out=hT_lo[:, kc, :], in0=ps[kc][:, :], scalar=G("mix_g")[:, kc:kc + 1], in1=hT_hi[:, kc, :],
                                       op0=ALU.mult, op1=ALU.subtract).then_inc(*dve_pre.next(("hT", kc)))
                if kc == 5:
                    w_split(v, 0, True)
            w_split(v, 1, True)
            v.wait_ge(*act_pre.at("wba"))
            v.tensor_tensor(wba_lo[:, :, :], wba[:, :, :], wba_hi[:, :, :], ALU.subtract).then_inc(*dve_pre.next("wba"))

            def bias_parts(j):
                v.wait_ge(ld_bias.sem, 16 * 9)
                st, cols = bias_st[j], slice(j * D, (j + 1) * D)
                then(dve_pre, v.tensor_copy(bias_hi, st))
                then(dve_pre, v.tensor_tensor(st, st, bias_hi, ALU.subtract))
                then(dve_pre, v.tensor_copy(bias_mid, st))
                then(dve_pre, v.tensor_tensor(st, st, bias_mid, ALU.subtract))
                then(dve_pre, v.tensor_copy(bias_lo, st))
                then(dve_pre, v.tensor_copy(btab[0:32, cols], bias_hi[0:32, :]))
                then(dve_pre, v.tensor_copy(btab[32:64, cols], bias_mid[32:64, :]))
                then(dve_pre, v.tensor_copy(btab[64:96, cols], bias_lo[64:96, :]), "bias")

            def conv(ct):
                v.wait_ge(*act_conv.at(("raw", ct)))
                if ct >= 2:
                    v.wait_ge(*act_conv.at(("silu", ct - 2)))
                wt = G("conv")[:, 4 * ct:4 * ct + 4]
                src, dst = raw[ct % 2], cacc[ct % 2]
                then(dve_conv, v.tensor_scalar(dst, src[:, 3:3 + SEQ], wt[:, 3:4], None, ALU.mult))
                for j in range(3):
                    then(dve_conv, v.scalar_tensor_tensor(out=dst, in0=src[:, j:j + SEQ], scalar=wt[:, j:j + 1], in1=dst,
                                                          op0=ALU.mult, op1=ALU.add), ct if j == 2 else None)

            def per_head(ap):
                return ap.unsqueeze(1).to_broadcast([P, NT, H])

            def strength_and_decay():
                for k in range(2):
                    q, kk = G("lam")[:, 2 * k * DH:(2 * k + 1) * DH], G("lam")[:, (2 * k + 1) * DH:(2 * k + 2) * DH]
                    then(dve_gd, v.tensor_tensor(lamtmp, q, kk, ALU.mult))
                    then(dve_gd, v.tensor_reduce((nlam if k else lam2[:, 0:1]), lamtmp, AX.X, ALU.add), ("lam", k))
                v.wait_ge(*pe_proj.at("ba"))
                then(dve_gd, v.tensor_copy(ba, ps[7][:, 0:NT * 2 * H].rearrange("p (t c) -> p t c", t=NT)), "ba")
                then(dve_gd, v.tensor_tensor(spt, ba[:, :, H:2 * H], per_head(G("dt")), ALU.add))
                then(dve_gd, v.scalar_tensor_tensor(out=spe, in0=spt, scalar=-1.0, in1=spt, op0=ALU.mult, op1=ALU.min), "nabs")
                v.wait_ge(*act_gd.at("spe"))
                then(dve_gd, v.tensor_scalar(spe, spe, 1.0, None, ALU.add), "spe1")
                v.wait_ge(*act_gd.at("ln"))
                then(dve_gd, v.scalar_tensor_tensor(out=spt, in0=spt, scalar=0.0, in1=spe, op0=ALU.max, op1=ALU.add))
                then(dve_gd, v.scalar_tensor_tensor(out=gdec, in0=spt, scalar=-1.0, in1=per_head(ealog), op0=ALU.mult, op1=ALU.mult), "g")
                then(dve_gd, v.scalar_tensor_tensor(out=nlam, in0=lam2[:, 1:2], scalar=LAM_INIT, in1=lam2[:, 0:1],
                                                    op0=ALU.subtract, op1=ALU.subtract))

            def norms():
                v.wait_ge(*pe_gd.at(("ssq", 2 * H - 1)))
                then(dve_gd, v.tensor_scalar(nrm, ps[6][:, 0:NT * 2 * H].rearrange("p (t c) -> p t c", t=NT), EPS, None, ALU.add))
                then(dve_gd, v.reciprocal(k_s, nrm[:, :, H:2 * H]), "nrm")
                v.wait_ge(*act_gd.at("nrm"))
                then(dve_gd, v.reciprocal(nrm, nrm))
                then(dve_gd, v.tensor_tensor(k_s, k_s, beta, ALU.mult))
                then(dve_gd, v.tensor_tensor(v_s, nrm[:, :, H:2 * H], beta, ALU.mult))
                then(dve_gd, v.tensor_scalar(o_s, nrm[:, :, 0:H], P ** -0.5, None, ALU.mult))
                v.wait_ge(*act_gd.at("dec"))
                then(dve_gd, v.scalar_tensor_tensor(out=k_w, in0=k_s, scalar=-1.0, in1=eg, op0=ALU.mult, op1=ALU.mult))
                then(dve_gd, v.tensor_tensor(o_q, o_s, eg, ALU.mult), "coef")

            for ct in range(3 * H):
                conv(ct)
                if ct % 2 == 1 and (ct + 3) // 2 < DA:
                    w_split(v, (ct + 3) // 2, True)
                if ct == CT_BA + 2:
                    strength_and_decay()
                if ct == CT_NORM:
                    norms()
                if ct in (8, 10, 12):
                    bias_parts((ct - 8) // 2)
            then(dve_gd, v.tensor_scalar(G("subln"), G("subln"), (1.0 - LAM_INIT) / 2, None, ALU.mult))
            then(dve_gd, v.tensor_scalar(G("gd_g"), G("gd_g"), 1 / 4, None, ALU.mult))

            def bank4(b):
                return ps[b][:, :].rearrange("p (h n) -> p h n", h=4)

            for t in range(NT):
                if t > 0:
                    v.wait_ge(*pe_gd.at(("D", t - 1, 1)))
                then(dve_gd, v.tensor_tensor(gl, over_heads(C("later"), H), over_cols(gdec[:, t, :], P), ALU.mult), ("gl", t))
                for gr in range(2):
                    hs = slice(4 * gr, 4 * gr + 4)
                    v.wait_ge(*pe_gd.at(("V", t, gr)))
                    then(dve_gd, v.tensor_tensor(v_w[:, hs, :], bank4(6 + gr), over_cols(v_s[:, t, hs], P), ALU.mult), ("v", t, gr))
                for pr in range(4):
                    v.wait_ge(*pe_gd.at(("qk", t, pr)))
                    v.wait_ge(*pool_gd.at(("dT", t, pr // 2)))
                    if t > 0:
                        v.wait_ge(*pe_gd.at(("O", t - 1, 1)))
                    hs = slice(2 * pr, 2 * pr + 2)
                    then(dve_gd, v.tensor_tensor(qkd[:, hs, :, :], ps[2 + pr][:, :].rearrange("p (h c n) -> p h c n", h=2, c=2),
                                                 dT[:, hs, :].unsqueeze(2).to_broadcast([P, 2, 2, P]), ALU.mult), ("qkd", t, pr))
                for gr in range(2):
                    hs = slice(4 * gr, 4 * gr + 4)
                    v.wait_ge(*pe_gd.at(("Yt", t, gr)))
                    if t > 0:
                        v.wait_ge(*pool_gd.at(("o", t - 1, gr)) if t > 1 else dve_gd.last())
                    then(dve_gd, v.tensor_tensor(a_row[:, hs, :], bank4(gr), over_cols(k_s[:, t, hs], P), ALU.mult), ("a", t, gr))
                    then(dve_gd, v.tensor_tensor(tri[:, hs, :], a_row[:, hs, :], over_heads(C("neg_m0"), 4), ALU.mult))
                    then(dve_gd, v.tensor_tensor(tri[:, hs, :], tri[:, hs, :], over_heads(ident, 4), ALU.add), ("tri", t, 0, gr))
                for l in range(1, LEVELS):
                    for gr in range(2):
                        hs = slice(4 * gr, 4 * gr + 4)
                        if l < LEVELS - 1:
                            v.wait_ge(*pe_gd.at(("Y", t, l, gr)))
                            then(dve_gd, v.tensor_tensor(tri[:, hs, :], tri[:, hs, :], bank4(2 + gr), ALU.subtract), ("tri", t, l, gr))
                        v.wait_ge(*pe_gd.at(("YT", t, l, gr)))
                        then(dve_gd, v.tensor_tensor(triT[:, hs, :], triT[:, hs, :], bank4(4 + gr), ALU.subtract), ("triT", t, l, gr))
                if t > 0:
                    for gr in range(2):
                        hs = slice(4 * gr, 4 * gr + 4)
                        v.wait_ge(*pe_gd.at(("KS", t, gr)))
                        for h in range(4 * gr, 4 * gr + 4):
                            ins = v.scalar_tensor_tensor(out=w_rhs[:, h, :], in0=ps[6 + gr][:, (h % 4) * P:(h % 4 + 1) * P],
                                                         scalar=k_w[:, t, h:h + 1], in1=v_w[:, h, :], op0=ALU.mult, op1=ALU.add)
                        then(dve_gd, ins, ("w", t, gr))
                        v.wait_ge(*pe_gd.at(("QS", t, gr)))
                        if t > 1:
                            v.wait_ge(*pool_gd.at(("o", t - 1, gr)))
                        then(dve_gd, v.tensor_tensor(qs_s[:, hs, :], bank4(gr), over_cols(o_q[:, t, hs], P), ALU.mult), ("qs", t, gr))
                for gr in range(2):
                    hs = slice(4 * gr, 4 * gr + 4)
                    v.wait_ge(*act_gd.at(("P", t, gr)))
                    if t > 0:
                        v.wait_ge(*pe_gd.at(("dS", t - 1, 1)))
                    then(dve_gd, v.tensor_tensor(p_dec[:, hs, :], p_out[:, hs, :], over_cols(ed[:, t, hs], P), ALU.mult), ("pd", t, gr))
                for gr in range(2):
                    hs = slice(4 * gr, 4 * gr + 4)
                    v.wait_ge(*pe_gd.at(("O", t, gr)))
                    out = ob[:, t, gr * HALF:(gr + 1) * HALF].rearrange("p (h n) -> p h n", h=4)
                    then(dve_gd, v.tensor_tensor(out, bank4(6 + gr), over_cols(o_s[:, t, hs], P), ALU.mult), ("o", t, gr))
                if t < NT - 1:
                    for gr in range(2):
                        hs = slice(4 * gr, 4 * gr + 4)
                        v.wait_ge(*pe_gd.at(("dS", t, gr)))
                        if t == 0:
                            then(dve_gd, v.tensor_copy(state[:, hs, :], bank4(4 + gr)), ("S", t, gr))
                        else:
                            for h in range(4 * gr, 4 * gr + 4):
                                ins = v.scalar_tensor_tensor(out=state[:, h, :], in0=state[:, h, :], scalar=glast[:, t, h:h + 1],
                                                             in1=ps[4 + gr][:, (h % 4) * P:(h % 4 + 1) * P], op0=ALU.mult, op1=ALU.add)
                            then(dve_gd, ins, ("S", t, gr))
            dve_gd.marks["end"] = dve_gd.count

            v.wait_ge(*pool_gd.at("end"))
            cos = C("cos").rearrange("p (t j) -> p t j", t=NT)
            sin = C("sin").rearrange("p (t b j) -> p t b j", t=NT, b=2)
            w_split(v, DA, True)
            w_split(v, DA + 1, True)
            for t in range(NT):
                v.wait_ge(*pool_att.at(("sq", t)))
                then(dve_att, v.tensor_reduce(osq[:, t * H:(t + 1) * H], heads(sqm[t % 2]), AX.X, ALU.add), ("osq", t))
            then(dve_att, v.tensor_scalar(osq, osq, 1.0 / P, EPS, ALU.mult, ALU.add), "ovar")
            v.wait_ge(*act_att.at("ostd"))
            then(dve_att, v.reciprocal(osq, osq))
            for c in range(6):
                for t in range(NT):
                    if c == 1:
                        o = heads(ob[:, t, :])
                        then(dve_att, v.tensor_tensor(o, o, over_cols(osq[:, t * H:(t + 1) * H], P), ALU.mult))
                        then(dve_att, v.tensor_tensor(o, o, over_heads(G("gd_g"), H), ALU.mult))
                    if t % 2 == 1:
                        w_split(v, DA + 2 * c + 2 + t // 2, True)
                    if c >= 4:
                        continue
                    k = c * NT + t
                    v.wait_ge(*pe_proj.at(("da", c, t)))
                    if k >= 2:
                        v.wait_ge(*pool_att.at(("rope", (k - 2) // NT, (k - 2) % NT)))
                    x4 = ps[t][:, :].rearrange("p (g b j) -> p g b j", b=2, j=32)
                    r1, r2 = (r[k % 2].rearrange("p (g b j) -> p g b j", b=2, j=32) for r in (rope1, rope2))
                    v.tensor_tensor(r1, x4, cos[:, t, :].unsqueeze(1).unsqueeze(1).to_broadcast([P, 8, 2, 32]), ALU.mult).then_inc(*dve_att.next())
                    for b in range(2):
                        ins = v.tensor_tensor(r2[:, :, b, :], x4[:, :, 1 - b, :], sin[:, t, b, :].unsqueeze(1).to_broadcast([P, 8, 32]), ALU.mult)
                        ins.then_inc(*dve_att.next(("rope", c, t) if b else None))

            def diff(n):
                i, k = n % NT, 2 * (n % 2)
                for c in range(2):
                    v.wait_ge(*act_att.at(("exp", n, c)))
                if n >= 2:
                    v.wait_ge(*act_att.at(("out", n - 2)))
                    v.wait_ge(*pe_att.at(("wT", n - 2)))
                then(dve_att, v.reciprocal(recs[:, k:k + 2], esum[:, k:k + 2]))
                rr = ratio[:, n % 2:n % 2 + 1]
                then(dve_att, v.scalar_tensor_tensor(out=rr, in0=esum[:, k:k + 1], scalar=recs[:, k + 1:k + 2], in1=nlam,
                                                     op0=ALU.mult, op1=ALU.mult))
                cols = slice(0, (i + 1) * P)
                then(dve_att, v.scalar_tensor_tensor(out=wdiff[n % 2][:, cols], in0=probs[n % 2][1][:, cols], scalar=rr,
                                                     in1=probs[n % 2][0][:, cols], op0=ALU.mult, op1=ALU.add), ("diff", n))

            NS = H * NT
            v.wait_ge(*pe_att.at(("qkT", 3, 3)))
            v.wait_ge(*pool_att.at("end"))

            def gates(k):
                for u in ended(k, KC):
                    (j, q), t = divmod(u // NT, 4), u % NT
                    if j == 1:
                        continue
                    e, cols = gate_s[u % 2][:, :], slice(q * QUART, (q + 1) * QUART)
                    v.wait_ge(*act_att.at(("gate", u)))
                    o = ob[:, t, cols]
                    if j == 0:
                        then(dve_att, v.scalar_tensor_tensor(out=e, in0=e, scalar=1.0, in1=ps[6 + u % 2][:, 0:QUART], op0=ALU.add, op1=ALU.mult))
                        then(dve_att, v.tensor_tensor(o, o, e, ALU.mult), ("gate", u))
                    else:
                        then(dve_att, v.scalar_tensor_tensor(out=o, in0=e, scalar=1.0, in1=o, op0=ALU.add, op1=ALU.mult), ("gate", u))
                for g in ended(k, NT * KC):
                    w_split(v, GATE + 2 + g, True)

            for n in range(NS + 1):
                gates(3 * n - 1)
                if n >= 1:
                    diff(n - 1)
                if n < NS:
                    i = n % NT
                    k = 2 * (n % 2)
                    for c in range(2):
                        v.wait_ge(*pe_att.at(("sc", n, c)))
                    diag = banks[:, k:k + 2, i * P:(i + 1) * P]
                    then(dve_att, v.tensor_tensor(diag, diag, over_heads(causal, 2), ALU.add))
                    then(dve_att, v.tensor_reduce(mx[:, k:k + 2], banks[:, k:k + 2, 0:(i + 1) * P], AX.X, ALU.max))
                    then(dve_att, v.tensor_scalar(nmx[:, k:k + 2], mx[:, k:k + 2], -DH ** -0.5, None, ALU.mult), ("max", n))
                gates(3 * n)
                gates(3 * n + 1)

            v.wait_ge(*act_att.at(("out", NS - 1)))
            then(dve_mrg, v.tensor_scalar(oasq, oasq, 1.0 / P, EPS, ALU.mult, ALU.add), "ovar")
            v.wait_ge(*act_mrg.at("ostd"))
            then(dve_mrg, v.reciprocal(oasq, oasq))
            v.wait_ge(*pool_mrg.at(("ga", NT - 1)))

            def merged_lo(kc):
                v.wait_ge(*act_mrg.at(("mT", kc)))
                v.tensor_tensor(mT_lo[:, kc, :], ps[4 + kc % 4][:, :], mT_hi[:, kc, :], ALU.subtract).then_inc(*dve_mrg.next(("mT", kc)))

            for h in range(H):
                for i in range(NT):
                    o = qaT[:, h, i * P:(i + 1) * P]
                    ins = v.scalar_tensor_tensor(out=o, in0=o, scalar=oasq[:, h * NT + i:h * NT + i + 1], in1=ga[:, i, h * P:(h + 1) * P],
                                                 op0=ALU.mult, op1=ALU.mult)
                then(dve_mrg, ins)
                m = ob[:, :, h * P:(h + 1) * P]
                then(dve_mrg, v.tensor_tensor(m, m, qaT[:, h, :].rearrange("p (t n) -> p t n", t=NT), ALU.add), ("m", h))
                if h:
                    merged_lo(h - 1)
            merged_lo(H - 1)
            for s in (OUT + 2, OUT + 3):
                w_split(v, s, True)
            v.wait_ge(ld_x2.sem, 16)
            v.wait_ge(ld_g.sem, 48)
            for c in range(2):
                for t in range(NT):
                    v.wait_ge(*pe_proj.at(("out", c, t)))
                    xc = xs[:, t, c * HALF:(c + 1) * HALF]
                    v.tensor_tensor(xc, xc, ps[t][:, :], ALU.add).then_inc(*dve_mrg.next(("x1", c, t)))
                    if c == 0:
                        continue
                    v.wait_ge(*act_rt.at(("ss", t)))
                    sst, rst = ss[:, t:t + 1], rstd[:, t:t + 1]
                    then(dve_rt, v.tensor_scalar(sst, sst, 1.0 / D, EPS, ALU.mult, ALU.add), ("var", t))
                    v.wait_ge(*act_rt.at(("std", t)))
                    then(dve_rt, v.reciprocal(rst, rst))
                    v.scalar_tensor_tensor(out=h2[:, t, :], in0=xs[:, t, :], scalar=rst, in1=g2,
                                           op0=ALU.mult, op1=ALU.mult).then_inc(*dve_rt.next(("h2", t)))

            lg = rt_at("lg").rearrange("p (t e) -> p t e", t=NT)
            top = rt_at("top").rearrange("p (t k) -> p t k", t=NT)
            tix = rt_at("tix").bitcast(U32).rearrange("p (t k) -> p t k", t=NT)
            gw3 = gw.rearrange("p (t k) -> p t k", t=NT)
            v.wait_ge(*pe_rt.at("logits"))
            then(dve_rt, v.tensor_tensor(lg, ps[0][:, 0:NT * NE].rearrange("p (t e) -> p t e", t=NT),
                                         G("router_b").unsqueeze(1).to_broadcast([P, NT, NE]), ALU.add))
            for t in range(NT):
                then(dve_rt, v.max(top[:, t, :], lg[:, t, :]))
                then(dve_rt, v.max_index(tix[:, t, :], top[:, t, :], lg[:, t, :]))
            then(dve_rt, v.tensor_tensor(gw3, top[:, :, 0:TOPK], top[:, :, 0:1].to_broadcast([P, NT, TOPK]), ALU.subtract), "gsub")
            tixf, hot = rt_at("tixf"), rt_at("hot").rearrange("p (a e) -> p a e", e=NE)
            then(dve_rt, v.tensor_copy(tixf.rearrange("p (t k) -> p t k", t=NT), tix[:, :, 0:TOPK]))
            then(dve_rt, v.tensor_tensor(hot, C("iota").unsqueeze(1).to_broadcast([P, NT * TOPK, NE]), over_cols(tixf, NE), ALU.is_equal))
            mask = rt_at("mask").rearrange("p (t e) -> p t e", t=NT)
            then(dve_rt, v.tensor_reduce(mask, rt_at("hot").rearrange("p (t k e) -> p t e k", t=NT, k=TOPK), AX.X, ALU.add), "mask")
            gsum = rt_at("gsum")
            v.wait_ge(*act_rt.at("gexp"))
            then(dve_rt, v.tensor_reduce(gsum, gw3, AX.X, ALU.add))
            then(dve_rt, v.reciprocal(gsum, gsum))
            then(dve_rt, v.tensor_tensor(gw3, gw3, over_cols(gsum, TOPK), ALU.mult))
            cnt, xb, inc, shift = rt_at("cnt"), rt_at("xb"), rt_at("inc"), rt_at("shift")
            v.wait_ge(*pe_rt.at("rank"))
            then(dve_rt, v.tensor_copy(cnt, ps[2][:, 0:NE]))
            then(dve_rt, v.tensor_scalar(xb, cnt, float(P), None, ALU.is_gt))
            for m in range(2, NT):
                then(dve_rt, v.scalar_tensor_tensor(out=xb, in0=cnt, scalar=float(m * P), in1=xb, op0=ALU.is_gt, op1=ALU.add))
            then(dve_rt, v.tensor_tensor_scan(inc, C("ones")[:, 0:NE], xb, 0.0, ALU.mult, ALU.add))
            then(dve_rt, v.tensor_tensor(shift, inc, xb, ALU.subtract))
            then(dve_rt, v.scalar_tensor_tensor(out=shift, in0=shift, scalar=float(P), in1=C("base"), op0=ALU.mult, op1=ALU.subtract))
            then(dve_rt, v.tensor_scalar(shift, shift, float(P * (NE - 1)), None, ALU.add))
            big = rt_at("big").rearrange("p (b e) -> p b e", e=NE)
            then(dve_rt, v.tensor_tensor(big, over_cols(C("iota")[:, 0:16], NE), inc.unsqueeze(1).to_broadcast([P, 16, NE]), ALU.is_ge))
            bef = rt_at("bef")
            then(dve_rt, v.tensor_reduce(bef, big, AX.X, ALU.add))
            then(dve_rt, v.tensor_scalar(bef, bef, float(NE - 1), None, ALU.min))
            then(dve_rt, v.tensor_copy(bef[:, 15:16], inc[:, NE - 1:NE]))
            then(dve_rt, v.tensor_copy(be, bef), "be")
            rank, dest = rt_at("rank").rearrange("p (t e) -> p t e", t=NT), rt_at("dest").rearrange("p (t e) -> p t e", t=NT)
            then(dve_rt, v.tensor_copy(rank, ps[1][:, 0:NT * NE].rearrange("p (t e) -> p t e", t=NT)))
            then(dve_rt, v.scalar_tensor_tensor(out=dest, in0=rank, scalar=float(P), in1=shift.unsqueeze(1).to_broadcast([P, NT, NE]),
                                                op0=ALU.is_ge, op1=ALU.mult))
            then(dve_rt, v.tensor_tensor(dest, dest, rank, ALU.add))
            then(dve_rt, v.tensor_tensor(dest, dest, C("base").unsqueeze(1).to_broadcast([P, NT, NE]), ALU.add))
            hot4, dk = rt_at("hot").rearrange("p (t k e) -> p t k e", t=NT, k=TOPK), rt_at("dk")
            then(dve_rt, v.tensor_tensor(hot4, hot4, dest.unsqueeze(2).to_broadcast([P, NT, TOPK, NE]), ALU.mult))
            then(dve_rt, v.tensor_reduce(dk, hot, AX.X, ALU.add))
            then(dve_rt, v.tensor_copy(y_idx, dk))
            blk, blkf = rt_at("blk").bitcast(I32), rt_at("blkf")
            then(dve_rt, v.tensor_scalar(blk, y_idx, 7, None, ALU.logical_shift_right))
            then(dve_rt, v.tensor_copy(blkf, blk))
            then(dve_rt, v.tensor_scalar(blkf, blkf, float(-(P * RT_W - 1)), None, ALU.mult))
            then(dve_rt, v.scalar_tensor_tensor(out=blkf, in0=dk, scalar=float(RT_W), in1=blkf, op0=ALU.mult, op1=ALU.add))
            then(dve_rt, v.tensor_copy(rt_at("scat").bitcast(I32), blkf), "dest")
            dve_rt.marks["end"] = dve_rt.count

            def to_lo(dst, hi, k, bank, value):
                v.wait_ge(a_tr.sem, value)
                cols = slice(k * HALF, (k + 1) * HALF)
                v.tensor_tensor(dst[:, cols], ps[bank][:, :], hi[:, cols], ALU.subtract).then_inc(v_tr.sem, 1)

            for half in range(2):
                to_lo(xT_lo, xT_hi, half, 7 - half, half + 1)

            def w_parts(i, chunks):
                for c in chunks:
                    if c in ON_POOL:
                        continue
                    v.wait_ge(a_hi.sem, 12 * i + c + 1)
                    v.tensor_tensor(w_lo[c % 4][:, :], raw_chunk(c), w_hi[c % 4][:, :], ALU.subtract).then_inc(v_lo.sem, 1)

            def swiglu(i, hf):
                n = 8 * i + 4 * hf + 8
                v.wait_ge(e_used.sem, 12 * i + 4 * hf + 6)
                v.wait_ge(v_act.sem, n)
                v.tensor_scalar(gm[hf], ps[2 * hf][:, :], LIMIT, None, ALU.min).then_inc(v_act.sem, 1)
                v.wait_ge(e_used.sem, 12 * i + 4 * hf + 8)
                v.tensor_scalar(um[hf], ps[2 * hf + 1][:, :], LIMIT, -LIMIT, ALU.min, ALU.max).then_inc(v_act.sem, 1)
                v.wait_ge(v_act.sem, n + 2)
                v.scalar_tensor_tensor(out=um[hf], in0=um[hf], scalar=1.0, in1=gm[hf], op0=ALU.add, op1=ALU.mult).then_inc(v_act.sem, 1)
                v.wait_ge(v_act.sem, n + 3)
                v.wait_ge(a_sig.sem, 2 * i + hf + 1)
                v.wait_ge(e_tr.sem, 4 * i + 2)
                v.tensor_tensor(av[hf], um[hf], sg[hf], ALU.mult).then_inc(v_act.sem, 1)

            def result(i):
                v.wait_ge(e_used.sem, 12 * i + 16)
                v.wait_ge(st_y.sem, 16 * i + 16)
                v.tensor_copy(ys[:, 0:HALF], ps[4][:, :]).then_inc(v_y.sem, 1)

            def body(i, before=False):
                w_parts(i, range(0, 3))
                if before:
                    result(i - 1)
                w_parts(i, range(3, 8))
                swiglu(i, 0)
                w_parts(i, range(8, 10))
                to_lo(avT_lo, avT_hi, 0, 6, 4 * i + 3)
                w_parts(i, range(10, 11))
                swiglu(i, 1)
                to_lo(xT_lo, xT_hi, 0, 7, 4 * i + 4)
                to_lo(xT_lo, xT_hi, 1, 6, 4 * i + 5)
                w_parts(i, range(11, 12))
                to_lo(avT_lo, avT_hi, 1, 7, 4 * i + 6)

            body(0)
            with v.Fori(1, NE) as i:
                body(i, True)
            result(NE - 1)
            n_extra = v.value_load(be[0:1, 15:16], min_val=0, max_val=EXTRA)
            with v.If(n_extra > 0):
                with v.Fori(NE, NBLK) as i:
                    body(i)
                    result(i)

            for t in range(NT):
                for k in range(TOPK):
                    n = t * TOPK + k
                    v.wait_ge(ld_row[n % 6].sem, 16 * (n // 6 + 1))
                    then(dve_fin, v.scalar_tensor_tensor(out=xs[:, t, :], in0=ring[:, n % 6, 0:D], scalar=gw[:, n:n + 1], in1=xs[:, t, :],
                                                         op0=ALU.mult, op1=ALU.add), ("row", n))
                dve_fin.marks[("sum", t)] = dve_fin.count
                v.wait_ge(*act_fin.at(("ss", t)))
                then(dve_fin, v.tensor_scalar(ss[:, t:t + 1], ss[:, t:t + 1], 1.0 / D, EPS, ALU.mult, ALU.add), ("var", t))
                v.wait_ge(*act_fin.at(("std", t)))
                then(dve_fin, v.reciprocal(rstd[:, t:t + 1], rstd[:, t:t + 1]))
                v.scalar_tensor_tensor(out=xs[:, t, :], in0=xs[:, t, :], scalar=rstd[:, t:t + 1], in1=gf,
                                       op0=ALU.mult, op1=ALU.mult).then_inc(*dve_fin.next(("out", t)))

    return {name: s.marks for name, s in signals.items()}


def constants():
    i = np.arange(P)
    c = np.zeros((P, NCST), np.float32)

    def put(name, a):
        lo, hi = CST[name]
        c[:, lo:hi] = np.asarray(a, np.float32).reshape(P, hi - lo)

    put("ident", np.eye(P))
    put("upper", i[:, None] <= i[None, :])
    put("later", i[:, None] > i[None, :])
    put("before", i[:, None] < i[None, :])
    put("ones", np.ones((P, P)))

    def between(l, row, col):
        return (row >> (l + 1) == col >> (l + 1)) & ((row >> l) & 1 == 1) & ((col >> l) & 1 == 0)

    put("neg_m0", np.where(between(0, i[:, None], i[None, :]), -1.0, 0.0))
    put("masks", np.concatenate([between(l, i[None, :], i[:, None]) for l in range(1, LEVELS)], axis=1))
    put("causal", np.where(i[None, :] <= i[:, None], 0.0, NEG))
    inv = (1.0 / (np.float32(10000.0) ** (np.arange(0, DH, 2, dtype=np.float32) / np.float32(DH)))).astype(np.float32)
    ang = np.arange(SEQ, dtype=np.float32)[:, None] * inv[None, :]
    cos, sin = np.cos(ang), np.sin(ang)
    put("cos", cos.reshape(NT, P, 32).transpose(1, 0, 2))
    put("sin", np.stack([-sin, sin], axis=1).reshape(NT, P, 2, 32).transpose(1, 0, 2, 3))
    put("iota", np.broadcast_to(np.arange(NE), (P, NE)))
    put("base", np.broadcast_to(P * np.arange(NE), (P, NE)))
    put("onehot", i[:, None] % NE == np.arange(NE)[None, :])
    tok = np.repeat(np.arange(NT)[None, :] * P + i[:, None], TOPK, axis=1).astype(np.int32)
    return c, tok


_IO = dict(w_in="w_in", w_out="w_out", router_w="router_w", b_gate="exp_b_gate", b_up="exp_b_up", b_down="exp_b_down",
           w_gate="exp_w_gate", w_up="exp_w_up", w_down="exp_w_down")


def kernel(**inputs):
    import concourse.bacc as bacc
    from concourse.bass_utils import run_bass_kernel_spmd

    x = {k: np.asarray(v) for k, v in inputs.items()}

    def rows(a):
        return np.broadcast_to(a.reshape(1, -1), (P, a.size))

    cst, tok = constants()
    conv = x["gd_conv_w"][0].reshape(4, 24, P).transpose(2, 1, 0).reshape(P, 96)
    par = np.concatenate([x["mix_norm_g"].reshape(KC, P).T, conv, rows(x["gd_a_log"]), rows(x["gd_dt_bias"]), rows(x["router_b"]),
                          rows(x["da_lambda_q1"]), rows(x["da_lambda_k1"]), rows(x["da_lambda_q2"]), rows(x["da_lambda_k2"]),
                          rows(x["da_subln_g"]), rows(x["gd_norm_g"])], axis=1)
    arrays = {"x": x["x"].reshape(SEQ, D), "cst": cst, "par": np.ascontiguousarray(par), "tokid": tok,
              "ffn_g": x["ffn_norm_g"].reshape(1, D), "final_g": x["final_norm_g"].reshape(1, D)}
    for name, source in _IO.items():
        arrays[name] = x[source][0]

    def build(known):
        nc = bacc.Bacc("TRN2", target_bir_lowering=False, num_devices=1)
        io = {name: nc.dram_tensor(f"in_{name}", a.shape, mybir.dt.from_np(a.dtype), kind="ExternalInput").ap()
              for name, a in arrays.items()}
        io["out"] = nc.dram_tensor("out_rows", (SEQ, D), F32, kind="ExternalOutput").ap()
        return nc, layer_kernel(nc, io, known)

    _, counts = build({})
    nc, _ = build(counts)
    got = run_bass_kernel_spmd(nc, [{f"in_{n}": a for n, a in arrays.items()}], core_ids=[0])
    return got.results[0]["out_rows"].reshape(x["x"].shape)
```

```python
import math
from contextlib import ExitStack

import numpy as np

import concourse.bass as bass
from concourse import mybir

F32 = mybir.dt.float32
F32R = mybir.dt.float32r
BF16 = mybir.dt.bfloat16
I32 = mybir.dt.int32
U32 = mybir.dt.uint32
ALU = mybir.AluOpType
ACT = mybir.ActivationFunctionType
AX = mybir.AxisListType

P = 128
D = 1024
SEQ = 512
NT = SEQ // P
KC = D // P
HALF = 512
QUART = HALF // 2
CT_BA = 3
CT_NORM = 19
EARLY = 5
H = 8
DH = 64
NE, TOPK = 32, 4
LEVELS = 7
EXTRA = SEQ * TOPK // (P + 1)
NBLK = NE + EXTRA
RT_W = NBLK + 1
EPS = 1e-6
LAM_INIT = 0.8 - 0.6 * math.exp(0.0)
NEG = -1e30
LIMIT, ALPHA = 7.0, 1.702

C_DAQ, C_DAK, C_DAV, C_GDQ = 0, D, 2 * D, 3 * D
C_Z, C_BA, C_GA, C_GB = 6 * D, 7 * D, 7 * D + 2 * H, 8 * D + 2 * H
IN_DIM = 9 * D + 2 * H

_widths = dict(ident=P, upper=P, later=P, before=P, ones=P, neg_m0=P, masks=(LEVELS - 1) * P, causal=P,
               cos=NT * 32, sin=NT * DH, iota=NE, base=NE, onehot=NE)
CST, _at = {}, 0
for _k, _w in _widths.items():
    CST[_k] = (_at, _at + _w)
    _at += _w
NCST = _at
_widths = dict(mix_g=KC, conv=24 * 4, a_log=H, dt=H, router_b=NE, lam=4 * DH, subln=P, gd_g=P)
PAR, _at = {}, 0
for _k, _w in _widths.items():
    PAR[_k] = (_at, _at + _w)
    _at += _w
NPAR = _at


class Signal:

    def __init__(self, sem, known):
        self.sem, self.known, self.count, self.marks = sem, known, 0, {}

    def next(self, key=None, by=1):
        self.count += by
        self.marks[key] = self.count
        return self.sem, by

    def at(self, key):
        return self.sem, self.known.get(key, 1)

    def last(self):
        return self.sem, self.count


def layer_kernel(nc, io, known):
    signals = {}
    with ExitStack() as ctx:
        def sb(name, shape, dt=F32):
            return ctx.enter_context(nc.sbuf_tensor(name, shape, dt))

        def signal(name):
            s = Signal(ctx.enter_context(nc.semaphore(name)), known.get(name, {}))
            signals[name] = s
            return s

        h2_dram = nc.dram_tensor("h2_rows", [SEQ, D], F32, kind="Internal").ap()
        rowtok_dram = nc.dram_tensor("row_token", [P * RT_W, 1], I32, kind="Internal").ap()
        y_dram = nc.dram_tensor("expert_rows", [NBLK * P, D], F32, kind="Internal").ap()

        cst = sb("cst", [P, NCST])
        par = sb("par", [P, NPAR])
        tokid = sb("tokid", [P, NT * TOPK], I32)
        arena_at = -(-nc.sbuf_base // 32) * 32
        arena = sb("arena", [P, 46 * 1024])

        def place(name, word, shape, dt=F32):
            return nc.alloc_sbuf_tensor_at(name, shape, dt, offset=arena_at + 4 * word)

        K = 1024
        ring = place("ring", 0, [P, 6, 2 * K])
        ob = place("ob", 20 * K, [P, NT, D])
        x0 = place("x0", 20 * K, [P, NT, D])
        xs = place("xs", 40 * K, [P, NT, D])
        hT_hi = place("hT_hi", 12 * K, [P, KC, SEQ], F32R)
        hT_lo = place("hT_lo", 16 * K, [P, KC, SEQ], F32R)
        mT_hi, mT_lo = hT_hi, hT_lo
        h2T = place("h2T", 24 * K, [P, KC, SEQ])
        scratch = place("scratch", 28 * K, [P, 18 * K])
        raw_w = [place(f"raw_w{r}", w * K, [P, 2 * K]) for r, w in enumerate((24, 26, 44))]
        wba_hi = place("wba_hi", 44 * K - 256, [P, KC, 2 * H], F32R)
        wba_lo = place("wba_lo", 44 * K - 128, [P, KC, 2 * H], F32R)
        CHUNK = 2048
        w_hi = [place(f"w_hi{i}", w * K, [P, CHUNK], F32R) for i, w in enumerate((28, 32, 12, 16))]
        w_lo = [place(f"w_lo{i}", w * K, [P, CHUNK], F32R) for i, w in enumerate((30, 34, 14, 18))]
        xT_hi, xT_lo, avT_hi, avT_lo = (place(n, w * K, [P, D], F32R) for n, w in (
            ("xT_hi", 39), ("xT_lo", 20), ("avT_hi", 21), ("avT_lo", 22)))
        btab = sb("btab", [96, 3 * D], BF16)
        sel = sb("sel", [96, NE], BF16)
        wba = sb("wba", [P, KC, 2 * H])
        gate_s = [sb(f"gate{k}", [P, QUART]) for k in range(2)]
        small = sb("small", [P, 1024])

        def C(name):
            a, b = CST[name]
            return cst[:, a:b]

        def G(name):
            a, b = PAR[name]
            return par[:, a:b]

        small_at = [0]

        def sm(width):
            a = small_at[0]
            small_at[0] += width
            assert small_at[0] <= 1024
            return small[:, a:a + width]

        ident = C("ident")
        causal = C("causal")

        def over_heads(ap, n):
            return ap.unsqueeze(1).to_broadcast([P, n, ap.shape[1]])

        def over_cols(ap, n):
            return ap.unsqueeze(2).to_broadcast([P, ap.shape[1], n])

        q_place = ring[:, :, :].rearrange("p s n -> p (s n)")
        qkvT = q_place.rearrange("p (c t) -> p c t", c=24)
        xn = q_place[:, 0:4 * K].rearrange("p (t c) -> p t c", t=NT)
        qaT = q_place[:, 0:4 * K].rearrange("p (h t) -> p h t", h=H)
        kaT = q_place[:, 4 * K:8 * K].rearrange("p (h t) -> p h t", h=H)
        va = q_place[:, 8 * K:12 * K].rearrange("p (t c) -> p t c", t=NT)
        h2 = ob[:, :, :]

        def at_k(k, n=K):
            a = round((k - 28) * K)
            return scratch[:, a:a + n]

        def heads(ap):
            return ap.rearrange("p (h n) -> p h n", h=H)

        gdn = [scratch[:, k * K:(k + 1) * K] for k in range(18)]
        k_tok, v_w, aT, tri, triT, xlev, gl, dT = (heads(gdn[k]) for k in range(8))
        btm = [heads(gdn[8]), heads(gdn[9])]
        state, w_rhs, p_out, p_dec = (heads(gdn[k]) for k in range(10, 14))
        qs_s, a_row = heads(gdn[14]), heads(gdn[15])
        qkd = scratch[:, 16 * K:18 * K].rearrange("p (h c n) -> p h c n", h=H, c=2)
        raw = [scratch[:, 8 * K + k * 520:8 * K + k * 520 + SEQ + 3] for k in range(2)]
        cacc = [scratch[:, 8 * K + 1040 + k * SEQ:8 * K + 1040 + (k + 1) * SEQ] for k in range(2)]
        sqb = [scratch[:, 8 * K + 2064 + k * SEQ:8 * K + 2064 + (k + 1) * SEQ] for k in range(2)]
        bias_st = [at_k(39.25 + j)[0:96, :] for j in range(3)]
        bias_hi, bias_mid, bias_lo = (at_k(42.25 + j / 2, K // 2)[0:96, :].bitcast(BF16) for j in range(3))
        baT = at_k(42.25, HALF)[0:2 * H, :]
        rope1 = [at_k(38 + k / 2, HALF) for k in range(2)]
        rope2 = [at_k(39 + k / 2, HALF) for k in range(2)]
        roped = [at_k(40 + 2 * k, 2 * K).rearrange("p (t c) -> p t c", t=NT) for k in range(2)]
        probs = [[at_k(36 + k + c / 2, HALF) for c in range(2)] for k in range(2)]
        wdiff = [at_k(38 + k / 2, HALF) for k in range(2)]
        wT = [at_k(39 + k / 2, HALF) for k in range(2)]
        sqm = [at_k(36 + k) for k in range(2)]
        ga = at_k(40, 4 * K).rearrange("p (t c) -> p t c", t=NT)
        gf, g2, junk = at_k(36), at_k(37), at_k(39)
        rw = at_k(38, KC * NE).rearrange("p (c e) -> p c e", c=KC)
        rank_row = at_k(38.25, P)
        rt = place("rt", 44 * K, [P, 2 * K])
        rt_cols, n = {}, 0
        for name, w in dict(scat=16, lg=128, top=32, tix=32, tixf=16, hot=512, mask=128, gsum=4, cnt=32, xb=32, inc=32, shift=32,
                            big=512, bef=16, rank=128, dest=128, dk=16, blk=16, blkf=16, tokf=16).items():
            rt_cols[name] = (n, n + w)
            n += w
        assert n <= 2 * K

        def rt_at(name):
            lo, hi = rt_cols[name]
            return rt[:, lo:hi]

        xg = at_k(37)
        gm, sg, um, av = ([raw_ap[:, k * HALF:(k + 1) * HALF] for k in range(2)] for raw_ap in
                          (place(n, w * K, [P, D]) for n, w in (("gm", 24), ("sg", 25), ("um", 26), ("av", 27))))
        ys = place("ys", 23 * K, [P, D])
        junk_fin = place("junk_fin", 26 * K, [P, D])

        banks = ctx.enter_context(nc.psum_tensor("banks", [P, 8, HALF], F32))
        ps = [banks[:, b, :] for b in range(8)]

        ss, rstd = sm(NT), sm(NT)
        ba = sm(NT * 2 * H).rearrange("p (t c) -> p t c", t=NT)
        beta, gdec, spt, spe = (sm(NT * H).rearrange("p (t h) -> p t h", t=NT) for _ in range(4))
        ealog = sm(H)
        dec = sm(3 * NT * H)
        eg, ed, glast = (dec[:, k * NT * H:(k + 1) * NT * H].rearrange("p (t h) -> p t h", t=NT) for k in range(3))
        nrm = sm(NT * 2 * H).rearrange("p (t c) -> p t c", t=NT)
        k_s, v_s, k_w, o_q, o_s = (sm(NT * H).rearrange("p (t h) -> p t h", t=NT) for _ in range(5))
        lam2, nlam = sm(2), sm(1)
        mx, nmx, esum, recs, ratio = sm(4), sm(4), sm(4), sm(4), sm(2)
        osq, oasq = sm(NT * H), sm(NT * H)
        e_idx = sm(RT_W).bitcast(I32)
        e_idx1 = sm(1).bitcast(I32)
        e_held, e_idx0 = sm(1).bitcast(I32), sm(1).bitcast(I32)
        y_idx = sm(NT * TOPK).bitcast(I32)
        gw = sm(NT * TOPK)
        be = sm(16).bitcast(I32)
        lamtmp = sm(DH)

        ld_x = [signal(f"ld_tile{t}") for t in range(NT)]
        ld_cst, ld_ba, ld_bias, ld_rt, ld_x2, ld_g = (signal(n) for n in (
            "ld_cst", "ld_ba", "ld_bias", "ld_rt", "ld_x2", "ld_g"))
        ld_w = [signal(f"ld_w{s}") for s in range(3)]
        w_hi_done, w_lo_done, w_lo_pool = signal("w_hi_done"), signal("w_lo_done"), signal("w_lo_pool")
        pe_hT, pe_proj, pe_gd, pe_att, pe_mrg, pe_rt = (signal(n) for n in (
            "pe_hT", "pe_proj", "pe_gd", "pe_att", "pe_mrg", "pe_rt"))
        act_pre, act_conv, act_gd, act_att, act_mrg, act_rt = (signal(n) for n in (
            "act_pre", "act_conv", "act_gd", "act_att", "act_mrg", "act_rt"))
        dve_pre, dve_conv, dve_gd, dve_att, dve_mrg, dve_rt, dve_fin = (signal(n) for n in (
            "dve_pre", "dve_conv", "dve_gd", "dve_att", "dve_mrg", "dve_rt", "dve_fin"))
        pool_pre, pool_gd, pool_att, pool_mrg = (signal(n) for n in ("pool_pre", "pool_gd", "pool_att", "pool_mrg"))
        st_h2, st_rt, st_y, st_out, act_fin = (signal(n) for n in ("st_h2", "st_rt", "st_y", "st_out", "act_fin"))
        ld_row = [signal(f"ld_row{s}") for s in range(6)]
        x_rows, x_idx = signal("x_rows"), signal("x_idx")
        e_tr = signal("e_tr")
        ld_e = [signal(f"ld_e{r}") for r in range(6)]
        e_used, a_hi, v_lo, p_lo = signal("e_used"), signal("a_hi"), signal("v_lo"), signal("p_lo")
        v_act, v_y, v_tr = signal("v_act"), signal("v_y"), signal("v_tr")
        a_sig, a_tr, a_y = signal("a_sig"), signal("a_tr"), signal("a_y")

        columns = [("w_in", c0 + QUART * j) for c0, n in ((C_GDQ, 12), (C_DAQ, 12), (C_Z, 4), (C_GA, 4), (C_GB, 4)) for j in range(n)]
        columns += [("w_out", QUART * j) for j in range(4)]
        DA, GATE, OUT = 12, 24, 36

        def by_rows(ap):
            return ap.rearrange("p (c n) -> p c n", c=KC)

        def by_pool(s):
            return GATE + 2 <= s < OUT + 2

        def w_done(s):
            return (w_lo_pool if by_pool(s) else w_lo_done).at(s)

        def w_split(e, s, small):
            if small:
                e.wait_ge(*w_hi_done.at(s))
                e.tensor_tensor(w_lo[s % 2][:, :], raw_w[s % 3][:, :], w_hi[s % 2][:, :], ALU.subtract).then_inc(*(w_lo_pool if by_pool(s) else w_lo_done).next(s))
            else:
                e.wait_ge(ld_w[s % 3].sem, 16 * (s // 3 + 1))
                if s >= 2:
                    e.wait_ge(*pe_proj.at(("used", s - 2)))
                e.activation(w_hi[s % 2][:, :], raw_w[s % 3][:, :], ACT.Copy).then_inc(*w_hi_done.next(s))

        NS = H * NT
        GATE_ROWS = 12 * NT * KC // (3 * NS)

        def ended(k, rows):
            return range(GATE_ROWS * k // rows, GATE_ROWS * (k + 1) // rows) if 0 <= k < 3 * NS else ()

        block = ctx.enter_context(nc.Block())

        def chunk_source(e, c):
            if c < 8:
                w, hf, rows = io["w_up" if c // 2 % 2 else "w_gate"], c // 4, D // 2
                return w[bass.ds(e, 1), c % 2 * rows:(c % 2 + 1) * rows, hf * HALF:(hf + 1) * HALF].rearrange("e (c p) n -> p (e c) n", p=P)
            rows = D // 4
            return io["w_down"][bass.ds(e, 1), (c - 8) * rows:(c - 7) * rows, :].rearrange("e (c p) n -> p (e c) n", p=P)

        def raw_chunk(c):
            return ring[:, c % 6, :]

        def on_pool(i):
            return (0, 1, 2) if isinstance(i, int) and i == 0 else (1, 5, 9)

        def small_part(i, c):
            mine = [k for k in range(12) if (k in on_pool(i)) == (c in on_pool(i))]
            return (p_lo if c in on_pool(i) else v_lo).sem, len(mine) * i + mine.index(c) + 1

        @block.sync
        def _(sp):
            for t in range(NT):
                sp.dma_start(x0[:, t, :], io["x"].rearrange("(t p) c -> p t c", p=P)[:, t, :]).then_inc(ld_x[t].sem, 16)
            sp.dma_start(cst[:, :], io["cst"]).then_inc(ld_cst.sem, 16)
            sp.dma_start(par[:, :], io["par"]).then_inc(ld_cst.sem, 16)
            sp.dma_start(tokid[:, :], io["tokid"]).then_inc(ld_cst.sem, 16)
            for s, (name, c0) in enumerate(columns):
                if s >= 3:
                    sp.wait_ge(*w_done(s - 3))
                if s == DA + 2:
                    sp.wait_ge(*dve_gd.at("end"))
                    sp.wait_ge(*pool_gd.at("end"))
                sp.dma_start(by_rows(raw_w[s % 3][:, :]), io[name][:, c0:c0 + QUART].rearrange("(c p) n -> p c n", p=P)).then_inc(ld_w[s % 3].sem, 16)
                if s == 1:
                    sp.dma_start(wba[:, :, :], io["w_in"][:, C_BA:C_BA + 2 * H].rearrange("(c p) n -> p c n", p=P)).then_inc(ld_ba.sem, 16)
            sp.wait_ge(*dve_mrg.at(("m", H - 1)))
            sp.dma_start(xs[:, :, :], io["x"].rearrange("(t p) c -> p t c", p=P)).then_inc(ld_x2.sem, 16)
            sp.dma_start(g2, io["ffn_g"].to_broadcast([P, D])).then_inc(ld_g.sem, 16)
            sp.dma_start(rank_row, io["rank_row"].to_broadcast([P, P])).then_inc(ld_g.sem, 16)
            sp.dma_start(rw, io["router_w"].rearrange("(c p) e -> p c e", p=P)).then_inc(ld_g.sem, 16)
            sp.dma_start(gf, io["final_g"].to_broadcast([P, D])).then_inc(ld_g.sem, 16)

            def load_block(e, i):
                for c in range(12):
                    if c >= 6 or not isinstance(i, int) or i > 0:
                        sp.wait_ge(*(small_part(i, c - 6) if c >= 6 else small_part(i - 1, c + 6)))
                    sp.dma_start(raw_chunk(c).rearrange("p (c n) -> p c n", n=HALF if c < 8 else D), chunk_source(e, c)).then_inc(ld_e[c % 6].sem, 16)

            load_block(0, 0)
            load_block(1, 1)
            with sp.Fori(2, NE) as i:
                load_block(i, i)
            sp.wait_ge(*dve_rt.at("be"))
            n_extra = sp.value_load(be[0:1, 15:16], min_val=0, max_val=EXTRA)
            with sp.If(n_extra > 0):
                with sp.Fori(NE, NBLK) as i:
                    e = sp.value_load(be[0:1, bass.ds(i - NE, 1)], min_val=0, max_val=NE - 1)
                    load_block(e, i)
            for t in range(NT):
                sp.wait_ge(*dve_fin.at(("out", t)))
                sp.dma_start(io["out"].rearrange("(t p) c -> p t c", p=P)[:, t, :], xs[:, t, :]).then_inc(st_out.sem, 16)
            sp.wait_ge(st_out.sem, 16 * NT)

        @block.gpsimd
        def _(g):
            def nxt(key=None):
                return pool_pre.next(key)

            g.memset(e_idx[:, :], 0).then_inc(*nxt())
            g.wait_ge(*pool_pre.last())
            g.dma_start(rowtok_dram.rearrange("(p b) o -> p (b o)", p=P), e_idx[:, :]).then_inc(st_rt.sem, 16)
            for r in range(2):
                g.memset(raw[r][:, 0:3], 0.0).then_inc(*nxt("pad"))
            for j, name in enumerate(("b_gate", "b_up", "b_down")):
                for part in range(3):
                    g.dma_start(bias_st[j][32 * part:32 * part + NE, :], io[name]).then_inc(ld_bias.sem, 16)
            g.wait_ge(ld_cst.sem, 48)
            g.tensor_copy(sel[:, :], C("onehot")[0:96, :]).then_inc(*nxt("bias"))

            for ct in range(2 * H):
                g.wait_ge(*act_conv.at(("silu", ct)))
                if ct >= 2:
                    g.wait_ge(*pe_gd.at(("ssq", ct - 2)))
                g.tensor_tensor(sqb[ct % 2], qkvT[:, ct, :], qkvT[:, ct, :], ALU.mult).then_inc(*pool_gd.next(("sq", ct)))

            def earlier_only(t):
                for gr in range(2):
                    hs = slice(4 * gr, 4 * gr + 4)
                    g.wait_ge(*act_gd.at(("dT", t, gr)))
                    g.tensor_tensor(dT[:, hs, :], dT[:, hs, :], over_heads(C("upper"), 4), ALU.mult).then_inc(*pool_gd.next(("dT", t, gr)))

            def gdn_pool(t):
                if t == 0:
                    earlier_only(0)
                for l in range(1, LEVELS):
                    for gr in range(2):
                        hs = slice(4 * gr, 4 * gr + 4)
                        if l == 1:
                            g.wait_ge(*act_gd.at(("aT", t, gr)))
                        if l >= 3:
                            g.wait_ge(*pe_gd.at(("X", t, l - 2, gr)))
                        a = C("masks")[:, (l - 1) * P:l * P]
                        g.tensor_tensor(btm[l % 2][:, hs, :], aT[:, hs, :], over_heads(a, 4), ALU.mult).then_inc(*pool_gd.next(("B", t, l, gr)))
                if t < NT - 1:
                    earlier_only(t + 1)
                if t > 0:
                    for gr in range(2):
                        hs = slice(4 * gr, 4 * gr + 4)
                        cs = slice(gr * HALF, (gr + 1) * HALF)
                        g.wait_ge(*dve_gd.at(("o", t, gr)))
                        g.tensor_tensor(ob[:, t, cs], ob[:, t, cs], qs_s[:, hs, :].rearrange("p h n -> p (h n)"), ALU.add).then_inc(*pool_gd.next(("o", t, gr)))

            for t in range(NT):
                gdn_pool(t)
            g.wait_ge(*pool_gd.last())
            g.memset(e_idx1, 0).then_inc(*pool_gd.next("end"))

            for t in range(NT):
                if t >= 2:
                    g.wait_ge(*dve_att.at(("osq", t - 2)))
                g.tensor_tensor(sqm[t % 2], ob[:, t, :], ob[:, t, :], ALU.mult).then_inc(*pool_att.next(("sq", t)))

            for c in range(4):
                for t in range(NT):
                    k = c * NT + t
                    g.wait_ge(*dve_att.at(("rope", c, t)))
                    if c >= 2 and t == 0:
                        g.wait_ge(*pe_att.at(("qkT", c - 2, 3)))
                    g.tensor_tensor(roped[c % 2][:, t, :], rope1[k % 2], rope2[k % 2], ALU.add).then_inc(*pool_att.next(("rope", c, t)))
            g.wait_ge(*pool_att.last())
            g.memset(e_idx1, 0).then_inc(*pool_att.next("end"))
            for s in range(GATE + 2, OUT + 2):
                w_split(g, s, True)
                t = s - GATE - 9
                if 0 <= t < NT:
                    g.wait_ge(*act_att.at(("gate", 8 * NT - 1)))
                    g.tensor_scalar(ga[:, t, :], ga[:, t, :], 1.0, None, ALU.add).then_inc(*pool_mrg.next())
                    g.wait_ge(*pool_mrg.last())
                    g.tensor_tensor(heads(ga[:, t, :]), heads(ga[:, t, :]), over_heads(G("subln"), H), ALU.mult).then_inc(*pool_mrg.next(("ga", t)))

            def w_part(i, c):
                g.wait_ge(a_hi.sem, 12 * i + c + 1)
                g.tensor_tensor(w_lo[c % 4][:, :], raw_chunk(c), w_hi[c % 4][:, :], ALU.subtract).then_inc(p_lo.sem, 1)

            w_part(0, 0)
            w_part(0, 1)
            g.wait_ge(st_h2.sem, 16 * NT)
            g.wait_ge(*dve_rt.at("idx0"))
            g.indirect_dma_start(out=xg, out_offset=None, in_=h2_dram[:, :],
                                 in_offset=bass.IndirectOffsetOnAxis(ap=e_idx0, axis=0)).then_inc(x_rows.sem, 16)
            w_part(0, 2)
            g.wait_ge(st_rt.sem, 16)
            g.wait_ge(*dve_rt.at("dest"))
            scat = rt_at("scat").bitcast(I32)
            for k in range(NT * TOPK):
                g.indirect_dma_start(out=rowtok_dram[:, :], out_offset=bass.IndirectOffsetOnAxis(ap=scat[:, k:k + 1], axis=0),
                                     in_=tokid[:, k:k + 1], in_offset=None).then_inc(st_rt.sem, 16)
            g.wait_ge(st_rt.sem, 16 * (NT * TOPK + 1))
            g.dma_start(e_idx[:, :], rowtok_dram.rearrange("(p b) o -> p (b o)", p=P)).then_inc(ld_rt.sem, 16)
            g.wait_ge(ld_rt.sem, 16)

            def gather(i):
                g.tensor_copy(e_idx1, e_idx[:, bass.ds(i, 1)]).then_inc(x_idx.sem, 1)
                g.wait_ge(x_idx.sem, 2 * i - 1)
                g.tensor_tensor(e_held, e_idx1, e_idx1, ALU.add).then_inc(x_idx.sem, 1)
                g.indirect_dma_start(out=xg, out_offset=None, in_=h2_dram[:, :],
                                     in_offset=bass.IndirectOffsetOnAxis(ap=e_idx1, axis=0)).then_inc(x_rows.sem, 16)

            def body(i, first=False):
                g.wait_ge(e_tr.sem, 4 * i + 2)
                g.wait_ge(x_rows.sem, 16 * i + 16)
                if not first:
                    g.wait_ge(x_idx.sem, 2 * i)
                gather(i + 1)
                if not first:
                    for c in on_pool(i):
                        w_part(i, c)

            body(0, True)
            with g.Fori(1, NE) as i:
                body(i)
            n_extra = g.value_load(be[0:1, 15:16], min_val=0, max_val=EXTRA)
            with g.If(n_extra > 0):
                with g.Fori(NE, NBLK) as i:
                    body(i)
                g.wait_ge(x_rows.sem, 16 * (NBLK + 1))
                g.wait_ge(st_y.sem, 16 * (NBLK + 1))
            g.wait_ge(x_rows.sem, 16 * (NE + 1))
            g.wait_ge(st_y.sem, 16 * (NE + 1))

            def collect(rows):
                for k in range(NT * TOPK):
                    r = k % 6
                    if k >= 6:
                        g.wait_ge(*dve_fin.at(("row", k - 6)))
                    g.indirect_dma_start(out=ring[:, r, 0:D], out_offset=None, in_=rows,
                                         in_offset=bass.IndirectOffsetOnAxis(ap=y_idx[:, k:k + 1], axis=0)).then_inc(ld_row[r].sem, 16)

            with g.If(n_extra > 0):
                collect(y_dram[:, :])
            with g.Else():
                collect(y_dram[0:NE * P, :])

        @block.scalar
        def _(a):
            for t in range(NT):
                a.wait_ge(ld_x[t].sem, 16)
                a.activation(xn[:, t, :], x0[:, t, :], ACT.Square, accum_out=ss[:, t:t + 1]).then_inc(*act_pre.next(("ss", t)))
                a.wait_ge(*dve_pre.at(("var", t)))
                a.activation(rstd[:, t:t + 1], ss[:, t:t + 1], ACT.Sqrt).then_inc(*act_pre.next(("std", t)))
            a.wait_ge(ld_cst.sem, 48)
            for kc in range(KC):
                a.wait_ge(*pe_hT.at(kc))
                a.activation(hT_hi[:, kc, :], ps[kc][:, :], ACT.Copy, scale=G("mix_g")[:, kc:kc + 1]).then_inc(*act_pre.next(("hT", kc)))
                if kc == 3:
                    w_split(a, 0, False)
            w_split(a, 1, False)
            a.wait_ge(ld_ba.sem, 16)
            a.activation(wba_hi[:, :, :], wba[:, :, :], ACT.Copy).then_inc(*act_pre.next("wba"))

            def silu(ct):
                a.wait_ge(*dve_conv.at(ct))
                a.activation(qkvT[:, ct, :], cacc[ct % 2], ACT.Silu).then_inc(*act_conv.next(("silu", ct)))

            def strength_and_decay():
                a.wait_ge(*dve_gd.at("ba"))
                a.activation(beta, ba[:, :, 0:H], ACT.Sigmoid).then_inc(*act_gd.next("beta"))
                a.activation(ealog, G("a_log"), ACT.Exp).then_inc(*act_gd.next())
                for k in range(2):
                    a.wait_ge(*dve_gd.at(("lam", k)))
                    a.activation(lam2[:, k:k + 1], nlam if k else lam2[:, 0:1], ACT.Exp).then_inc(*act_gd.next(("lam", k)))
                a.wait_ge(*dve_gd.at("nabs"))
                a.activation(spe, spe, ACT.Exp).then_inc(*act_gd.next("spe"))
                a.wait_ge(*dve_gd.at("spe1"))
                a.activation(spe, spe, ACT.Ln).then_inc(*act_gd.next("ln"))

            def norms_and_decays():
                a.wait_ge(*dve_gd.at("nrm"))
                a.activation(nrm, nrm, ACT.Sqrt).then_inc(*act_gd.next("nrm"))
                a.wait_ge(*pe_gd.at("dec"))
                a.activation(dec, ps[5][:, 0:3 * NT * H], ACT.Exp).then_inc(*act_gd.next("dec"))

            for ct in range(3 * H):
                a.wait_ge(*pe_proj.at(("gd", ct)))
                if ct == 0:
                    a.wait_ge(*pool_pre.at("pad"))
                if ct >= 2:
                    a.wait_ge(*dve_conv.at(ct - 2))
                a.activation(raw[ct % 2][:, 3:], ps[ct % 4][:, :], ACT.Copy).then_inc(*act_conv.next(("raw", ct)))
                if ct >= 1:
                    silu(ct - 1)
                if ct % 2 == 1 and (ct + 3) // 2 < DA:
                    w_split(a, (ct + 3) // 2, False)
                if ct == CT_BA:
                    a.wait_ge(*pe_proj.at("baT"))
                    a.activation(baT, ps[4][0:2 * H, :], ACT.Copy).then_inc(*act_gd.next("baT"))
                if ct == CT_BA + 2:
                    strength_and_decay()
                if ct == CT_NORM:
                    norms_and_decays()
            silu(3 * H - 1)

            def flat(ap, gr):
                return ap[:, 4 * gr:4 * gr + 4, :].rearrange("p h n -> p (h n)")

            def decays(t):
                for gr in range(2):
                    a.wait_ge(*pe_gd.at(("D", t, gr)))
                    if t > 0:
                        a.wait_ge(*dve_gd.at(("qkd", t - 1, 3)))
                    a.activation(flat(dT, gr), ps[(6 if t else 0) + gr][:, :], ACT.Exp).then_inc(*act_gd.next(("dT", t, gr)))

            decays(0)
            for t in range(NT):
                for gr in range(2):
                    a.wait_ge(*pe_gd.at(("aT", t, gr)))
                    if t > 0:
                        a.wait_ge(*pool_gd.at(("B", t - 1, LEVELS - 1, gr)))
                    a.activation(flat(aT, gr), ps[4 + gr][:, :], ACT.Copy).then_inc(*act_gd.next(("aT", t, gr)))
                for gr in range(2):
                    a.wait_ge(*pe_gd.at(("triT", t, gr)))
                    a.activation(flat(triT, gr), ps[2 + gr][:, :], ACT.Copy).then_inc(*act_gd.next(("triT", t, gr)))
                for l in range(1, LEVELS):
                    for gr in range(2):
                        a.wait_ge(*pe_gd.at(("X", t, l, gr)))
                        a.wait_ge(*pe_gd.at(("YT", t, l - 1, gr) if l > 1 else ("triT", t, gr)))
                        a.activation(flat(xlev, gr), ps[gr][:, :], ACT.Copy).then_inc(*act_gd.next(("X", t, l, gr)))
                    if l == 2 and t < NT - 1:
                        for gr in range(2):
                            a.wait_ge(*pe_gd.at(("K", t, gr)))
                            if t > 0:
                                a.wait_ge(*pe_gd.at(("dS", t - 1, 1)))
                            a.activation(flat(k_tok, gr), ps[6 + gr][:, :], ACT.Copy).then_inc(*act_gd.next(("K", t, gr)))
                    if l == EARLY and t < NT - 1:
                        decays(t + 1)
                for gr in range(2):
                    a.wait_ge(*pe_gd.at(("P", t, gr)))
                    a.activation(flat(p_out, gr), ps[2 + gr][:, :], ACT.Copy).then_inc(*act_gd.next(("P", t, gr)))

            a.wait_ge(*dve_gd.at(("w", NT - 1, 1)))
            a.wait_ge(*pool_gd.at(("B", NT - 1, LEVELS - 1, 1)))
            w_split(a, DA, False)
            a.wait_ge(*dve_gd.at("end"))
            a.wait_ge(*pool_gd.at("end"))
            w_split(a, DA + 1, False)
            a.wait_ge(*dve_att.at("ovar"))
            a.activation(osq, osq, ACT.Sqrt).then_inc(*act_att.next("ostd"))
            for c in range(6):
                for t in range(NT):
                    if c >= 4:
                        a.wait_ge(*pe_proj.at(("da", c, t)))
                        a.activation(va[:, t, (c - 4) * HALF:(c - 3) * HALF], ps[t][:, :], ACT.Copy).then_inc(*act_att.next(("v", c - 4, t)))
                    if t % 2 == 1:
                        w_split(a, DA + 2 * c + 2 + t // 2, False)
                if 1 <= c < 5:
                    for h4 in range(4):
                        a.wait_ge(*pe_att.at(("qkT", c - 1, h4)))
                        dst = (qaT if c < 3 else kaT)[:, 4 * ((c - 1) % 2) + h4, :]
                        a.activation(dst, ps[4 + h4][:, :], ACT.Copy).then_inc(*act_att.next(("qkT", c - 1, h4)))

            def att_wT(n):
                h, i = divmod(n, NT)
                a.wait_ge(*pe_att.at(("wT", n)))
                a.activation(wT[n % 2][:, 0:(i + 1) * P], ps[4][:, 0:(i + 1) * P], ACT.Copy).then_inc(*act_att.next(("wT", n)))

            def att_out(n):
                h, i = divmod(n, NT)
                a.wait_ge(*pe_att.at(("pv", n)))
                k = n % 2
                rec = recs[:, 2 * k:2 * k + 1]
                if n >= 2:
                    a.wait_ge(*act_att.at(("ssq", n - 2)))
                a.activation(ps[5][:, (1 + k) * P:(2 + k) * P], ps[5][:, 0:P], ACT.Square, scale=rec,
                             accum_out=oasq[:, n:n + 1]).then_inc(*act_att.next(("ssq", n)))
                a.activation(qaT[:, h, i * P:(i + 1) * P], ps[5][:, 0:P], ACT.Copy, scale=rec).then_inc(*act_att.next(("out", n)))

            def gates(k):
                for u in ended(k, KC):
                    (j, q), t = divmod(u // NT, 4), u % NT
                    a.wait_ge(*pe_proj.at(("gate", u)))
                    if j != 1 and u >= 2:
                        a.wait_ge(*dve_att.at(("gate", u - 2)))
                    dst = ga[:, t, q * QUART:(q + 1) * QUART] if j == 1 else gate_s[u % 2][:, :]
                    a.activation(dst, ps[6 + u % 2][:, 0:QUART], ACT.Tanh, scale=0.5).then_inc(*act_att.next(("gate", u)))
                for g in ended(k, NT * KC):
                    w_split(a, GATE + 2 + g, False)

            for n in range(NS + 2):
                gates(3 * n - 1)
                if n < NS:
                    i = n % NT
                    for c in range(2):
                        k = 2 * (n % 2) + c
                        a.wait_ge(*dve_att.at(("max", n)))
                        if n >= 2:
                            a.wait_ge(*dve_att.at(("diff", n - 2)))
                        a.activation(probs[n % 2][c][:, 0:(i + 1) * P], ps[k][:, 0:(i + 1) * P], ACT.Exp, bias=nmx[:, k:k + 1],
                                     scale=DH ** -0.5, accum_out=esum[:, k:k + 1]).then_inc(*act_att.next(("exp", n, c)))
                gates(3 * n)
                if n >= 1 and n - 1 < NS:
                    att_wT(n - 1)
                gates(3 * n + 1)
                if n >= 2:
                    att_out(n - 2)
            act_att.marks["end"] = act_att.count

            a.wait_ge(*dve_mrg.at("ovar"))
            a.activation(oasq, oasq, ACT.Sqrt).then_inc(*act_mrg.next("ostd"))
            for kc in range(KC):
                a.wait_ge(*pe_mrg.at(("mT", kc)))
                a.activation(mT_hi[:, kc, :], ps[4 + kc % 4][:, :], ACT.Copy).then_inc(*act_mrg.next(("mT", kc)))
            for s in (OUT + 2, OUT + 3):
                w_split(a, s, False)

            def h2_out(t):
                for half in range(2):
                    a.wait_ge(*pe_rt.at(("h2T", t, half)))
                    a.activation(h2T[:, 4 * half:4 * half + 4, t * P:(t + 1) * P], ps[4 + 2 * (t % 2) + half].rearrange("p (c n) -> p c n", c=4),
                                 ACT.Copy).then_inc(*act_rt.next(("h2T", t, half)))

            for t in range(NT):
                a.wait_ge(*dve_mrg.at(("x1", 1, t)))
                if t:
                    a.wait_ge(*act_rt.at(("ss", t - 1)))
                a.activation(junk, xs[:, t, :], ACT.Square, accum_out=ss[:, t:t + 1]).then_inc(*act_rt.next(("ss", t)))
                a.wait_ge(*dve_rt.at(("var", t)))
                a.activation(rstd[:, t:t + 1], ss[:, t:t + 1], ACT.Sqrt).then_inc(*act_rt.next(("std", t)))
                a.wait_ge(*dve_rt.at(("h2", t)))
                a.dma_start(h2_dram[t * P:(t + 1) * P, :], h2[:, t, :]).then_inc(st_h2.sem, 16)
                if 0 < t:
                    h2_out(t - 1)
            def w_parts(i, chunks):
                for c in chunks:
                    a.wait_ge(ld_e[c % 6].sem, 32 * i + 16 * (c // 6) + 16)
                    a.wait_ge(e_used.sem, 12 * i + c + 1)
                    a.activation(w_hi[c % 4][:, :], raw_chunk(c), ACT.Copy).then_inc(a_hi.sem, 1)

            w_parts(0, range(0, 1))
            h2_out(NT - 1)
            w_parts(0, range(1, 4))
            a.wait_ge(*dve_rt.at("gsub"))
            a.activation(gw, gw, ACT.Exp).then_inc(*act_rt.next("gexp"))

            def to_hi(dst, k, bank, value):
                a.wait_ge(e_tr.sem, value)
                a.activation(dst[:, k * HALF:(k + 1) * HALF], ps[bank][:, :], ACT.Copy).then_inc(a_tr.sem, 1)

            for half in range(2):
                to_hi(xT_hi, half, 7 - half, half + 1)

            def result(i):
                a.wait_ge(e_used.sem, 12 * i + 16)
                a.wait_ge(st_y.sem, 16 * i + 16)
                a.activation(ys[:, HALF:D], ps[5][:, :], ACT.Copy).then_inc(a_y.sem, 1)
                a.wait_ge(v_y.sem, i + 2)
                a.wait_ge(a_y.sem, i + 2)
                a.dma_start(y_dram[bass.ds(i * P, P), :], ys[:, :]).then_inc(st_y.sem, 16)

            def body(i, before=False, early=0):
                w_parts(i, range(early, 3))
                if before:
                    result(i - 1)
                w_parts(i, range(max(early, 3), 8))
                a.wait_ge(v_act.sem, 8 * i + 9)
                a.activation(sg[0], gm[0], ACT.Sigmoid, scale=ALPHA).then_inc(a_sig.sem, 1)
                w_parts(i, range(8, 10))
                to_hi(avT_hi, 0, 6, 4 * i + 3)
                w_parts(i, range(10, 11))
                a.wait_ge(v_act.sem, 8 * i + 13)
                a.activation(sg[1], gm[1], ACT.Sigmoid, scale=ALPHA).then_inc(a_sig.sem, 1)
                to_hi(xT_hi, 0, 7, 4 * i + 4)
                w_parts(i, range(11, 12))
                to_hi(xT_hi, 1, 6, 4 * i + 5)
                to_hi(avT_hi, 1, 7, 4 * i + 6)

            a.sem_inc(st_y.sem, 16)
            a.sem_inc(a_y.sem, 1)
            body(0, early=4)
            with a.Fori(1, NE) as i:
                body(i, True)
            result(NE - 1)
            n_extra = a.value_load(be[0:1, 15:16], min_val=0, max_val=EXTRA)
            with a.If(n_extra > 0):
                with a.Fori(NE, NBLK) as i:
                    body(i)
                    result(i)

            for t in range(NT):
                a.wait_ge(*dve_fin.at(("sum", t)))
                if t:
                    a.wait_ge(*act_fin.at(("ss", t - 1)))
                a.activation(junk_fin[:, :], xs[:, t, :], ACT.Square,
                             accum_out=ss[:, t:t + 1]).then_inc(*act_fin.next(("ss", t)))
                a.wait_ge(*dve_fin.at(("var", t)))
                a.activation(rstd[:, t:t + 1], ss[:, t:t + 1], ACT.Sqrt).then_inc(*act_fin.next(("std", t)))

        @block.tensor
        def _(pe):
            pe.sem_inc(e_used.sem, 4)
            pe.wait_ge(ld_cst.sem, 48)
            pe.wait_ge(*dve_pre.at(("xn", NT - 1)))
            for kc in range(KC):
                for t in range(NT):
                    mm = pe.transpose(ps[kc][:, t * P:(t + 1) * P], xn[:, t, kc * P:(kc + 1) * P], ident)
                mm.then_inc(*pe_hT.next(kc))

            def in_three(out, k_hi, k_lo, n_hi, n_lo, first, last):
                pe.matmul(out, k_hi, n_hi, start=first, stop=False)
                pe.matmul(out, k_hi, n_lo, start=False, stop=False)
                return pe.matmul(out, k_lo, n_hi, start=False, stop=last)

            def by_channel(ct):
                s, cols = ct // 2, slice(ct % 2 * P, (ct % 2 + 1) * P)
                pe.wait_ge(*w_done(s))
                for kc in range(KC):
                    mm = in_three(ps[ct % 4][:, :], by_rows(w_hi[s % 2][:, :])[:, kc, cols], by_rows(w_lo[s % 2][:, :])[:, kc, cols],
                                  hT_hi[:, kc, :], hT_lo[:, kc, :], kc == 0, kc == KC - 1)
                mm.then_inc(*pe_proj.next(("gd", ct)))
                if ct % 2:
                    pe_proj.marks[("used", s)] = pe_proj.count

            def by_token(out, src_hi, src_lo, t, s, kc, first=True, last=True):
                tok = slice(t * P, (t + 1) * P)
                return in_three(out, src_hi[:, kc, tok], src_lo[:, kc, tok], by_rows(w_hi[s % 2][:, :])[:, kc, :],
                                by_rows(w_lo[s % 2][:, :])[:, kc, :], first and kc == 0, last and kc == KC - 1)

            def ssq(ct):
                pe.wait_ge(*pool_gd.at(("sq", ct)))
                for t in range(NT):
                    c = t * 2 * H + ct
                    mm = pe.matmul(ps[6][:, c:c + 1], sqb[ct % 2][:, t * P:(t + 1) * P], C("ones")[:, 0:1], start=True, stop=True)
                mm.then_inc(*pe_gd.next(("ssq", ct)))

            pe.wait_ge(*dve_pre.at(("hT", KC - 1)))
            for ct in range(3 * H):
                if ct >= 4:
                    pe.wait_ge(*act_conv.at(("raw", ct - 4)))
                by_channel(ct)
                if ct == CT_BA:
                    pe.wait_ge(*dve_pre.at("wba"))
                    for kc in range(KC):
                        mm = in_three(ps[4][0:2 * H, :], wba_hi[:, kc, :], wba_lo[:, kc, :], hT_hi[:, kc, :], hT_lo[:, kc, :],
                                      kc == 0, kc == KC - 1)
                    mm.then_inc(*pe_proj.next("baT"))
                if ct == CT_BA + 1:
                    pe.wait_ge(*act_gd.at("baT"))
                    for t in range(NT):
                        mm = pe.transpose(ps[7][:, t * 2 * H:(t + 1) * 2 * H], baT[:, t * P:(t + 1) * P], ident[0:2 * H, 0:2 * H])
                    mm.then_inc(*pe_proj.next("ba"))
                if ct == CT_BA + 5:
                    pe.wait_ge(*dve_gd.at("g"))
                    gall = gdec.rearrange("p t h -> p (t h)")
                    n = NT * H
                    for j, name in enumerate(("upper", "later", "ones")):
                        mm = pe.matmul(ps[5][:, j * n:(j + 1) * n], C(name), gall, start=True, stop=True)
                    mm.then_inc(*pe_gd.next("dec"))
                if 2 <= ct < 2 * H + 2:
                    ssq(ct - 2)

            def qT(h, t):
                return qkvT[:, h, t * P:(t + 1) * P]

            def kT(h, t):
                return qkvT[:, H + h, t * P:(t + 1) * P]

            def four(bank, gr, name, key, lhsT, rhs=None):
                for j in range(4):
                    h = 4 * gr + j
                    out = ps[bank][:, j * P:(j + 1) * P]
                    if rhs is None:
                        mm = pe.transpose(out, lhsT(h), ident)
                    else:
                        mm = pe.matmul(out, lhsT(h), rhs(h), start=True, stop=True)
                mm.then_inc(*pe_gd.next((name,) + key))

            pe.wait_ge(*act_gd.at("dec"))
            pe.wait_ge(*act_conv.at(("silu", 3 * H - 1)))
            pe.wait_ge(*dve_gd.at("coef"))
            def decays(t):
                pe.wait_ge(*dve_gd.at(("gl", t)))
                for gr in range(2):
                    if t:
                        pe.wait_ge(*act_gd.at(("K", t - 1, gr)))
                    four((6 if t else 0) + gr, gr, "D", (t, gr), lambda h: gl[:, h, :], lambda h: C("upper"))

            decays(0)
            for t in range(NT):
                for pr in range(4):
                    if t > 0:
                        if pr < 2:
                            pe.wait_ge(*act_gd.at(("P", t - 1, pr)))
                        else:
                            pe.wait_ge(*dve_gd.at(("S", t - 1, pr - 2)))
                    for j in range(2):
                        h = 2 * pr + j
                        qk = qkvT[:, h:h + H + 1:H, t * P:(t + 1) * P]
                        mm = pe.matmul(ps[2 + pr][:, j * 2 * P:(j + 1) * 2 * P], kT(h, t), qk, start=True, stop=True)
                    mm.then_inc(*pe_gd.next(("qk", t, pr)))
                for gr in range(2):
                    if t > 0:
                        pe.wait_ge(*dve_gd.at(("o", t - 1, gr)))
                    four(6 + gr, gr, "V", (t, gr), lambda h: qkvT[:, 2 * H + h, t * P:(t + 1) * P])
                for gr in range(2):
                    pe.wait_ge(*dve_gd.at(("qkd", t, 2 * gr + 1)))
                    if t > 1:
                        pe.wait_ge(*dve_gd.at(("qs", t - 1, gr)))
                    pe.wait_ge(*act_gd.at(("dT", t, gr)))
                    four(gr, gr, "Yt", (t, gr), lambda h: qkd[:, h, 1, :])
                for gr in range(2):
                    pe.wait_ge(*dve_gd.at(("a", t, gr)))
                    pe.wait_ge(*dve_gd.at(("qkd", t, 3)))
                    four(4 + gr, gr, "aT", (t, gr), lambda h: a_row[:, h, :])
                for gr in range(2):
                    pe.wait_ge(*dve_gd.at(("tri", t, 0, gr)))
                    four(2 + gr, gr, "triT", (t, gr), lambda h: tri[:, h, :])
                for l in range(1, LEVELS):
                    for gr in range(2):
                        pe.wait_ge(*pool_gd.at(("B", t, l, gr)))
                        pe.wait_ge(*dve_gd.at(("tri", t, l - 1, gr)))
                        if l > 1:
                            pe.wait_ge(*act_gd.at(("X", t, l - 1, gr)))
                        four(gr, gr, "X", (t, l, gr), lambda h: btm[l % 2][:, h, :], lambda h: tri[:, h, :])
                    for gr in range(2):
                        pe.wait_ge(*act_gd.at(("X", t, l, gr)))
                        if l > 1:
                            pe.wait_ge(*dve_gd.at(("triT", t, l - 1, gr)))
                        else:
                            pe.wait_ge(*act_gd.at(("triT", t, gr)))
                        if l < LEVELS - 1:
                            four(2 + gr, gr, "Y", (t, l, gr), lambda h: triT[:, h, :], lambda h: xlev[:, h, :])
                        four(4 + gr, gr, "YT", (t, l, gr), lambda h: xlev[:, h, :], lambda h: triT[:, h, :])
                    if l == 1 and t < NT - 1:
                        for gr in range(2):
                            pe.wait_ge(*dve_gd.at(("v", t, gr)))
                            four(6 + gr, gr, "K", (t, gr), lambda h: kT(h, t))
                    if l == EARLY - 1 and t < NT - 1:
                        decays(t + 1)
                if t < NT - 1:
                    pe.wait_ge(*act_gd.at(("K", t, 1)))
                    pe.wait_ge(*act_gd.at(("dT", t + 1, 1)))
                if t == NT - 1:
                    pe.wait_ge(*dve_gd.at(("v", t, 1)))
                if t > 0:
                    for gr in range(2):
                        pe.wait_ge(*dve_gd.at(("S", t - 1, gr)))
                        four(6 + gr, gr, "KS", (t, gr), lambda h: kT(h, t), lambda h: state[:, h, :])
                        pe.wait_ge(*act_gd.at(("X", t, LEVELS - 1, gr)))
                        four(gr, gr, "QS", (t, gr), lambda h: qT(h, t), lambda h: state[:, h, :])
                for gr in range(2):
                    pe.wait_ge(*dve_gd.at(("w", t, gr) if t else ("v", t, gr)))
                    pe.wait_ge(*dve_gd.at(("triT", t, LEVELS - 1, gr)))
                    four(2 + gr, gr, "P", (t, gr), lambda h: triT[:, h, :], lambda h: (w_rhs if t else v_w)[:, h, :])
                for gr in range(2):
                    pe.wait_ge(*act_gd.at(("P", t, gr)))
                    four(6 + gr, gr, "O", (t, gr), lambda h: qkd[:, h, 0, :], lambda h: p_out[:, h, :])
                if t < NT - 1:
                    for gr in range(2):
                        pe.wait_ge(*dve_gd.at(("pd", t, gr)))
                        four(4 + gr, gr, "dS", (t, gr), lambda h: k_tok[:, h, :], lambda h: p_dec[:, h, :])

            def qkT(c):
                for h4 in range(4):
                    for t in range(NT):
                        pe.wait_ge(*pool_att.at(("rope", c, t)))
                    if c >= 1:
                        pe.wait_ge(*act_att.at(("qkT", c - 1, h4)))
                    for t in range(NT):
                        mm = pe.transpose(ps[4 + h4][:, t * P:(t + 1) * P], roped[c % 2][:, t, h4 * P:(h4 + 1) * P], ident)
                    mm.then_inc(*pe_att.next(("qkT", c, h4)))

            pe.wait_ge(*act_gd.at(("P", NT - 1, 1)))
            pe.wait_ge(*dve_gd.at(("qs", NT - 1, 1)))
            for c in range(6):
                for part in range(2):
                    s = DA + 2 * c + part
                    pe.wait_ge(*w_done(s))
                    for t in range(NT):
                        if part == 0 and 1 <= c < 5:
                            pe.wait_ge(*dve_att.at(("rope", c - 1, t)))
                        elif part == 0 and c:
                            pe.wait_ge(*act_att.at(("v", c - 5, t)))
                        for kc in range(KC):
                            mm = by_token(ps[t][:, part * QUART:(part + 1) * QUART], hT_hi, hT_lo, t, s, kc)
                        mm.then_inc(*pe_proj.next(("da", c, t) if part else None))
                    pe_proj.marks[("used", s)] = pe_proj.count
                if 1 <= c < 5:
                    qkT(c - 1)

            def scores(n):
                h, i = divmod(n, NT)
                for c in range(2):
                    if n >= 2:
                        pe.wait_ge(*act_att.at(("exp", n - 2, c)))
                    else:
                        pe.wait_ge(*act_att.at(("v", 1, 2 * n + c)))
                    r = slice(c * DH, (c + 1) * DH)
                    pe.matmul(ps[2 * (n % 2) + c][:, 0:(i + 1) * P], qaT[r, h, i * P:(i + 1) * P], kaT[r, h, 0:(i + 1) * P],
                              start=True, stop=True).then_inc(*pe_att.next(("sc", n, c)))

            def diff_T(n):
                h, i = divmod(n, NT)
                pe.wait_ge(*dve_att.at(("diff", n)))
                if n:
                    pe.wait_ge(*act_att.at(("wT", n - 1)))
                for kb in range(i + 1):
                    mm = pe.transpose(ps[4][:, kb * P:(kb + 1) * P], wdiff[n % 2][:, kb * P:(kb + 1) * P], ident)
                mm.then_inc(*pe_att.next(("wT", n)))

            def pv(n):
                h, i = divmod(n, NT)
                pe.wait_ge(*act_att.at(("wT", n)))
                if n:
                    pe.wait_ge(*act_att.at(("out", n - 1)))
                for kb in range(i + 1):
                    mm = pe.matmul(ps[5][:, 0:P], wT[n % 2][:, kb * P:(kb + 1) * P], va[:, kb, h * P:(h + 1) * P],
                                   start=kb == 0, stop=kb == i)
                mm.then_inc(*pe_att.next(("pv", n)))

            def gate_rows(k):
                for q in range(GATE_ROWS * k, GATE_ROWS * (k + 1)):
                    u, kc = divmod(q, KC)
                    g, t = divmod(u, NT)
                    if kc == 0:
                        if t == 0:
                            pe.wait_ge(*w_done(GATE + g))
                        if u >= 2:
                            pe.wait_ge(*(dve_att if u - 2 < 4 * NT else act_att).at(("gate", u - 2)))
                    mm = by_token(ps[6 + u % 2][:, 0:QUART], hT_hi, hT_lo, t, GATE + g, kc)
                    if kc == KC - 1:
                        mm.then_inc(*pe_proj.next(("gate", u)))
                        if t == NT - 1:
                            pe_proj.marks[("used", GATE + g)] = pe_proj.count

            pe.wait_ge(*act_att.at(("qkT", 3, 3)))
            pe.wait_ge(*act_att.at(("v", 1, NT - 1)))
            for n in range(NS + 2):
                if n < NS:
                    scores(n)
                    gate_rows(3 * n)
                if 1 <= n <= NS:
                    diff_T(n - 1)
                if n < NS:
                    gate_rows(3 * n + 1)
                if n >= 2:
                    pv(n - 2)
                if n < NS:
                    gate_rows(3 * n + 2)

            pe.wait_ge(*act_att.at("end"))

            def merged_T(kc):
                if kc >= 4:
                    pe.wait_ge(*dve_mrg.at(("mT", kc - 4)))
                pe.wait_ge(*dve_mrg.at(("m", kc)))
                for t in range(NT):
                    mm = pe.transpose(ps[4 + kc % 4][:, t * P:(t + 1) * P], ob[:, t, kc * P:(kc + 1) * P], ident)
                mm.then_inc(*pe_mrg.next(("mT", kc)))

            merged_T(0)
            for s in (OUT, OUT + 1):
                pe.wait_ge(*w_done(s))
            for kc in range(KC):
                if kc < KC - 1:
                    merged_T(kc + 1)
                pe.wait_ge(*dve_mrg.at(("mT", kc)))
                for part in range(2 if kc < KC // 2 else 1):
                    for t in range(NT):
                        mm = by_token(ps[t][:, part * QUART:(part + 1) * QUART], mT_hi, mT_lo, t, OUT + part, kc, part == 0, part == 1)
                        if kc == KC - 1:
                            mm.then_inc(*pe_proj.next())
            pe_proj.marks[("used", OUT)] = pe_proj.count
            for t in range(NT):
                for kc in range(KC // 2, KC):
                    mm = by_token(ps[t][:, QUART:HALF], mT_hi, mT_lo, t, OUT + 1, kc, False, True)
                mm.then_inc(*pe_proj.next(("out", 0, t)))
            pe_proj.marks[("used", OUT + 1)] = pe_proj.count
            def h2_T(t):
                pe.wait_ge(*dve_rt.at(("h2", t)))
                for half in range(2):
                    if t >= 2:
                        pe.wait_ge(*act_rt.at(("h2T", t - 2, half)))
                    for j in range(4):
                        kc = 4 * half + j
                        mm = pe.transpose(ps[4 + 2 * (t % 2) + half][:, j * P:(j + 1) * P], h2[:, t, kc * P:(kc + 1) * P], ident)
                    mm.then_inc(*pe_rt.next(("h2T", t, half)))

            def logits(t):
                for kc in range(KC):
                    if kc % 4 == 0:
                        pe.wait_ge(*act_rt.at(("h2T", t, kc // 4)))
                    mm = pe.matmul(ps[t][:, 0:NE], h2T[:, kc, t * P:(t + 1) * P], rw[:, kc, :], start=kc == 0, stop=kc == KC - 1)
                mm.then_inc(*pe_rt.next(("logits", t)))

            pe.wait_ge(ld_g.sem, 64)
            for t in range(NT):
                pe.wait_ge(*dve_mrg.at(("x1", 0, t)))
                for part in range(2):
                    pe.wait_ge(*w_done(OUT + 2 + part))
                    for kc in range(KC):
                        mm = by_token(ps[t][:, part * QUART:(part + 1) * QUART], mT_hi, mT_lo, t, OUT + 2 + part, kc)
                mm.then_inc(*pe_proj.next(("out", 1, t)))
                if t >= 2:
                    logits(t - 2)
                if t >= 1:
                    h2_T(t - 1)
            logits(NT - 2)
            h2_T(NT - 1)
            logits(NT - 1)
            pe.wait_ge(*dve_rt.at("mask"))
            mask = rt_at("mask").rearrange("p (t e) -> p t e", t=NT)
            pe.matmul(ps[0][:, 0:NT * NE], C("before"), rt_at("mask"), start=True, stop=False)
            for u in range(NT):
                n = NT - 1 - u
                if n:
                    pe.matmul(ps[0][:, (u + 1) * NE:NT * NE], C("ones"), mask[:, u:u + 1, :].to_broadcast([P, n, NE]), start=False, stop=False)
                mm = pe.matmul(ps[0][:, NT * NE:(NT + 1) * NE], C("ones"), mask[:, u, :], start=False, stop=u == NT - 1)
            mm.then_inc(*pe_rt.next("rank"))
            pe.wait_ge(*dve_rt.at("hot0"))
            for t in range(NT):
                mm = pe.matmul(ps[1][:, 0:1], rt_at("big")[:, t * P:(t + 1) * P], rt_at("tokf")[:, TOPK * t:TOPK * t + 1], start=t == 0, stop=t == NT - 1)
            mm.then_inc(*pe_rt.next("idx0"))

            def rows_T(b, half):
                for j in range(4):
                    c = 4 * half + j
                    mm = pe.transpose(ps[b][:, j * P:(j + 1) * P], xg[:, c * P:(c + 1) * P], ident)
                mm.then_inc(e_tr.sem, 1)

            pe.wait_ge(x_rows.sem, 16)
            rows_T(7, 0)
            rows_T(6, 1)
            pe.wait_ge(*pool_pre.at("bias"))
            pe.wait_ge(*dve_pre.at("bias"))

            def bias(b, e, col):
                pe.matmul(ps[b][:, :], sel[:, bass.ds(e, 1)].to_broadcast([96, P]), btab[:, col:col + HALF], start=True, stop=False)

            def in_parts(bank, x_hi, x_lo, kc, c, col, stop):
                k, n = slice(kc * P, (kc + 1) * P), slice(col, col + HALF)
                pe.matmul(ps[bank][:, :], x_hi[:, k], w_hi[c % 4][:, n], start=False, stop=False)
                pe.matmul(ps[bank][:, :], x_lo[:, k], w_hi[c % 4][:, n], start=False, stop=False)
                return pe.matmul(ps[bank][:, :], x_hi[:, k], w_lo[c % 4][:, n], start=False, stop=stop)

            def body(i, e):
                def act_T(hf):
                    pe.wait_ge(v_act.sem, 8 * i + 4 * hf + 12)
                    if hf:
                        pe.wait_ge(v_tr.sem, 4 * i + 4)
                    for j in range(4):
                        mm = pe.transpose(ps[6 + hf][:, j * P:(j + 1) * P], av[hf][:, j * P:(j + 1) * P], ident)
                    mm.then_inc(e_tr.sem, 1)

                pe.wait_ge(v_tr.sem, 4 * i + 2)
                for s in range(4):
                    pe.wait_ge(v_act.sem, 8 * i + 4 * (s // 2) + s % 2 + 1)
                    bias(s, e, s % 2 * D + s // 2 * HALF)
                    for c in (2 * s, 2 * s + 1):
                        pe.wait_ge(*small_part(i, c))
                        for j in range(4):
                            mm = in_parts(s, xT_hi, xT_lo, 4 * (c % 2) + j, c, j * HALF, c % 2 == 1 and j == 3)
                        mm.then_inc(e_used.sem, 1)
                        if c == 6:
                            act_T(0)
                pe.wait_ge(x_rows.sem, 16 * i + 32)
                rows_T(7, 0)
                pe.wait_ge(v_y.sem, i + 1)
                pe.wait_ge(a_y.sem, i + 1)
                for nh in range(2):
                    bias(4 + nh, e, 2 * D + nh * HALF)
                pe.wait_ge(v_tr.sem, 4 * i + 3)
                for c in range(8, 12):
                    pe.wait_ge(*small_part(i, c))
                    if c == 9:
                        rows_T(6, 1)
                    if c == 10:
                        pe.wait_ge(v_tr.sem, 4 * i + 6)
                    for j in range(2):
                        for nh in range(2):
                            mm = in_parts(4 + nh, avT_hi, avT_lo, 2 * (c - 8) + j, c, j * D + nh * HALF, c == 11 and j == 1)
                        if c == 9 and j == 0:
                            act_T(1)
                    mm.then_inc(e_used.sem, 1)

            body(0, 0)
            with pe.Fori(1, NE) as i:
                body(i, i)
            n_extra = pe.value_load(be[0:1, 15:16], min_val=0, max_val=EXTRA)
            with pe.If(n_extra > 0):
                with pe.Fori(NE, NBLK) as i:
                    e = pe.value_load(be[0:1, bass.ds(i - NE, 1)], min_val=0, max_val=NE - 1)
                    body(i, e)

        @block.vector
        def _(v):
            v.sem_inc(v_act.sem, 8)
            v.sem_inc(v_y.sem, 1)

            def then(sig, ins, key=None):
                ins.then_inc(*sig.next(key))
                v.wait_ge(*sig.last())

            for t in range(NT):
                sst, rst = ss[:, t:t + 1], rstd[:, t:t + 1]
                v.wait_ge(*act_pre.at(("ss", t)))
                then(dve_pre, v.tensor_scalar(sst, sst, 1.0 / D, EPS, ALU.mult, ALU.add), ("var", t))
                v.wait_ge(*act_pre.at(("std", t)))
                then(dve_pre, v.reciprocal(rst, rst))
                v.tensor_scalar(xn[:, t, :], x0[:, t, :], rst, None, ALU.mult).then_inc(*dve_pre.next(("xn", t)))
            v.wait_ge(ld_cst.sem, 48)
            for kc in range(KC):
                v.wait_ge(*act_pre.at(("hT", kc)))
                v.scalar_tensor_tensor(out=hT_lo[:, kc, :], in0=ps[kc][:, :], scalar=G("mix_g")[:, kc:kc + 1], in1=hT_hi[:, kc, :],
                                       op0=ALU.mult, op1=ALU.subtract).then_inc(*dve_pre.next(("hT", kc)))
                if kc == 5:
                    w_split(v, 0, True)
            w_split(v, 1, True)
            v.wait_ge(*act_pre.at("wba"))
            v.tensor_tensor(wba_lo[:, :, :], wba[:, :, :], wba_hi[:, :, :], ALU.subtract).then_inc(*dve_pre.next("wba"))

            def bias_step(j, step):
                st, cols = bias_st[j], slice(j * D, (j + 1) * D)
                if step == 0:
                    v.wait_ge(ld_bias.sem, 16 * 9)
                    then(dve_pre, v.tensor_copy(bias_hi, st))
                    then(dve_pre, v.tensor_tensor(st, st, bias_hi, ALU.subtract))
                elif step == 1:
                    then(dve_pre, v.tensor_copy(bias_mid, st))
                    then(dve_pre, v.tensor_tensor(st, st, bias_mid, ALU.subtract))
                elif step == 2:
                    then(dve_pre, v.tensor_copy(bias_lo, st))
                    then(dve_pre, v.tensor_copy(btab[0:32, cols], bias_hi[0:32, :]))
                else:
                    then(dve_pre, v.tensor_copy(btab[32:64, cols], bias_mid[32:64, :]))
                    then(dve_pre, v.tensor_copy(btab[64:96, cols], bias_lo[64:96, :]), "bias")

            def conv(ct):
                v.wait_ge(*act_conv.at(("raw", ct)))
                if ct >= 2:
                    v.wait_ge(*act_conv.at(("silu", ct - 2)))
                wt = G("conv")[:, 4 * ct:4 * ct + 4]
                src, dst = raw[ct % 2], cacc[ct % 2]
                then(dve_conv, v.tensor_scalar(dst, src[:, 3:3 + SEQ], wt[:, 3:4], None, ALU.mult))
                for j in range(3):
                    then(dve_conv, v.scalar_tensor_tensor(out=dst, in0=src[:, j:j + SEQ], scalar=wt[:, j:j + 1], in1=dst,
                                                          op0=ALU.mult, op1=ALU.add), ct if j == 2 else None)

            def per_head(ap):
                return ap.unsqueeze(1).to_broadcast([P, NT, H])

            def strength_and_decay():
                for k in range(2):
                    q, kk = G("lam")[:, 2 * k * DH:(2 * k + 1) * DH], G("lam")[:, (2 * k + 1) * DH:(2 * k + 2) * DH]
                    then(dve_gd, v.tensor_tensor(lamtmp, q, kk, ALU.mult))
                    then(dve_gd, v.tensor_reduce((nlam if k else lam2[:, 0:1]), lamtmp, AX.X, ALU.add), ("lam", k))
                v.wait_ge(*pe_proj.at("ba"))
                then(dve_gd, v.tensor_copy(ba, ps[7][:, 0:NT * 2 * H].rearrange("p (t c) -> p t c", t=NT)), "ba")
                then(dve_gd, v.tensor_tensor(spt, ba[:, :, H:2 * H], per_head(G("dt")), ALU.add))
                then(dve_gd, v.scalar_tensor_tensor(out=spe, in0=spt, scalar=-1.0, in1=spt, op0=ALU.mult, op1=ALU.min), "nabs")
                v.wait_ge(*act_gd.at("spe"))
                then(dve_gd, v.tensor_scalar(spe, spe, 1.0, None, ALU.add), "spe1")
                v.wait_ge(*act_gd.at("ln"))
                then(dve_gd, v.scalar_tensor_tensor(out=spt, in0=spt, scalar=0.0, in1=spe, op0=ALU.max, op1=ALU.add))
                then(dve_gd, v.scalar_tensor_tensor(out=gdec, in0=spt, scalar=-1.0, in1=per_head(ealog), op0=ALU.mult, op1=ALU.mult), "g")
                then(dve_gd, v.scalar_tensor_tensor(out=nlam, in0=lam2[:, 1:2], scalar=LAM_INIT, in1=lam2[:, 0:1],
                                                    op0=ALU.subtract, op1=ALU.subtract))

            def norms():
                v.wait_ge(*pe_gd.at(("ssq", 2 * H - 1)))
                then(dve_gd, v.tensor_scalar(nrm, ps[6][:, 0:NT * 2 * H].rearrange("p (t c) -> p t c", t=NT), EPS, None, ALU.add))
                then(dve_gd, v.reciprocal(k_s, nrm[:, :, H:2 * H]), "nrm")
                v.wait_ge(*act_gd.at("nrm"))
                then(dve_gd, v.reciprocal(nrm, nrm))
                then(dve_gd, v.tensor_tensor(k_s, k_s, beta, ALU.mult))
                then(dve_gd, v.tensor_tensor(v_s, nrm[:, :, H:2 * H], beta, ALU.mult))
                then(dve_gd, v.tensor_scalar(o_s, nrm[:, :, 0:H], P ** -0.5, None, ALU.mult))
                v.wait_ge(*act_gd.at("dec"))
                then(dve_gd, v.scalar_tensor_tensor(out=k_w, in0=k_s, scalar=-1.0, in1=eg, op0=ALU.mult, op1=ALU.mult))
                then(dve_gd, v.tensor_tensor(o_q, o_s, eg, ALU.mult), "coef")

            for ct in range(3 * H):
                conv(ct)
                if ct % 2 == 1 and (ct + 3) // 2 < DA:
                    w_split(v, (ct + 3) // 2, True)
                if ct == CT_BA + 2:
                    strength_and_decay()
                if ct == CT_NORM:
                    norms()
                if 7 <= ct < 19:
                    bias_step(*divmod(ct - 7, 4))
            then(dve_gd, v.tensor_scalar(G("subln"), G("subln"), (1.0 - LAM_INIT) / 2, None, ALU.mult))
            then(dve_gd, v.tensor_scalar(G("gd_g"), G("gd_g"), 1 / 4, None, ALU.mult))

            def bank4(b):
                return ps[b][:, :].rearrange("p (h n) -> p h n", h=4)

            def log_decays(t):
                if t > 0:
                    v.wait_ge(*pe_gd.at(("D", t - 1, 1)))
                then(dve_gd, v.tensor_tensor(gl, over_heads(C("later"), H), over_cols(gdec[:, t, :], P), ALU.mult), ("gl", t))

            log_decays(0)
            for t in range(NT):
                for pr in range(4):
                    v.wait_ge(*pe_gd.at(("qk", t, pr)))
                    v.wait_ge(*pool_gd.at(("dT", t, pr // 2)))
                    if t > 0:
                        v.wait_ge(*pe_gd.at(("O", t - 1, 1)))
                    hs = slice(2 * pr, 2 * pr + 2)
                    then(dve_gd, v.tensor_tensor(qkd[:, hs, :, :], ps[2 + pr][:, :].rearrange("p (h c n) -> p h c n", h=2, c=2),
                                                 dT[:, hs, :].unsqueeze(2).to_broadcast([P, 2, 2, P]), ALU.mult), ("qkd", t, pr))
                for gr in range(2):
                    hs = slice(4 * gr, 4 * gr + 4)
                    v.wait_ge(*pe_gd.at(("Yt", t, gr)))
                    if t > 0:
                        v.wait_ge(*pool_gd.at(("o", t - 1, gr)) if t > 1 else dve_gd.last())
                    then(dve_gd, v.tensor_tensor(a_row[:, hs, :], bank4(gr), over_cols(k_s[:, t, hs], P), ALU.mult), ("a", t, gr))
                for gr in range(2):
                    hs = slice(4 * gr, 4 * gr + 4)
                    then(dve_gd, v.tensor_tensor(tri[:, hs, :], a_row[:, hs, :], over_heads(C("neg_m0"), 4), ALU.mult))
                    then(dve_gd, v.tensor_tensor(tri[:, hs, :], tri[:, hs, :], over_heads(ident, 4), ALU.add), ("tri", t, 0, gr))
                for gr in range(2):
                    hs = slice(4 * gr, 4 * gr + 4)
                    v.wait_ge(*pe_gd.at(("V", t, gr)))
                    then(dve_gd, v.tensor_tensor(v_w[:, hs, :], bank4(6 + gr), over_cols(v_s[:, t, hs], P), ALU.mult), ("v", t, gr))
                for l in range(1, LEVELS):
                    for gr in range(2):
                        hs = slice(4 * gr, 4 * gr + 4)
                        if l < LEVELS - 1:
                            v.wait_ge(*pe_gd.at(("Y", t, l, gr)))
                            then(dve_gd, v.tensor_tensor(tri[:, hs, :], tri[:, hs, :], bank4(2 + gr), ALU.subtract), ("tri", t, l, gr))
                        v.wait_ge(*pe_gd.at(("YT", t, l, gr)))
                        then(dve_gd, v.tensor_tensor(triT[:, hs, :], triT[:, hs, :], bank4(4 + gr), ALU.subtract), ("triT", t, l, gr))
                    if l == 1 and t < NT - 1:
                        log_decays(t + 1)
                if t > 0:
                    for gr in range(2):
                        hs = slice(4 * gr, 4 * gr + 4)
                        v.wait_ge(*pe_gd.at(("KS", t, gr)))
                        for h in range(4 * gr, 4 * gr + 4):
                            ins = v.scalar_tensor_tensor(out=w_rhs[:, h, :], in0=ps[6 + gr][:, (h % 4) * P:(h % 4 + 1) * P],
                                                         scalar=k_w[:, t, h:h + 1], in1=v_w[:, h, :], op0=ALU.mult, op1=ALU.add)
                        then(dve_gd, ins, ("w", t, gr))
                        v.wait_ge(*pe_gd.at(("QS", t, gr)))
                        if t > 1:
                            v.wait_ge(*pool_gd.at(("o", t - 1, gr)))
                        then(dve_gd, v.tensor_tensor(qs_s[:, hs, :], bank4(gr), over_cols(o_q[:, t, hs], P), ALU.mult), ("qs", t, gr))
                for gr in range(2 if t < NT - 1 else 0):
                    hs = slice(4 * gr, 4 * gr + 4)
                    v.wait_ge(*act_gd.at(("P", t, gr)))
                    if t > 0:
                        v.wait_ge(*pe_gd.at(("dS", t - 1, 1)))
                    then(dve_gd, v.tensor_tensor(p_dec[:, hs, :], p_out[:, hs, :], over_cols(ed[:, t, hs], P), ALU.mult), ("pd", t, gr))
                if t == NT - 1:
                    w_split(v, DA, True)
                for gr in range(2):
                    hs = slice(4 * gr, 4 * gr + 4)
                    v.wait_ge(*pe_gd.at(("O", t, gr)))
                    out = ob[:, t, gr * HALF:(gr + 1) * HALF].rearrange("p (h n) -> p h n", h=4)
                    then(dve_gd, v.tensor_tensor(out, bank4(6 + gr), over_cols(o_s[:, t, hs], P), ALU.mult), ("o", t, gr))
                if t < NT - 1:
                    for gr in range(2):
                        hs = slice(4 * gr, 4 * gr + 4)
                        v.wait_ge(*pe_gd.at(("dS", t, gr)))
                        if t == 0:
                            then(dve_gd, v.tensor_copy(state[:, hs, :], bank4(4 + gr)), ("S", t, gr))
                        else:
                            for h in range(4 * gr, 4 * gr + 4):
                                ins = v.scalar_tensor_tensor(out=state[:, h, :], in0=state[:, h, :], scalar=glast[:, t, h:h + 1],
                                                             in1=ps[4 + gr][:, (h % 4) * P:(h % 4 + 1) * P], op0=ALU.mult, op1=ALU.add)
                            then(dve_gd, ins, ("S", t, gr))
            dve_gd.marks["end"] = dve_gd.count

            v.wait_ge(*pool_gd.at("end"))
            cos = C("cos").rearrange("p (t j) -> p t j", t=NT)
            sin = C("sin").rearrange("p (t b j) -> p t b j", t=NT, b=2)
            w_split(v, DA + 1, True)
            for t in range(NT):
                v.wait_ge(*pool_att.at(("sq", t)))
                then(dve_att, v.tensor_reduce(osq[:, t * H:(t + 1) * H], heads(sqm[t % 2]), AX.X, ALU.add), ("osq", t))
            then(dve_att, v.tensor_scalar(osq, osq, 1.0 / P, EPS, ALU.mult, ALU.add), "ovar")
            v.wait_ge(*act_att.at("ostd"))
            then(dve_att, v.reciprocal(osq, osq))
            for c in range(6):
                for t in range(NT):
                    if c == 1:
                        o = heads(ob[:, t, :])
                        then(dve_att, v.tensor_tensor(o, o, over_cols(osq[:, t * H:(t + 1) * H], P), ALU.mult))
                        then(dve_att, v.tensor_tensor(o, o, over_heads(G("gd_g"), H), ALU.mult))
                    if t % 2 == 1:
                        w_split(v, DA + 2 * c + 2 + t // 2, True)
                    if c >= 4:
                        continue
                    k = c * NT + t
                    v.wait_ge(*pe_proj.at(("da", c, t)))
                    if k >= 2:
                        v.wait_ge(*pool_att.at(("rope", (k - 2) // NT, (k - 2) % NT)))
                    x4 = ps[t][:, :].rearrange("p (g b j) -> p g b j", b=2, j=32)
                    r1, r2 = (r[k % 2].rearrange("p (g b j) -> p g b j", b=2, j=32) for r in (rope1, rope2))
                    v.tensor_tensor(r1, x4, cos[:, t, :].unsqueeze(1).unsqueeze(1).to_broadcast([P, 8, 2, 32]), ALU.mult).then_inc(*dve_att.next())
                    for b in range(2):
                        ins = v.tensor_tensor(r2[:, :, b, :], x4[:, :, 1 - b, :], sin[:, t, b, :].unsqueeze(1).to_broadcast([P, 8, 32]), ALU.mult)
                        ins.then_inc(*dve_att.next(("rope", c, t) if b else None))

            def diff(n):
                i, k = n % NT, 2 * (n % 2)
                for c in range(2):
                    v.wait_ge(*act_att.at(("exp", n, c)))
                if n >= 2:
                    v.wait_ge(*act_att.at(("out", n - 2)))
                    v.wait_ge(*pe_att.at(("wT", n - 2)))
                then(dve_att, v.reciprocal(recs[:, k:k + 2], esum[:, k:k + 2]))
                rr = ratio[:, n % 2:n % 2 + 1]
                then(dve_att, v.scalar_tensor_tensor(out=rr, in0=esum[:, k:k + 1], scalar=recs[:, k + 1:k + 2], in1=nlam,
                                                     op0=ALU.mult, op1=ALU.mult))
                cols = slice(0, (i + 1) * P)
                then(dve_att, v.scalar_tensor_tensor(out=wdiff[n % 2][:, cols], in0=probs[n % 2][1][:, cols], scalar=rr,
                                                     in1=probs[n % 2][0][:, cols], op0=ALU.mult, op1=ALU.add), ("diff", n))

            NS = H * NT
            v.wait_ge(*pe_att.at(("qkT", 3, 3)))
            v.wait_ge(*pool_att.at("end"))

            def gates(k):
                for u in ended(k, KC):
                    (j, q), t = divmod(u // NT, 4), u % NT
                    if j == 1:
                        continue
                    e, cols = gate_s[u % 2][:, :], slice(q * QUART, (q + 1) * QUART)
                    v.wait_ge(*act_att.at(("gate", u)))
                    o = ob[:, t, cols]
                    if j == 0:
                        then(dve_att, v.scalar_tensor_tensor(out=e, in0=e, scalar=1.0, in1=ps[6 + u % 2][:, 0:QUART], op0=ALU.add, op1=ALU.mult))
                        then(dve_att, v.tensor_tensor(o, o, e, ALU.mult), ("gate", u))
                    else:
                        then(dve_att, v.scalar_tensor_tensor(out=o, in0=e, scalar=1.0, in1=o, op0=ALU.add, op1=ALU.mult), ("gate", u))

            for n in range(NS + 1):
                gates(3 * n - 1)
                if n >= 1:
                    diff(n - 1)
                if n < NS:
                    i = n % NT
                    k = 2 * (n % 2)
                    for c in range(2):
                        v.wait_ge(*pe_att.at(("sc", n, c)))
                    diag = banks[:, k:k + 2, i * P:(i + 1) * P]
                    then(dve_att, v.tensor_tensor(diag, diag, over_heads(causal, 2), ALU.add))
                    then(dve_att, v.tensor_reduce(mx[:, k:k + 2], banks[:, k:k + 2, 0:(i + 1) * P], AX.X, ALU.max))
                    then(dve_att, v.tensor_scalar(nmx[:, k:k + 2], mx[:, k:k + 2], -DH ** -0.5, None, ALU.mult), ("max", n))
                gates(3 * n)
                gates(3 * n + 1)

            v.wait_ge(*act_att.at(("out", NS - 1)))
            then(dve_mrg, v.tensor_scalar(oasq, oasq, 1.0 / P, EPS, ALU.mult, ALU.add), "ovar")
            v.wait_ge(*act_mrg.at("ostd"))
            then(dve_mrg, v.reciprocal(oasq, oasq))
            v.wait_ge(*pool_mrg.at(("ga", NT - 1)))

            def merged_lo(kc):
                v.wait_ge(*act_mrg.at(("mT", kc)))
                v.tensor_tensor(mT_lo[:, kc, :], ps[4 + kc % 4][:, :], mT_hi[:, kc, :], ALU.subtract).then_inc(*dve_mrg.next(("mT", kc)))

            for h in range(H):
                for i in range(NT):
                    o = qaT[:, h, i * P:(i + 1) * P]
                    ins = v.scalar_tensor_tensor(out=o, in0=o, scalar=oasq[:, h * NT + i:h * NT + i + 1], in1=ga[:, i, h * P:(h + 1) * P],
                                                 op0=ALU.mult, op1=ALU.mult)
                then(dve_mrg, ins)
                m = ob[:, :, h * P:(h + 1) * P]
                then(dve_mrg, v.tensor_tensor(m, m, qaT[:, h, :].rearrange("p (t n) -> p t n", t=NT), ALU.add), ("m", h))
                if h:
                    merged_lo(h - 1)
            merged_lo(H - 1)
            w_split(v, OUT + 2, True)
            v.wait_ge(ld_x2.sem, 16)
            v.wait_ge(ld_g.sem, 64)
            lg = rt_at("lg").rearrange("p (t e) -> p t e", t=NT)
            top = rt_at("top").rearrange("p (t k) -> p t k", t=NT)
            tix = rt_at("tix").bitcast(U32).rearrange("p (t k) -> p t k", t=NT)

            def best(t):
                v.wait_ge(*pe_rt.at(("logits", t)))
                then(dve_rt, v.tensor_tensor(lg[:, t, :], ps[t][:, 0:NE], G("router_b"), ALU.add))
                then(dve_rt, v.max(top[:, t, :], lg[:, t, :]))
                then(dve_rt, v.max_index(tix[:, t, :], top[:, t, :], lg[:, t, :]))

            v.wait_ge(*w_done(OUT + 2))
            then(dve_rt, v.tensor_copy(rt_at("tokf"), tokid[:, :]))
            for c in range(2):
                for t in range(NT):
                    v.wait_ge(*pe_proj.at(("out", c, t)))
                    xc = xs[:, t, c * HALF:(c + 1) * HALF]
                    v.tensor_tensor(xc, xc, ps[t][:, :], ALU.add).then_inc(*dve_mrg.next(("x1", c, t)))
                    if c == 0:
                        if t == NT - 1:
                            w_split(v, OUT + 3, True)
                        continue
                    v.wait_ge(*act_rt.at(("ss", t)))
                    sst, rst = ss[:, t:t + 1], rstd[:, t:t + 1]
                    then(dve_rt, v.tensor_scalar(sst, sst, 1.0 / D, EPS, ALU.mult, ALU.add), ("var", t))
                    v.wait_ge(*act_rt.at(("std", t)))
                    then(dve_rt, v.reciprocal(rst, rst))
                    v.scalar_tensor_tensor(out=h2[:, t, :], in0=xs[:, t, :], scalar=rst, in1=g2,
                                           op0=ALU.mult, op1=ALU.mult).then_inc(*dve_rt.next(("h2", t)))
                    if t >= 2:
                        best(t - 2)
            best(NT - 2)
            best(NT - 1)
            gw3 = gw.rearrange("p (t k) -> p t k", t=NT)
            then(dve_rt, v.tensor_tensor(gw3, top[:, :, 0:TOPK], top[:, :, 0:1].to_broadcast([P, NT, TOPK]), ALU.subtract), "gsub")
            tixf, hot = rt_at("tixf"), rt_at("hot").rearrange("p (a e) -> p a e", e=NE)
            then(dve_rt, v.tensor_copy(tixf.rearrange("p (t k) -> p t k", t=NT), tix[:, :, 0:TOPK]))
            then(dve_rt, v.tensor_tensor(hot, C("iota").unsqueeze(1).to_broadcast([P, NT * TOPK, NE]), over_cols(tixf, NE), ALU.is_equal))
            mask = rt_at("mask").rearrange("p (t e) -> p t e", t=NT)
            then(dve_rt, v.tensor_reduce(mask, rt_at("hot").rearrange("p (t k e) -> p t e k", t=NT, k=TOPK), AX.X, ALU.add), "mask")
            rank = rt_at("rank").rearrange("p (t e) -> p t e", t=NT)
            v.wait_ge(*pe_rt.at("rank"))
            then(dve_rt, v.tensor_copy(rank, ps[0][:, 0:NT * NE].rearrange("p (t e) -> p t e", t=NT)))
            for t in range(NT):
                then(dve_rt, v.tensor_scalar(rt_at("big")[:, t * P:(t + 1) * P], rank_row, rank[:, t, 0:1], mask[:, t, 0:1],
                                             ALU.is_equal, ALU.mult), "hot0")
            cnt = rt_at("cnt")
            then(dve_rt, v.tensor_copy(cnt, ps[0][:, NT * NE:(NT + 1) * NE]))
            v.wait_ge(*pe_rt.at("idx0"))
            then(dve_rt, v.tensor_copy(e_idx0, ps[1][:, 0:1]), "idx0")
            gsum = rt_at("gsum")
            v.wait_ge(*act_rt.at("gexp"))
            then(dve_rt, v.tensor_reduce(gsum, gw3, AX.X, ALU.add))
            then(dve_rt, v.reciprocal(gsum, gsum))
            then(dve_rt, v.tensor_tensor(gw3, gw3, over_cols(gsum, TOPK), ALU.mult))
            xb, inc, shift = rt_at("xb"), rt_at("inc"), rt_at("shift")
            then(dve_rt, v.tensor_scalar(xb, cnt, float(P), None, ALU.is_gt))
            for m in range(2, NT):
                then(dve_rt, v.scalar_tensor_tensor(out=xb, in0=cnt, scalar=float(m * P), in1=xb, op0=ALU.is_gt, op1=ALU.add))
            then(dve_rt, v.tensor_tensor_scan(inc, C("ones")[:, 0:NE], xb, 0.0, ALU.mult, ALU.add))
            then(dve_rt, v.tensor_tensor(shift, inc, xb, ALU.subtract))
            then(dve_rt, v.scalar_tensor_tensor(out=shift, in0=shift, scalar=float(P), in1=C("base"), op0=ALU.mult, op1=ALU.subtract))
            then(dve_rt, v.tensor_scalar(shift, shift, float(P * (NE - 1)), None, ALU.add))
            big = rt_at("big").rearrange("p (b e) -> p b e", e=NE)
            then(dve_rt, v.tensor_tensor(big, over_cols(C("iota")[:, 0:16], NE), inc.unsqueeze(1).to_broadcast([P, 16, NE]), ALU.is_ge))
            bef = rt_at("bef")
            then(dve_rt, v.tensor_reduce(bef, big, AX.X, ALU.add))
            then(dve_rt, v.tensor_scalar(bef, bef, float(NE - 1), None, ALU.min))
            then(dve_rt, v.tensor_copy(bef[:, 15:16], inc[:, NE - 1:NE]))
            then(dve_rt, v.tensor_copy(be, bef), "be")
            dest = rt_at("dest").rearrange("p (t e) -> p t e", t=NT)
            then(dve_rt, v.scalar_tensor_tensor(out=dest, in0=rank, scalar=float(P), in1=shift.unsqueeze(1).to_broadcast([P, NT, NE]),
                                                op0=ALU.is_ge, op1=ALU.mult))
            then(dve_rt, v.tensor_tensor(dest, dest, rank, ALU.add))
            then(dve_rt, v.tensor_tensor(dest, dest, C("base").unsqueeze(1).to_broadcast([P, NT, NE]), ALU.add))
            hot4, dk = rt_at("hot").rearrange("p (t k e) -> p t k e", t=NT, k=TOPK), rt_at("dk")
            then(dve_rt, v.tensor_tensor(hot4, hot4, dest.unsqueeze(2).to_broadcast([P, NT, TOPK, NE]), ALU.mult))
            then(dve_rt, v.tensor_reduce(dk, hot, AX.X, ALU.add))
            then(dve_rt, v.tensor_copy(y_idx, dk))
            blk, blkf = rt_at("blk").bitcast(I32), rt_at("blkf")
            then(dve_rt, v.tensor_scalar(blk, y_idx, 7, None, ALU.logical_shift_right))
            then(dve_rt, v.tensor_copy(blkf, blk))
            then(dve_rt, v.tensor_scalar(blkf, blkf, float(-(P * RT_W - 1)), None, ALU.mult))
            then(dve_rt, v.scalar_tensor_tensor(out=blkf, in0=dk, scalar=float(RT_W), in1=blkf, op0=ALU.mult, op1=ALU.add))
            then(dve_rt, v.tensor_copy(rt_at("scat").bitcast(I32), blkf), "dest")
            dve_rt.marks["end"] = dve_rt.count

            def to_lo(dst, hi, k, bank, value):
                v.wait_ge(a_tr.sem, value)
                cols = slice(k * HALF, (k + 1) * HALF)
                v.tensor_tensor(dst[:, cols], ps[bank][:, :], hi[:, cols], ALU.subtract).then_inc(v_tr.sem, 1)

            for half in range(2):
                to_lo(xT_lo, xT_hi, half, 7 - half, half + 1)

            def w_parts(i, chunks):
                for c in chunks:
                    if c in on_pool(i):
                        continue
                    v.wait_ge(a_hi.sem, 12 * i + c + 1)
                    v.tensor_tensor(w_lo[c % 4][:, :], raw_chunk(c), w_hi[c % 4][:, :], ALU.subtract).then_inc(v_lo.sem, 1)

            def swiglu(i, hf):
                n = 8 * i + 4 * hf + 8
                v.wait_ge(e_used.sem, 12 * i + 4 * hf + 6)
                v.wait_ge(v_act.sem, n)
                v.tensor_scalar(gm[hf], ps[2 * hf][:, :], LIMIT, None, ALU.min).then_inc(v_act.sem, 1)
                v.wait_ge(e_used.sem, 12 * i + 4 * hf + 8)
                v.tensor_scalar(um[hf], ps[2 * hf + 1][:, :], LIMIT, -LIMIT, ALU.min, ALU.max).then_inc(v_act.sem, 1)
                v.wait_ge(v_act.sem, n + 2)
                v.scalar_tensor_tensor(out=um[hf], in0=um[hf], scalar=1.0, in1=gm[hf], op0=ALU.add, op1=ALU.mult).then_inc(v_act.sem, 1)
                v.wait_ge(v_act.sem, n + 3)
                v.wait_ge(a_sig.sem, 2 * i + hf + 1)
                v.wait_ge(e_tr.sem, 4 * i + 2)
                v.tensor_tensor(av[hf], um[hf], sg[hf], ALU.mult).then_inc(v_act.sem, 1)

            def result(i):
                v.wait_ge(e_used.sem, 12 * i + 16)
                v.wait_ge(st_y.sem, 16 * i + 16)
                v.tensor_copy(ys[:, 0:HALF], ps[4][:, :]).then_inc(v_y.sem, 1)

            def body(i, before=False):
                w_parts(i, range(0, 3))
                if before:
                    result(i - 1)
                w_parts(i, range(3, 8))
                swiglu(i, 0)
                w_parts(i, range(8, 10))
                to_lo(avT_lo, avT_hi, 0, 6, 4 * i + 3)
                w_parts(i, range(10, 11))
                swiglu(i, 1)
                to_lo(xT_lo, xT_hi, 0, 7, 4 * i + 4)
                to_lo(xT_lo, xT_hi, 1, 6, 4 * i + 5)
                w_parts(i, range(11, 12))
                to_lo(avT_lo, avT_hi, 1, 7, 4 * i + 6)

            body(0)
            with v.Fori(1, NE) as i:
                body(i, True)
            result(NE - 1)
            n_extra = v.value_load(be[0:1, 15:16], min_val=0, max_val=EXTRA)
            with v.If(n_extra > 0):
                with v.Fori(NE, NBLK) as i:
                    body(i)
                    result(i)

            def finish(t):
                v.wait_ge(*act_fin.at(("ss", t)))
                then(dve_fin, v.tensor_scalar(ss[:, t:t + 1], ss[:, t:t + 1], 1.0 / D, EPS, ALU.mult, ALU.add), ("var", t))
                v.wait_ge(*act_fin.at(("std", t)))
                then(dve_fin, v.reciprocal(rstd[:, t:t + 1], rstd[:, t:t + 1]))
                v.scalar_tensor_tensor(out=xs[:, t, :], in0=xs[:, t, :], scalar=rstd[:, t:t + 1], in1=gf,
                                       op0=ALU.mult, op1=ALU.mult).then_inc(*dve_fin.next(("out", t)))

            for t in range(NT):
                for k in range(TOPK):
                    n = t * TOPK + k
                    v.wait_ge(ld_row[n % 6].sem, 16 * (n // 6 + 1))
                    then(dve_fin, v.scalar_tensor_tensor(out=xs[:, t, :], in0=ring[:, n % 6, 0:D], scalar=gw[:, n:n + 1], in1=xs[:, t, :],
                                                         op0=ALU.mult, op1=ALU.add), ("row", n))
                dve_fin.marks[("sum", t)] = dve_fin.count
                if t:
                    finish(t - 1)
            finish(NT - 1)

    return {name: s.marks for name, s in signals.items()}


def constants():
    i = np.arange(P)
    c = np.zeros((P, NCST), np.float32)

    def put(name, a):
        lo, hi = CST[name]
        c[:, lo:hi] = np.asarray(a, np.float32).reshape(P, hi - lo)

    put("ident", np.eye(P))
    put("upper", i[:, None] <= i[None, :])
    put("later", i[:, None] > i[None, :])
    put("before", i[:, None] < i[None, :])
    put("ones", np.ones((P, P)))

    def between(l, row, col):
        return (row >> (l + 1) == col >> (l + 1)) & ((row >> l) & 1 == 1) & ((col >> l) & 1 == 0)

    put("neg_m0", np.where(between(0, i[:, None], i[None, :]), -1.0, 0.0))
    put("masks", np.concatenate([between(l, i[None, :], i[:, None]) for l in range(1, LEVELS)], axis=1))
    put("causal", np.where(i[None, :] <= i[:, None], 0.0, NEG))
    inv = (1.0 / (np.float32(10000.0) ** (np.arange(0, DH, 2, dtype=np.float32) / np.float32(DH)))).astype(np.float32)
    ang = np.arange(SEQ, dtype=np.float32)[:, None] * inv[None, :]
    cos, sin = np.cos(ang), np.sin(ang)
    put("cos", cos.reshape(NT, P, 32).transpose(1, 0, 2))
    put("sin", np.stack([-sin, sin], axis=1).reshape(NT, P, 2, 32).transpose(1, 0, 2, 3))
    put("iota", np.broadcast_to(np.arange(NE), (P, NE)))
    put("base", np.broadcast_to(P * np.arange(NE), (P, NE)))
    put("onehot", i[:, None] % NE == np.arange(NE)[None, :])
    tok = np.repeat(np.arange(NT)[None, :] * P + i[:, None], TOPK, axis=1).astype(np.int32)
    return c, tok


_IO = dict(w_in="w_in", w_out="w_out", router_w="router_w", b_gate="exp_b_gate", b_up="exp_b_up", b_down="exp_b_down",
           w_gate="exp_w_gate", w_up="exp_w_up", w_down="exp_w_down")


def kernel(**inputs):
    import concourse.bacc as bacc
    from concourse.bass_utils import run_bass_kernel_spmd

    x = {k: np.asarray(v) for k, v in inputs.items()}

    def rows(a):
        return np.broadcast_to(a.reshape(1, -1), (P, a.size))

    cst, tok = constants()
    conv = x["gd_conv_w"][0].reshape(4, 24, P).transpose(2, 1, 0).reshape(P, 96)
    par = np.concatenate([x["mix_norm_g"].reshape(KC, P).T, conv, rows(x["gd_a_log"]), rows(x["gd_dt_bias"]), rows(x["router_b"]),
                          rows(x["da_lambda_q1"]), rows(x["da_lambda_k1"]), rows(x["da_lambda_q2"]), rows(x["da_lambda_k2"]),
                          rows(x["da_subln_g"]), rows(x["gd_norm_g"])], axis=1)
    arrays = {"x": x["x"].reshape(SEQ, D), "cst": cst, "par": np.ascontiguousarray(par), "tokid": tok,
              "rank_row": np.arange(P, dtype=np.float32).reshape(1, P), "ffn_g": x["ffn_norm_g"].reshape(1, D), "final_g": x["final_norm_g"].reshape(1, D)}
    for name, source in _IO.items():
        arrays[name] = x[source][0]

    def build(known):
        nc = bacc.Bacc("TRN2", target_bir_lowering=False, num_devices=1)
        io = {name: nc.dram_tensor(f"in_{name}", a.shape, mybir.dt.from_np(a.dtype), kind="ExternalInput").ap()
              for name, a in arrays.items()}
        io["out"] = nc.dram_tensor("out_rows", (SEQ, D), F32, kind="ExternalOutput").ap()
        return nc, layer_kernel(nc, io, known)

    _, counts = build({})
    nc, _ = build(counts)
    got = run_bass_kernel_spmd(nc, [{f"in_{n}": a for n, a in arrays.items()}], core_ids=[0])
    return got.results[0]["out_rows"].reshape(x["x"].shape)
```
